# Optimizing a Trainium2 kernel written in Bass

```python
import math
import jax, jax.numpy as jnp
from jax import lax
import numpy as np

D_MODEL = 1024
BATCH = 1
SEQ = 1024
DEPTH = 1
DEC_BATCH = 1
DEC_SEQ = 64
PAST_LEN = 2048

CHUNK = 64
Q_BLOCK = 128
EPS = 1e-6
NEG_INF = -1e30
SSM_WIDTH = D_MODEL // 2
SSM_GROUP = 16
SSM_GROUPS = SSM_WIDTH // SSM_GROUP
SSM_STATE = 64
DT_MIN = 0.001
DT_MAX = 0.1
N_HEADS = 8
HEAD_DIM = 64
ATTN_WIDTH = N_HEADS * HEAD_DIM
IDX_HEADS = 8
IDX_DIM = 32
IDX_WEIGHT_SCALE = (IDX_HEADS * IDX_DIM) ** -0.5
TOPK_MAX = 256
N_GROUPS = 4
EXPERTS_PER_GROUP = 4
N_EXPERTS = N_GROUPS * EXPERTS_PER_GROUP
EXPERT_DIM = 256
TOP_K_IN_GROUP = 2
IN_SPLITS = (SSM_WIDTH, ATTN_WIDTH, HEAD_DIM, HEAD_DIM, IDX_HEADS * IDX_DIM, IDX_DIM, IDX_HEADS, D_MODEL, D_MODEL)
IN_WIDTH = sum(IN_SPLITS)
IN_OFFSETS = tuple(int(o) for o in np.cumsum(IN_SPLITS)[:-1])

kernel_name = 'chunk_causal_s5_dsa_hmoe_step'

def rms_norm(x, gain=None):
    x32 = x.astype(jnp.float32)
    y = x32 * lax.rsqrt(jnp.mean(x32 * x32, axis=-1, keepdims=True) + EPS)
    if gain is not None:
        y = y * gain.astype(jnp.float32)
    return y.astype(x.dtype)

def _complex_affine_combine(e1, e2):
    a1r, a1i, b1r, b1i = e1
    a2r, a2i, b2r, b2i = e2
    return (a1r * a2r - a1i * a2i,
            a1r * a2i + a1i * a2r,
            a2r * b1r - a2i * b1i + b2r,
            a2r * b1i + a2i * b1r + b2i)

def s5_scan(u, a_re, a_im, log_dt, b_re, b_im, c_re, c_im, d_skip, h0_re, h0_im):
    bsz, t_len, _ = u.shape
    f32 = jnp.float32
    ug = u.astype(f32).reshape(bsz, t_len, SSM_GROUPS, SSM_GROUP)
    ar = a_re.astype(f32)
    ai = a_im.astype(f32)
    dt = jnp.exp(log_dt.astype(f32))[:, None]
    decay = jnp.exp(ar * dt)
    lam_re = decay * jnp.cos(ai * dt)
    lam_im = decay * jnp.sin(ai * dt)
    den = ar * ar + ai * ai
    num_re = lam_re - 1.0
    coef_re = (num_re * ar + lam_im * ai) / den
    coef_im = (lam_im * ar - num_re * ai) / den
    br = b_re.astype(f32)
    bi = b_im.astype(f32)
    bb_re = coef_re[..., None] * br - coef_im[..., None] * bi
    bb_im = coef_re[..., None] * bi + coef_im[..., None] * br
    x_re = jnp.einsum('gpj,btgj->btgp', bb_re, ug)
    x_im = jnp.einsum('gpj,btgj->btgp', bb_im, ug)
    if h0_re is not None:
        hr0 = h0_re.astype(f32)
        hi0 = h0_im.astype(f32)
        x_re = x_re.at[:, 0].add(lam_re * hr0 - lam_im * hi0)
        x_im = x_im.at[:, 0].add(lam_re * hi0 + lam_im * hr0)
    lr = jnp.broadcast_to(lam_re, x_re.shape)
    li = jnp.broadcast_to(lam_im, x_im.shape)
    _, _, h_re, h_im = lax.associative_scan(_complex_affine_combine, (lr, li, x_re, x_im), axis=1)
    y = (jnp.einsum('gjp,btgp->btgj', c_re.astype(f32), h_re)
         - jnp.einsum('gjp,btgp->btgj', c_im.astype(f32), h_im)
         + d_skip.astype(f32).reshape(SSM_GROUPS, SSM_GROUP) * ug)
    return y.reshape(bsz, t_len, SSM_WIDTH).astype(u.dtype), h_re[:, -1], h_im[:, -1]

def dsa_block(q, qi, wi, q_pos, k, v, ki, k_pos, top_k):
    f32 = jnp.float32
    idx_dot = jnp.einsum('bthi,bsi->bths', qi, ki)
    score = jnp.einsum('bth,bths->bts', wi.astype(f32), jax.nn.relu(idx_dot).astype(f32))
    q_chunk = q_pos // CHUNK
    admissible = (k_pos[None, :] // CHUNK) <= q_chunk[:, None]
    score = jnp.where(admissible[None], score, NEG_INF)
    _, sel = lax.top_k(score, top_k)
    gather = jax.vmap(lambda rows, ids: rows[ids])
    k_sel = gather(k, sel)
    v_sel = gather(v, sel)
    valid = (k_pos[sel] // CHUNK) <= q_chunk[None, :, None]
    logits = jnp.einsum('bthd,btjd->bthj', q, k_sel).astype(f32) * HEAD_DIM ** -0.5
    logits = jnp.where(valid[:, :, None, :], logits, NEG_INF)
    probs = jax.nn.softmax(logits, axis=-1).astype(v.dtype)
    return jnp.einsum('bthj,btjd->bthd', probs, v_sel)

def dsa_prompt(q, k, v, qi, ki, wi):
    bsz, seq_len = k.shape[0], k.shape[1]
    top_k = min(TOPK_MAX, seq_len // 4)
    pos = jnp.arange(seq_len, dtype=jnp.int32)
    n_blk = seq_len // Q_BLOCK

    def to_blocks(t):
        return jnp.swapaxes(t.reshape((bsz, n_blk, Q_BLOCK) + t.shape[2:]), 0, 1)

    def body(args):
        qb, qib, wib, pb = args
        return dsa_block(qb, qib, wib, pb, k, v, ki, pos, top_k)

    out = lax.map(body, (to_blocks(q), to_blocks(qi), to_blocks(wi), pos.reshape(n_blk, Q_BLOCK)))
    return jnp.swapaxes(out, 0, 1).reshape(bsz, seq_len, N_HEADS, HEAD_DIM)

def dsa_step(q, k, v, qi, ki, wi, past_k, past_v, past_ki):
    past_len = past_k.shape[1]
    t_len = q.shape[1]
    k_all = jnp.concatenate([past_k, k], axis=1)
    v_all = jnp.concatenate([past_v, v], axis=1)
    ki_all = jnp.concatenate([past_ki, ki], axis=1)
    total = past_len + t_len
    top_k = min(TOPK_MAX, total // 4)
    k_pos = jnp.arange(total, dtype=jnp.int32)
    q_pos = past_len + jnp.arange(t_len, dtype=jnp.int32)
    return dsa_block(q, qi, wi, q_pos, k_all, v_all, ki_all, k_pos, top_k)

def hier_moe(h, w_rg, b_rg, w_re, b_re, w_gate, w_up, w_down):
    shp = h.shape
    f32 = jnp.float32
    t = h.reshape(-1, D_MODEL)
    g_logits = (t @ w_rg + b_rg).astype(f32)
    g_prob = jax.nn.softmax(g_logits, axis=-1)
    g_idx = jnp.argmax(g_logits, axis=-1)
    g_w = jnp.take_along_axis(g_prob, g_idx[:, None], axis=-1)
    e_logits = (t @ w_re + b_re).astype(f32).reshape(-1, N_GROUPS, EXPERTS_PER_GROUP)
    e_in = jnp.take_along_axis(e_logits, g_idx[:, None, None], axis=1)[:, 0]
    top_v, top_i = lax.top_k(e_in, TOP_K_IN_GROUP)
    top_w = jax.nn.softmax(top_v, axis=-1) * g_w
    eid = g_idx[:, None] * EXPERTS_PER_GROUP + top_i
    combine = jnp.sum(jax.nn.one_hot(eid, N_EXPERTS, dtype=f32) * top_w[..., None], axis=1)
    hid = jax.nn.silu(jnp.einsum('nd,edf->nef', t, w_gate)) * jnp.einsum('nd,edf->nef', t, w_up)
    out = jnp.einsum('nef,efd->nd', hid * combine[..., None].astype(hid.dtype), w_down)
    return out.reshape(shp)

def hybrid_layer(x, c, lw, past):
    (w_ada, b_ada, w_in, a_re, a_im, log_dt, sb_re, sb_im, sc_re, sc_im, d_skip, w_glu,
     q_gain, k_gain, kidx_gain, w_attn_out, w_out,
     w_rg, b_rg, w_re, b_re, w_gate, w_up, w_down) = lw
    bsz, t_len, _ = x.shape
    mod = jax.nn.silu(c) @ w_ada + b_ada
    sh1, sc1, g1, sh2, sc2, g2 = jnp.split(mod[:, None, :], 6, axis=-1)
    h = rms_norm(x) * (1.0 + sc1) + sh1
    proj = h @ w_in
    u, q, k, v, qi, ki, wi, gate_a, gate_b = jnp.split(proj, IN_OFFSETS, axis=-1)
    q = rms_norm(q.reshape(bsz, t_len, N_HEADS, HEAD_DIM), q_gain)
    k = rms_norm(k, k_gain)
    qi = qi.reshape(bsz, t_len, IDX_HEADS, IDX_DIM)
    ki = rms_norm(ki, kidx_gain)
    wi = wi * IDX_WEIGHT_SCALE
    if past is None:
        y_ssm, s_re, s_im = s5_scan(u, a_re, a_im, log_dt, sb_re, sb_im, sc_re, sc_im, d_skip, None, None)
        attn = dsa_prompt(q, k, v, qi, ki, wi)
    else:
        past_k, past_v, past_ki, h0_re, h0_im = past
        y_ssm, s_re, s_im = s5_scan(u, a_re, a_im, log_dt, sb_re, sb_im, sc_re, sc_im, d_skip, h0_re, h0_im)
        attn = dsa_step(q, k, v, qi, ki, wi, past_k, past_v, past_ki)
    z = jax.nn.gelu(y_ssm)
    glu_val, glu_gate = jnp.split(z @ w_glu, 2, axis=-1)
    out_a = glu_val * jax.nn.sigmoid(glu_gate)
    out_b = attn.reshape(bsz, t_len, ATTN_WIDTH) @ w_attn_out
    merged = jax.nn.sigmoid(gate_a) * out_a + jax.nn.sigmoid(gate_b) * out_b
    x = x + g1 * (merged @ w_out)
    h2 = rms_norm(x) * (1.0 + sc2) + sh2
    x = x + g2 * hier_moe(h2, w_rg, b_rg, w_re, b_re, w_gate, w_up, w_down)
    return x, k, v, ki, s_re, s_im

def setup_inputs(seed: int = 0) -> dict:
    key = jax.random.key(seed)
    ks = jax.random.split(key, 40)
    f32 = jnp.float32

    def nrm(i, shape, scale):
        return jax.random.normal(ks[i], shape, f32) * scale

    G, P, J = SSM_GROUPS, SSM_STATE, SSM_GROUP
    return {
        'x_prompt': nrm(0, (BATCH, SEQ, D_MODEL), 1.0),
        'x_sample': nrm(1, (DEC_BATCH, DEC_SEQ, D_MODEL), 1.0),
        'cache_k': nrm(2, (DEPTH, DEC_BATCH, PAST_LEN, HEAD_DIM), 1.0),
        'cache_v': nrm(3, (DEPTH, DEC_BATCH, PAST_LEN, HEAD_DIM), 1.0),
        'cache_kidx': nrm(4, (DEPTH, DEC_BATCH, PAST_LEN, IDX_DIM), 1.0),
        'state_ssm_re': nrm(5, (DEPTH, DEC_BATCH, G, P), 0.3),
        'state_ssm_im': nrm(6, (DEPTH, DEC_BATCH, G, P), 0.3),
        'c_prompt': nrm(7, (BATCH, D_MODEL), 1.0),
        'c_sample': nrm(8, (DEC_BATCH, D_MODEL), 1.0),
        'w_ada': nrm(9, (DEPTH, D_MODEL, 6 * D_MODEL), D_MODEL ** -0.5),
        'b_ada': nrm(10, (DEPTH, 6 * D_MODEL), 0.02),
        'w_in': nrm(11, (DEPTH, D_MODEL, IN_WIDTH), D_MODEL ** -0.5),
        'ssm_a_re': -0.5 + nrm(12, (DEPTH, G, P), 0.01),
        'ssm_a_im': jnp.pi * jnp.arange(P, dtype=f32) + nrm(13, (DEPTH, G, P), 0.01),
        'ssm_log_dt': jax.random.uniform(ks[14], (DEPTH, G), f32, math.log(DT_MIN), math.log(DT_MAX)),
        'ssm_b_re': nrm(15, (DEPTH, G, P, J), (2 * J) ** -0.5),
        'ssm_b_im': nrm(16, (DEPTH, G, P, J), (2 * J) ** -0.5),
        'ssm_c_re': nrm(17, (DEPTH, G, J, P), P ** -0.5),
        'ssm_c_im': nrm(18, (DEPTH, G, J, P), P ** -0.5),
        'ssm_d': nrm(19, (DEPTH, SSM_WIDTH), 0.5),
        'w_glu': nrm(20, (DEPTH, SSM_WIDTH, 2 * D_MODEL), SSM_WIDTH ** -0.5),
        'q_gain': 1.0 + nrm(21, (DEPTH, HEAD_DIM), 0.02),
        'k_gain': 1.0 + nrm(22, (DEPTH, HEAD_DIM), 0.02),
        'kidx_gain': 1.0 + nrm(23, (DEPTH, IDX_DIM), 0.02),
        'w_attn_out': nrm(24, (DEPTH, ATTN_WIDTH, D_MODEL), ATTN_WIDTH ** -0.5),
        'w_out': nrm(25, (DEPTH, D_MODEL, D_MODEL), D_MODEL ** -0.5),
        'w_route_group': nrm(26, (DEPTH, D_MODEL, N_GROUPS), D_MODEL ** -0.5),
        'b_route_group': nrm(27, (DEPTH, N_GROUPS), 0.01),
        'w_route_expert': nrm(28, (DEPTH, D_MODEL, N_EXPERTS), D_MODEL ** -0.5),
        'b_route_expert': nrm(29, (DEPTH, N_EXPERTS), 0.01),
        'w_gate': nrm(30, (DEPTH, N_EXPERTS, D_MODEL, EXPERT_DIM), D_MODEL ** -0.5),
        'w_up': nrm(31, (DEPTH, N_EXPERTS, D_MODEL, EXPERT_DIM), D_MODEL ** -0.5),
        'w_down': nrm(32, (DEPTH, N_EXPERTS, EXPERT_DIM, D_MODEL), EXPERT_DIM ** -0.5),
    }

def reference(x_prompt, x_sample, cache_k, cache_v, cache_kidx, state_ssm_re, state_ssm_im,
              c_prompt, c_sample, w_ada, b_ada, w_in, ssm_a_re, ssm_a_im, ssm_log_dt,
              ssm_b_re, ssm_b_im, ssm_c_re, ssm_c_im, ssm_d, w_glu, q_gain, k_gain, kidx_gain,
              w_attn_out, w_out, w_route_group, b_route_group, w_route_expert, b_route_expert,
              w_gate, w_up, w_down):
    xp = x_prompt
    xs = x_sample
    kp_l, vp_l, kip_l, srp_l, sip_l = [], [], [], [], []
    ks_l, vs_l, kis_l, srs_l, sis_l = [], [], [], [], []
    for l in range(DEPTH):
        lw = (w_ada[l], b_ada[l], w_in[l], ssm_a_re[l], ssm_a_im[l], ssm_log_dt[l],
              ssm_b_re[l], ssm_b_im[l], ssm_c_re[l], ssm_c_im[l], ssm_d[l], w_glu[l],
              q_gain[l], k_gain[l], kidx_gain[l], w_attn_out[l], w_out[l],
              w_route_group[l], b_route_group[l], w_route_expert[l], b_route_expert[l],
              w_gate[l], w_up[l], w_down[l])
        xp, kp, vp, kip, srp, sip = hybrid_layer(xp, c_prompt, lw, None)
        past = (cache_k[l], cache_v[l], cache_kidx[l], state_ssm_re[l], state_ssm_im[l])
        xs, kss, vss, kiss, srs, sis = hybrid_layer(xs, c_sample, lw, past)
        kp_l.append(kp); vp_l.append(vp); kip_l.append(kip); srp_l.append(srp); sip_l.append(sip)
        ks_l.append(kss); vs_l.append(vss); kis_l.append(kiss); srs_l.append(srs); sis_l.append(sis)
    return (xp, xs,
            jnp.stack(kp_l), jnp.stack(vp_l), jnp.stack(kip_l), jnp.stack(srp_l), jnp.stack(sip_l),
            jnp.stack(ks_l), jnp.stack(vs_l), jnp.stack(kis_l), jnp.stack(srs_l), jnp.stack(sis_l))


_drawn_inputs = setup_inputs


def setup_inputs(seed=0):
    import zlib

    import numpy as np

    out = dict(_drawn_inputs(seed))
    spreads = {}
    factors = {'ssm_a_re': 13.387,
     'q_gain': 8.0,
     'k_gain': 3.439,
     'kidx_gain': 3.335,
     'b_route_expert': 8.0,
     'b_route_group': 2.967}
    for name, (base, spread) in spreads.items():
        noise = np.random.default_rng([zlib.crc32(name.encode()), seed]).standard_normal(out[name].shape)
        drawn = base * np.exp(spread * noise) if base else spread * noise
        out[name] = __import__('jax').numpy.asarray(drawn.astype(out[name].dtype))
    for name, factor in factors.items():
        out[name] = (out[name] * factor).astype(out[name].dtype)
    return out
```

```python
import math
from contextlib import ExitStack

import concourse.bass as bass
from concourse import mybir

F32 = mybir.dt.float32
BF16 = mybir.dt.bfloat16
I32 = mybir.dt.int32
U32 = mybir.dt.uint32
ALU = mybir.AluOpType
ACT = mybir.ActivationFunctionType
AX = mybir.AxisListType

P = 128
D = 1024
KD = D // P
SEQ, DEC = 1024, 64
NT = SEQ + DEC
PT = SEQ // P
TILES = PT + 1
PAST = 2048
CB = PAST // P
NS = PAST + DEC
EPS = 1e-6
NEG = -1e30
H, HD = 8, 64
IH, ID = 8, 32
TOPK = 256
G, ST, J = 32, 64, 16
PAIR = G // 2
T = 8
NCH = SEQ // T
SCH = DEC // T
COLS = NCH + 1 + SCH + 1
S0 = NCH + 1
NG, EPG, NE, FD = 4, 4, 16, 256
SLOTS = 256
MAXT = (2 * NT + NE * (SLOTS - 1)) // SLOTS
MAXT += MAXT % 2
OFF_U, OFF_Q, OFF_R, OFF_GA, OFF_GB = 0, 512, 1024, 1448, 2472
RW = OFF_GA - OFF_R
TW = 512 + RW
K0, V0, QI0, KI0, WI0 = 512, 576, 640, 896, 928


def rows_of(t):
    return P if t < PT else DEC


class Chain:

    def __init__(self, engine, sem):
        self.engine, self.sem, self.n = engine, sem, 0

    def __call__(self, instruction):
        instruction.then_inc(self.sem, 1)
        self.n += 1
        self.engine.wait_ge(self.sem, self.n)


class Mem:
    pass


def constants(nc, m, A):
    made = m.sem("constants_made")
    with nc.Block() as block:
        @block.gpsimd
        def _(pool):
            step = Chain(pool, made)
            step(nc.gpsimd.memset(m.ident[:, :], 0.0))
            step(nc.gpsimd.affine_select(out=m.ident[:, :], in_=m.ident[:, :], compare_op=ALU.not_equal,
                                         fill=1.0, base=0, pattern=[[-1, P]], channel_multiplier=1))
            nc.gpsimd.memset(m.ones[:, :], 1.0)
            step(nc.gpsimd.memset(m.tri[:, :], 1.0))
            step(nc.gpsimd.affine_select(out=m.tri[:, :], in_=m.tri[:, :], compare_op=ALU.is_gt,
                                         fill=0.0, base=0, pattern=[[1, P]], channel_multiplier=-1))


def adaln(nc, m, A, first, last, tag):
    with ExitStack() as ctx:
        n = last - first
        NB = 3
        w = ctx.enter_context(nc.sbuf_tensor("wada" + tag, [P, NB, KD, 512], F32))
        b = ctx.enter_context(nc.sbuf_tensor("bada" + tag, [1, n * 512], F32))
        row = m.modrow
        stored = m.sem("ada_row_stored" + tag)
        c16 = ctx.enter_context(nc.sbuf_tensor("c16" + tag, [2 * KD, P], F32))
        w_in = [m.sem(f"ada_w_loaded{i}{tag}") for i in range(NB)]
        c_in = m.sem("ada_c_loaded" + tag)
        c_t = m.sem("ada_c_transposed" + tag)
        c_s = m.sem("ada_c_silu" + tag)
        ps = m.sem("ada_psum_ready" + tag)
        free = m.sem("ada_psum_free" + tag)
        wsrc = A.w_ada.rearrange("(k p) n -> p k n", p=P)
        with nc.Block() as block:
            @block.sync
            def _(sp):
                sp.dma_start(c16[0:KD, :], A.c_prompt.rearrange("o (k p) -> (o k) p", p=P)).then_inc(c_in, 16)
                sp.dma_start(c16[KD:2 * KD, :], A.c_sample.rearrange("o (k p) -> (o k) p", p=P)).then_inc(c_in, 16)
                sp.dma_start(b[:, :], A.b_ada[:, first * 512:last * 512]).then_inc(c_in, 16)
                for i in range(n):
                    if i >= NB:
                        sp.wait_ge(ps, i - NB + 1)
                    sp.dma_start(w[:, i % NB, :, :], wsrc[:, :, (first + i) * 512:(first + i + 1) * 512]) \
                        .then_inc(w_in[i % NB], 16)
                sp.wait_ge(free, n)
                sp.dma_start(m.mod_dram[:, first * 512:last * 512], row[0:2, 0:n * 512]).then_inc(stored, 16)
                sp.wait_ge(stored, 16)

            @block.tensor
            def _(pe):
                pe.wait_ge(c_in, 48)
                nc.tensor.transpose(m.ps[:, 7, 0:2 * KD], c16[:, :], m.ident[0:2 * KD, 0:2 * KD]).then_inc(c_t, 1)
                pe.wait_ge(c_s, 1)
                for i in range(n):
                    pe.wait_ge(w_in[i % NB], 16 * (i // NB + 1))
                    if i >= 2:
                        pe.wait_ge(free, i - 1)
                    for k in range(KD):
                        nc.tensor.matmul(m.ps[0:2, i % 2, :], m.cT[:, k, :], w[:, i % NB, k, :],
                                         start=k == 0, stop=False)
                    nc.tensor.matmul(m.ps[0:2, i % 2, :], m.ones[0:1, 0:2], b[0:1, i * 512:(i + 1) * 512],
                                     start=False, stop=True).then_inc(ps, 1)

            @block.scalar
            def _(act):
                act.wait_ge(c_t, 1)
                nc.scalar.activation(m.cT[:, :, :].rearrange("p k s -> p s k"),
                                     m.ps[:, 7, 0:2 * KD].rearrange("p (s k) -> p s k", s=2), ACT.Silu).then_inc(c_s, 1)

            @block.vector
            def _(dve):
                for i in range(n):
                    dve.wait_ge(ps, i + 1)
                    nc.vector.tensor_copy(row[0:2, i * 512:(i + 1) * 512],
                                          m.ps[0:2, i % 2, :]).then_inc(free, 1)


def mod_columns(nc, m):
    tr = m.sem("modcol_transposed")
    with nc.Block() as block:
        @block.tensor
        def _(pe):
            for j in range(2 * KD):
                i = nc.tensor.transpose(m.ps[:, 0, 2 * j:2 * j + 2], m.modrow[0:2, j * P:(j + 1) * P], m.ident[0:2, 0:2])
            i.then_inc(tr, 1)

        @block.vector
        def _(dve):
            dve.wait_ge(tr, 1)
            nc.vector.tensor_copy(m.sh1[:, :, :], m.ps[:, 0, 0:2 * KD].rearrange("p (k s) -> p k s", s=2))
            nc.vector.tensor_scalar(m.sc1[:, :, :], m.ps[:, 0, 2 * KD:4 * KD].rearrange("p (k s) -> p k s", s=2),
                                    1.0, None, ALU.add)


def norm_in(nc, m, A):
    with ExitStack() as ctx:
        NB = 3
        x = ctx.enter_context(nc.sbuf_tensor("n1_x", [P, NB, D], F32))
        xn = ctx.enter_context(nc.sbuf_tensor("n1_xn", [P, 2, D], F32))
        junk = ctx.enter_context(nc.sbuf_tensor("n1_sq", [P, D], F32))
        st = ctx.enter_context(nc.sbuf_tensor("n1_st", [P, TILES, 4], F32))
        x_in = [m.sem(f"n1_x_loaded{i}") for i in range(NB)]
        sq, ms, sr, chain = m.sem("n1_sumsq"), m.sem("n1_meansq"), m.sem("n1_root"), m.sem("n1_dve_chain")
        xnr, tr, ev, sqc = m.sem("n1_xn_ready"), m.sem("n1_transposed"), m.sem("n1_evacuated"), m.sem("n1_act_chain")
        with nc.Block() as block:
            @block.sync
            def _(sp):
                for t in range(TILES):
                    r = rows_of(t)
                    if t >= NB:
                        sp.wait_ge(xnr, t - NB + 1)
                    src = A.x_prompt[0, t * P:(t + 1) * P, :] if t < PT else A.x_sample[0, :, :]
                    sp.dma_start(x[0:r, t % NB, :], src).then_inc(x_in[t % NB], 16)

            @block.scalar
            def _(act):
                for t in range(TILES):
                    r = rows_of(t)
                    act.wait_ge(x_in[t % NB], 16 * (t // NB + 1))
                    if t:
                        act.wait_ge(sq, t)
                    nc.scalar.activation(junk[0:r, :], x[0:r, t % NB, :], ACT.Square,
                                         accum_out=st[0:r, t, 0:1]).then_inc(sq, 1)
                    act.wait_ge(ms, t + 1)
                    nc.scalar.activation(st[0:r, t, 2:3], st[0:r, t, 1:2], ACT.Sqrt).then_inc(sr, 1)

            @block.vector
            def _(dve):
                def evacuate(t):
                    r, s = rows_of(t), int(t == PT)
                    dve.wait_ge(tr, t + 1)
                    for k in range(KD):
                        i = nc.vector.tensor_scalar(m.hT[:, k, t * P:t * P + r],
                                                    m.ps[:, 2 * (t % 2) + k // 4, (k % 4) * P:(k % 4) * P + r],
                                                    m.sc1[:, k, s:s + 1], m.sh1[:, k, s:s + 1], ALU.mult, ALU.add)
                    i.then_inc(ev, 1)

                step = Chain(dve, chain)
                for t in range(TILES):
                    r = rows_of(t)
                    dve.wait_ge(sq, t + 1)
                    nc.vector.tensor_scalar(st[0:r, t, 1:2], st[0:r, t, 0:1], 1.0 / D, EPS, ALU.mult, ALU.add).then_inc(ms, 1)
                    dve.wait_ge(sr, t + 1)
                    step(nc.vector.reciprocal(st[0:r, t, 3:4], st[0:r, t, 2:3]))
                    if t >= 2:
                        dve.wait_ge(tr, t - 1)
                    nc.vector.tensor_scalar(xn[0:r, t % 2, :], x[0:r, t % NB, :], st[0:r, t, 3:4], None,
                                            ALU.mult).then_inc(xnr, 1)
                    if t:
                        evacuate(t - 1)
                evacuate(PT)

            @block.tensor
            def _(pe):
                for t in range(TILES):
                    r = rows_of(t)
                    pe.wait_ge(xnr, t + 1)
                    if t >= 2:
                        pe.wait_ge(ev, t - 1)
                    for k in range(KD):
                        i = nc.tensor.transpose(m.ps[:, 2 * (t % 2) + k // 4, (k % 4) * P:(k % 4) * P + r],
                                                xn[0:r, t % 2, k * P:(k + 1) * P], m.ident[0:r, 0:r])
                    i.then_inc(tr, 1)


def bc(ap, axis, n):
    shape = list(ap.shape)
    return ap.unsqueeze(axis).broadcast_to(shape[:axis] + [n] + shape[axis:])


def project(nc, m, A, O):
    with ExitStack() as ctx:
        sb = lambda name, shape: ctx.enter_context(nc.sbuf_tensor(name, shape, F32))
        w = sb("pj_w", [P, KD, 512 + 512 + RW])
        tok = sb("pj_tok", [P, 2, TW])
        sq = sb("pj_sq", [P, 608])
        st = sb("pj_st", [P, TILES, 4, 10])
        qn = sb("pj_qn", [P, 2, 512])
        kk = sb("pj_kk", [P, 2, 2, HD])
        ki4 = sb("pj_ki4", [P, 2, 4, ID])
        gk = sb("pj_gk", [P, HD])
        gki = sb("pj_gki", [P, ID])
        gqr = sb("pj_gqr", [2, HD])
        gq = sb("pj_gq", [P, 1])
        wl, gl = m.sem("pj_weights_loaded"), m.sem("pj_gains_loaded")
        qr, tokr, sqr, msr, rtr = (m.sem("pj_" + n) for n in ("qr_psum", "tok_copied", "squared", "mean", "root"))
        nr, tr, ev, chain = (m.sem("pj_" + n) for n in ("normalised", "transposed", "evacuated", "dve_chain"))
        up, ue, red = (m.sem("pj_" + n) for n in ("u_psum", "u_copied", "reduced"))
        vst = [m.sem(f"pj_v_stored{i}") for i in range(2)]
        kst = [m.sem(f"pj_k_stored{i}") for i in range(2)]
        gqt, gqe, qst = m.sem("pj_gq_transposed"), m.sem("pj_gq_copied"), m.sem("pj_q_stored")
        wsrc = A.w_in.rearrange("(k p) n -> p k n", p=P)
        with nc.Block() as block:
            @block.sync
            def _(sp):
                sp.dma_start(w[:, :, 512:1024], wsrc[:, :, 512:1024]).then_inc(wl, 16)
                sp.dma_start(w[:, :, 1024:1024 + RW], wsrc[:, :, 1024:OFF_GA]).then_inc(wl, 16)
                sp.dma_start(w[:, :, 0:512], wsrc[:, :, 0:512]).then_inc(wl, 16)
                sp.dma_start(gk[:, :], A.k_gain.broadcast_to([P, HD])).then_inc(gl, 16)
                sp.dma_start(gki[:, :], A.kidx_gain.broadcast_to([P, ID])).then_inc(gl, 16)
                sp.dma_start(gqr[:, :], A.q_gain.broadcast_to([2, HD])).then_inc(gl, 16)
                for t in range(TILES):
                    r = rows_of(t)
                    sl = slice(t * P, t * P + r)
                    vo = O.v_prompt[0, 0, sl, :] if t < PT else O.v_sample[0, 0, :, :]
                    ko = O.k_prompt[0, 0, sl, :] if t < PT else O.k_sample[0, 0, :, :]
                    kio = O.kidx_prompt[0, 0, sl, :] if t < PT else O.kidx_sample[0, 0, :, :]
                    sp.wait_ge(tokr, t + 1)
                    sp.dma_start(vo, tok[0:r, t % 2, V0:V0 + HD]).then_inc(vst[t % 2], 16)
                    sp.wait_ge(nr, t + 1)
                    sp.dma_start(ko, kk[0:r, t % 2, 0, :]).then_inc(kst[t % 2], 16)
                    sp.dma_start(kio, ki4[0:r, t % 2, 0, :]).then_inc(kst[t % 2], 16)
                sp.wait_ge(ev, TILES)
                sp.dma_start(m.q_dram, m.qT[:, :, :]).then_inc(qst, 16)
                sp.wait_ge(qst, 16)
                for i in range(2):
                    n = (TILES + 1 - i) // 2
                    sp.wait_ge(vst[i], 16 * n)
                    sp.wait_ge(kst[i], 32 * n)

            @block.tensor
            def _(pe):
                def transposes(t):
                    r = rows_of(t)
                    pe.wait_ge(nr, t + 1)
                    if t:
                        pe.wait_ge(ev, t)
                    for j in range(8):
                        src = (qn[0:r, t % 2, j * P:(j + 1) * P] if j < 4 else
                               m.tokqi[0:r, t % 2, (j - 4) * P:(j - 3) * P] if j < 6 else
                               (kk, ki4)[j - 6][0:r, t % 2, :, :].rearrange("p a d -> p (a d)"))
                        i = nc.tensor.transpose(m.ps[:, 6 + j // 4, (j % 4) * P:(j % 4) * P + r], src, m.ident[0:r, 0:r])
                    i.then_inc(tr, 1)

                pe.wait_ge(gl, 48)
                nc.tensor.transpose(m.ps[0:HD, 7, 0:2], gqr[:, :], m.ident[0:2, 0:2]).then_inc(gqt, 1)
                pe.wait_ge(gqe, 1)
                pe.wait_ge(wl, 48)
                for t in range(TILES):
                    r = rows_of(t)
                    if t >= 2:
                        pe.wait_ge(sqr, t - 1)
                    for k in range(KD):
                        nc.tensor.matmul(m.ps[0:r, 2 * (t % 2), :], m.hT[:, k, t * P:t * P + r], w[:, k, 512:1024],
                                         start=k == 0, stop=k == KD - 1)
                    for k in range(KD):
                        i = nc.tensor.matmul(m.ps[0:r, 2 * (t % 2) + 1, 0:RW], m.hT[:, k, t * P:t * P + r],
                                             w[:, k, 1024:1024 + RW], start=k == 0, stop=k == KD - 1)
                    i.then_inc(qr, 1)
                    if t >= 2:
                        pe.wait_ge(ue, t - 1)
                    for k in range(KD):
                        lhs = m.hT[:, k, t:SEQ:T] if t < T else m.hT[:, k, SEQ:NT]
                        i = nc.tensor.matmul(m.ps[0:r, 4 + t % 2, :], lhs, w[:, k, 0:512], start=k == 0, stop=k == KD - 1)
                    i.then_inc(up, 1)
                    if t:
                        transposes(t - 1)
                transposes(PT)

            @block.scalar
            def _(act):
                act.wait_ge(gqt, 1)
                nc.scalar.copy(gq[0:HD, :], m.ps[0:HD, 7, 0:1])
                nc.scalar.copy(gq[HD:P, :], m.ps[0:HD, 7, 1:2]).then_inc(gqe, 1)
                for t in range(TILES):
                    r = rows_of(t)
                    act.wait_ge(qr, t + 1)
                    if t >= 2:
                        act.wait_ge(nr, t - 1)
                        act.wait_ge(vst[t % 2], 16 * (t // 2))
                        act.wait_ge(tr, t - 1)
                    b = 2 * (t % 2)
                    nc.scalar.copy(tok[0:r, t % 2, 0:512], m.ps[0:r, b, :])
                    nc.scalar.copy(m.tokqi[0:r, t % 2, :], m.ps[0:r, b + 1, 128:384])
                    nc.scalar.copy(tok[0:r, t % 2, 512:TW], m.ps[0:r, b + 1, 0:RW]).then_inc(tokr, 1)
                    if t:
                        act.wait_ge(red, t)
                    nc.scalar.activation(sq[0:r, 0:512], m.ps[0:r, b, :], ACT.Square)
                    nc.scalar.activation(sq[0:r, 512:576], m.ps[0:r, b + 1, 0:64], ACT.Square)
                    nc.scalar.activation(sq[0:r, 576:608], m.ps[0:r, b + 1, 384:416], ACT.Square).then_inc(sqr, 1)
                    act.wait_ge(msr, t + 1)
                    nc.scalar.activation(st[0:r, t, 2, :], st[0:r, t, 1, :], ACT.Sqrt).then_inc(rtr, 1)
                    act.wait_ge(up, t + 1)
                    src = m.ps[0:r, 4 + t % 2, :]
                    if t < T:
                        i = nc.scalar.copy(m.u[:, :, t, :], src.rearrange("c (g j) -> c g j", j=J))
                    else:
                        i = nc.scalar.copy(m.us[:, :], src)
                    i.then_inc(ue, 1)

            @block.vector
            def _(dve):
                step = Chain(dve, chain)

                def evacuate(t):
                    r = rows_of(t)
                    sl = slice(t * P, t * P + r)
                    dve.wait_ge(tr, t + 1)
                    a = m.ps[:, 6, :].rearrange("p (j t) -> p j t", t=P)
                    b = m.ps[:, 7, :].rearrange("p (j t) -> p j t", t=P)
                    nc.vector.tensor_scalar(m.qT[:, :, sl], a[:, :, 0:r], gq[:, 0:1], None, ALU.mult)
                    nc.vector.tensor_copy(m.qiT[:, :, sl], b[:, 0:2, 0:r])
                    nc.vector.tensor_copy(m.kT[:, sl], b[:, 2, 0:r])
                    nc.vector.tensor_copy(m.kiT[:, sl], b[:, 3, 0:r]).then_inc(ev, 1)

                dve.wait_ge(gl, 48)
                dve.wait_ge(gqe, 1)
                for t in range(TILES):
                    r = rows_of(t)
                    dve.wait_ge(sqr, t + 1)
                    ss, ms, rt, rs = (st[0:r, t, j, :] for j in range(4))
                    nc.vector.tensor_reduce(ss[:, 0:9], sq[0:r, 0:576].rearrange("p (h d) -> p h d", d=HD), AX.X, ALU.add)
                    i = nc.vector.tensor_reduce(ss[:, 9:10], sq[0:r, 576:608], AX.X, ALU.add)
                    i.then_inc(red, 1)
                    dve.wait_ge(red, t + 1)
                    nc.vector.tensor_scalar(ms[:, 0:9], ss[:, 0:9], 1.0 / HD, EPS, ALU.mult, ALU.add)
                    nc.vector.tensor_scalar(ms[:, 9:10], ss[:, 9:10], 1.0 / ID, EPS, ALU.mult, ALU.add).then_inc(msr, 1)
                    dve.wait_ge(rtr, t + 1)
                    step(nc.vector.reciprocal(rs, rt))
                    if t >= 2:
                        dve.wait_ge(tr, t - 1)
                        dve.wait_ge(kst[t % 2], 32 * (t // 2))
                    row = tok[0:r, t % 2, :]
                    nc.vector.tensor_tensor(qn[0:r, t % 2, :].rearrange("p (h d) -> p h d", d=HD),
                                            row[:, 0:512].rearrange("p (h d) -> p h d", d=HD),
                                            bc(rs[:, 0:8], 2, HD), ALU.mult)
                    nc.vector.scalar_tensor_tensor(kk[0:r, t % 2, :, :], bc(row[:, K0:K0 + HD], 1, 2), rs[:, 8:9],
                                                   bc(gk[0:r, :], 1, 2), ALU.mult, ALU.mult)
                    nc.vector.scalar_tensor_tensor(ki4[0:r, t % 2, :, :], bc(row[:, KI0:KI0 + ID], 1, 4), rs[:, 9:10],
                                                   bc(gki[0:r, :], 1, 4), ALU.mult, ALU.mult)
                    nc.vector.tensor_scalar(m.wi[0:r, t, :], row[:, WI0:WI0 + IH], (IH * ID) ** -0.5, None, ALU.mult)
                    vd = m.v[:, t, :] if t < PT else m.vs[0:DEC, CB, :]
                    nc.vector.tensor_copy(vd, row[:, V0:V0 + HD]).then_inc(nr, 1)
                    if t:
                        evacuate(t - 1)
                evacuate(PT)


def cache_keys(nc, m, A):
    with ExitStack() as ctx:
        sb = lambda name, shape: ctx.enter_context(nc.sbuf_tensor(name, shape, F32))
        ck = sb("ck_k", [P, CB, HD])
        cki = sb("ck_ki", [P, CB, ID])
        kk = sb("ck_kk", [P, CB, 2, HD])
        ki4 = sb("ck_ki4", [P, CB, 4, ID])
        ld, dup, tr, ev = (m.sem("ck_" + n) for n in ("loaded", "repeated", "transposed", "evacuated"))
        with nc.Block() as block:
            @block.sync
            def _(sp):
                sp.dma_start(ck[:, :, :], A.cache_k[0].rearrange("(b p) d -> p b d", p=P)).then_inc(ld, 16)
                sp.dma_start(cki[:, :, :], A.cache_kidx[0].rearrange("(b p) d -> p b d", p=P)).then_inc(ld, 16)
                sp.dma_start(m.vs[:, 0:CB, :], A.cache_v[0].rearrange("(b p) d -> p b d", p=P)).then_inc(ld, 16)

            @block.vector
            def _(dve):
                dve.wait_ge(ld, 48)
                nc.vector.tensor_copy(m.kTs[:, PAST:], m.kT[:, SEQ:NT])
                nc.vector.tensor_copy(m.kiTs[:, PAST:], m.kiT[:, SEQ:NT])
                nc.vector.tensor_copy(kk[:, :, :, :], bc(ck[:, :, :], 2, 2))
                nc.vector.tensor_copy(ki4[:, :, :, :], bc(cki[:, :, :], 2, 4)).then_inc(dup, 1)
                for g in range(2 * CB // 4):
                    dve.wait_ge(tr, g + 1)
                    dst = (m.kTs, m.kiTs)[g // 4][:, (g % 4) * 512:(g % 4 + 1) * 512]
                    nc.vector.tensor_copy(dst, m.ps[:, g % 4, :]).then_inc(ev, 1)

            @block.tensor
            def _(pe):
                pe.wait_ge(dup, 1)
                for g in range(2 * CB // 4):
                    if g >= 4:
                        pe.wait_ge(ev, g - 3)
                    for j in range(4):
                        b = (g % 4) * 4 + j
                        src = (kk, ki4)[g // 4][:, b, :, :].rearrange("p a d -> p (a d)")
                        i = nc.tensor.transpose(m.ps[:, g % 4, j * P:(j + 1) * P], src, m.ident[:, :])
                    i.then_inc(tr, 1)


TWO_PI_HI = 6.28125
TWO_PI_MID = 0.0019350051879882812
TWO_PI_LO = 2 * math.pi - TWO_PI_HI - TWO_PI_MID
ROUND = 1.5 * 2.0 ** 23
PI_BELOW = 3.1415925


class ComplexSteps:

    def __init__(self, nc, step):
        self.nc, self.step = nc, step

    def mul(self, out_re, out_im, a_re, a_im, b_re, b_im, tmp, negate_im=False):
        v, step = self.nc.vector, self.step
        step(v.tensor_tensor(tmp, a_re, b_re, ALU.mult))
        step(v.tensor_tensor(out_re, a_im, b_im, ALU.mult))
        step(v.tensor_tensor(out_re, tmp, out_re, ALU.subtract))
        step(v.tensor_tensor(tmp, a_re, b_im, ALU.mult))
        step(v.tensor_tensor(out_im, a_im, b_re, ALU.mult))
        step(v.tensor_tensor(out_im, tmp, out_im, ALU.add))
        if negate_im:
            step(v.tensor_scalar(out_im, out_im, -1.0, None, ALU.mult))


def ssm_parameters(nc, m, A):
    with ExitStack() as ctx:
        sb = lambda name, shape: ctx.enter_context(nc.sbuf_tensor(name, shape, F32))
        rows = sb("sp_rows", [PAIR, 5, P])
        ldt = sb("sp_logdt", [PAIR, 2])
        prm = sb("sp_prm", [P, 5, PAIR])
        cin = sb("sp_c", [P, 2, 2, P])
        cT = sb("sp_cT", [P, 2, PAIR, J])
        b = sb("sp_b", [P, 2, PAIR, J])
        bb = sb("sp_bb", [P, 2, PAIR, J])
        s = sb("sp_small", [P, 24, PAIR])
        pw = sb("sp_powers", [P, 2, PAIR, T + 1])
        idle = m.zT[:, :, :].rearrange("p a n -> p (a n)")
        wt = idle[:, 0:2 * PAIR * P].rearrange("p (c q t j) -> p c q t j", c=2, q=PAIR, t=T)
        tmp = sb("sp_tmp", [P, PAIR * NCH // 2])
        ksb = idle[0:J, 0:G * P].rearrange("j (g n) -> j g n", g=G)
        dd = m.tokqi[0:J, :, :].rearrange("j a n -> j (a n)").rearrange("j (g i) -> j g i", g=G)
        ld, lc = m.sem("sp_loaded"), m.sem("sp_c_loaded")
        ldp, chain, tr, trd = m.sem("sp_dt_rows"), m.sem("sp_dve_chain"), m.sem("sp_transposed"), m.sem("sp_copied")
        a1, a2, a3, th, trig = m.sem("sp_dt"), m.sem("sp_decays"), m.sem("sp_adt"), m.sem("sp_angles"), m.sem("sp_trig")
        wtr, wps, wev, kps, kev, mz, mst, bbr = (m.sem("sp_" + n) for n in (
            "wt_ready", "w_psum", "w_copied", "k_psum", "k_ready", "m_zeroed", "m_stored", "bb_ready"))
        (dt, adt, ang, ang8, dec, n1, r1, sn, cs, n8, rr8, sn8, cs8, num, den, rden, t1, cr, ci, ab1, ab8) = \
            (s[:, j, :] for j in range(21))
        ar, ai, h0r, h0i, ldtT = (prm[:, j, :] for j in range(5))
        with nc.Block() as block:
            @block.sync
            def _(sp):
                for j, a in enumerate((A.ssm_a_re, A.ssm_a_im)):
                    sp.dma_start(rows[:, j, :], a.rearrange("(q g) p -> q (g p)", g=2)).then_inc(ld, 16)
                for j, a in enumerate((A.state_ssm_re, A.state_ssm_im)):
                    sp.dma_start(rows[:, 2 + j, :], a[0].rearrange("(q g) p -> q (g p)", g=2)).then_inc(ld, 16)
                sp.dma_start(ldt[:, :], A.ssm_log_dt.rearrange("(q g) -> q g", g=2)).then_inc(ld, 16)
                for j, a in enumerate((A.ssm_b_re, A.ssm_b_im)):
                    sp.dma_start(b[:, j, :, :], a.rearrange("(q g) p j -> (g p) q j", g=2)).then_inc(lc, 16)
                for j, a in enumerate((A.ssm_c_re, A.ssm_c_im)):
                    for q in range(PAIR):
                        dst = cin[J * (q % 8):J * (q % 8 + 1), j, q // 8, :].rearrange("j (g p) -> j g p", g=2)
                        sp.dma_start(dst, a[2 * q:2 * q + 2].rearrange("g j p -> j g p")).then_inc(lc, 16)
                sp.dma_start(dd[:, :, :].rearrange("j g i -> j (g i)"),
                             A.ssm_d.rearrange("(o n) -> o n", o=1).broadcast_to([J, 512])).then_inc(lc, 16)
                sp.wait_ge(mz, 1)
                sp.wait_ge(kev, 1)
                for p in range(T):
                    sp.dma_start(m.M[J * p:J * (p + 1), :, J * p:P], ksb[:, :, 0:P - J * p]).then_inc(mst, 16)
                sp.wait_ge(mst, 16 * T)

            @block.gpsimd
            def _(pool):
                nc.gpsimd.memset(m.M[:, :, :], 0.0).then_inc(mz, 1)

            @block.tensor
            def _(pe):
                pe.wait_ge(ldp, 1)
                for j in range(5):
                    nc.tensor.transpose(m.ps[:, 0, PAIR * j:PAIR * (j + 1)], rows[:, j, :], m.ident[0:PAIR, 0:PAIR])
                pe.wait_ge(lc, 16 * (3 + 2 * PAIR))
                for j in range(4):
                    i = nc.tensor.transpose(m.ps[:, 1, P * j:P * (j + 1)], cin[:, j // 2, j % 2, :], m.ident[:, :])
                i.then_inc(tr, 1)
                pe.wait_ge(wtr, 1)
                for x in range(8):
                    for y in range(4):
                        n = 4 * x + y
                        i = nc.tensor.transpose(m.ps[:, x, P * y:P * (y + 1)],
                                                wt[:, n // PAIR, n % PAIR, :, :].rearrange("p t j -> p (t j)"), m.ident[:, :])
                    i.then_inc(wps, 1)
                pe.wait_ge(bbr, 1)
                for x in range(4):
                    pe.wait_ge(wev, 2 * x + 2)
                    for g in range(8 * x, 8 * x + 8):
                        h = slice(ST * (g % 2), ST * (g % 2 + 1))
                        y = (g % 8) // 2
                        for c in range(2):
                            i = nc.tensor.matmul(m.ps[0:J, 2 * x + g % 2, P * y:P * (y + 1)], bb[h, c, g // 2, :],
                                                 m.V[h, c, g // 2, 0:T, :].rearrange("p t i -> p (t i)"),
                                                 start=c == 0, stop=c == 1)
                    i.then_inc(kps, 1)

            @block.scalar
            def _(act):
                act.wait_ge(trd, 1)
                nc.scalar.activation(dt, ldtT, ACT.Exp).then_inc(a1, 1)
                act.wait_ge(a3, 1)
                nc.scalar.activation(dec, adt, ACT.Exp)
                nc.scalar.activation(m.r8[:, :], adt, ACT.Exp, scale=float(T)).then_inc(a2, 1)
                act.wait_ge(th, 1)
                nc.scalar.activation(sn, r1, ACT.Sin)
                nc.scalar.activation(cs, ab1, ACT.Sin)
                nc.scalar.activation(sn8, rr8, ACT.Sin)
                nc.scalar.activation(cs8, ab8, ACT.Sin).then_inc(trig, 1)

            @block.vector
            def _(dve):
                step = Chain(dve, chain)
                cx = ComplexSteps(nc, step)
                v = nc.vector
                dve.wait_ge(ld, 80)
                v.tensor_copy(rows[:, 4, :].rearrange("q (g p) -> q g p", g=2), bc(ldt[:, :], 2, ST)).then_inc(ldp, 1)
                dve.wait_ge(tr, 1)
                v.tensor_copy(prm[:, :, :], m.ps[:, 0, 0:5 * PAIR].rearrange("p (a q) -> p a q", a=5)).then_inc(trd, 1)
                step(v.tensor_copy(cT[:, :, :, :].rearrange("p a q j -> p (a q j)"), m.ps[:, 1, :]))
                dve.wait_ge(trd, 1)
                dve.wait_ge(a1, 1)
                v.tensor_tensor(adt, ar, dt, ALU.mult).then_inc(a3, 1)
                step(v.tensor_tensor(ang, ai, dt, ALU.mult))
                step(v.tensor_scalar(ang8, ang, float(T), None, ALU.mult))
                for angle, turns, red, quarter in ((ang, n1, r1, ab1), (ang8, n8, rr8, ab8)):
                    step(v.tensor_scalar(turns, angle, 1.0 / (2 * math.pi), ROUND, ALU.mult, ALU.add))
                    step(v.tensor_scalar(turns, turns, -ROUND, None, ALU.add))
                    step(v.scalar_tensor_tensor(red, turns, -TWO_PI_HI, angle, ALU.mult, ALU.add))
                    step(v.scalar_tensor_tensor(red, turns, -TWO_PI_MID, red, ALU.mult, ALU.add))
                    step(v.scalar_tensor_tensor(red, turns, -TWO_PI_LO, red, ALU.mult, ALU.add))
                    step(v.tensor_scalar(red, red, PI_BELOW, -PI_BELOW, ALU.min, ALU.max))
                    step(v.scalar_tensor_tensor(quarter, red, -1.0, red, ALU.mult, ALU.max))
                    i = v.tensor_scalar(quarter, quarter, -1.0, math.pi / 2, ALU.mult, ALU.add)
                    if angle is ang:
                        step(i)
                i.then_inc(th, 1)
                dve.wait_ge(trig, 1)
                dve.wait_ge(a2, 1)
                pr, pi = pw[:, 0, :, :], pw[:, 1, :, :]
                v.memset(pr[:, :, 0], 1.0)
                v.memset(pi[:, :, 0], 0.0)
                step(v.tensor_tensor(pr[:, :, 1], dec, cs, ALU.mult))
                step(v.tensor_tensor(pi[:, :, 1], dec, sn, ALU.mult))
                for n in (1, 2, 4):
                    tv = tmp[:, 0:PAIR * n].rearrange("p (q n) -> p q n", n=n)
                    cx.mul(pr[:, :, n + 1:2 * n + 1], pi[:, :, n + 1:2 * n + 1], pr[:, :, 1:n + 1], pi[:, :, 1:n + 1],
                           pr[:, :, n:n + 1].broadcast_to([P, PAIR, n]), pi[:, :, n:n + 1].broadcast_to([P, PAIR, n]), tv)
                lr, li = pr[:, :, 1], pi[:, :, 1]
                step(v.tensor_scalar(num, lr, -1.0, None, ALU.add))
                step(v.tensor_tensor(den, ar, ar, ALU.mult))
                step(v.tensor_tensor(t1, ai, ai, ALU.mult))
                step(v.tensor_tensor(den, den, t1, ALU.add))
                step(v.reciprocal(rden, den))
                step(v.tensor_tensor(cr, num, ar, ALU.mult))
                step(v.tensor_tensor(t1, li, ai, ALU.mult))
                step(v.tensor_tensor(cr, cr, t1, ALU.add))
                step(v.tensor_tensor(cr, cr, rden, ALU.mult))
                step(v.tensor_tensor(ci, li, ar, ALU.mult))
                step(v.tensor_tensor(t1, num, ai, ALU.mult))
                step(v.tensor_tensor(ci, ci, t1, ALU.subtract))
                step(v.tensor_tensor(ci, ci, rden, ALU.mult))
                dve.wait_ge(lc, 16 * (3 + 2 * PAIR))
                tv = tmp[:, 0:PAIR * J].rearrange("p (q j) -> p q j", j=J)
                cx.mul(bb[:, 0, :, :], bb[:, 1, :, :], bc(cr, 2, J), bc(ci, 2, J), b[:, 0, :, :], b[:, 1, :, :], tv)
                for q4 in range(4):
                    q = slice(4 * q4, 4 * q4 + 4)
                    tv = tmp[:, 0:4 * T * J].rearrange("p (q t j) -> p q t j", q=4, t=T)
                    rev = pw[:, :, q, T - 1::-1]
                    cx.mul(wt[:, 0, q], wt[:, 1, q], bc(rev[:, 0], 3, J), bc(rev[:, 1], 3, J),
                           bc(bb[:, 0, q, :], 2, T), bc(bb[:, 1, q, :], 2, T), tv)
                v.tensor_copy(s[:, 21, 0:1], wt[:, 0, 0, 0, 0:1]).then_inc(wtr, 1)
                for q4 in range(4):
                    q = slice(4 * q4, 4 * q4 + 4)
                    tv = tmp[:, 0:4 * (T + 1) * J].rearrange("p (q t j) -> p q t j", q=4, t=T + 1)
                    cx.mul(m.V[:, 0, q], m.V[:, 1, q], bc(pr[:, q, :], 3, J), bc(pi[:, q, :], 3, J),
                           bc(cT[:, 0, q, :], 2, T + 1), bc(cT[:, 1, q, :], 2, T + 1), tv, negate_im=True)
                v.tensor_copy(s[:, 22, 0:1], wt[:, 0, 0, 0, 0:1]).then_inc(bbr, 1)
                for x in range(8):
                    dve.wait_ge(wps, x + 1)
                    v.tensor_copy(m.W[:, x // 4, 4 * (x % 4):4 * (x % 4) + 4, :].rearrange("p q n -> p (q n)"),
                                  m.ps[:, x, :]).then_inc(wev, 1)
                tc, ts = m.rot[:, 0, :, :], m.rot[:, 1, :, :]
                v.memset(tc[:, :, 0], 1.0)
                v.memset(ts[:, :, 0], 0.0)
                step(v.tensor_copy(tc[:, :, 1], cs8))
                step(v.tensor_copy(ts[:, :, 1], sn8))
                n = 1
                while n < NCH:
                    tv = tmp[:, 0:PAIR * n].rearrange("p (q n) -> p q n", n=n)
                    cx.mul(tc[:, :, n + 1:2 * n + 1], ts[:, :, n + 1:2 * n + 1], tc[:, :, 1:n + 1], ts[:, :, 1:n + 1],
                           tc[:, :, n:n + 1].broadcast_to([P, PAIR, n]), ts[:, :, n:n + 1].broadcast_to([P, PAIR, n]), tv)
                    n *= 2
                v.tensor_copy(m.rot[:, :, :, S0:COLS], m.rot[:, :, :, 0:COLS - S0])
                step(v.tensor_copy(m.decay[:, :, :], bc(m.r8[:, :], 2, COLS)))
                v.memset(m.decay[:, :, 0], 0.0)
                v.memset(m.decay[:, :, S0], 0.0)
                v.tensor_copy(m.h0[:, :, :], prm[:, 2:4, :])
                i = v.tensor_tensor(dd[:, :, :], dd[:, :, :], bc(m.ident[0:J, 0:J], 1, G), ALU.mult)
                step(i)
                for x in range(8):
                    dve.wait_ge(kps, x // 2 + 1)
                    g0 = 8 * (x // 2) + x % 2
                    i = v.tensor_copy(ksb[:, g0:min(g0 + 8, G):2, :], m.ps[0:J, x, :].rearrange("j (g n) -> j g n", n=P))
                step(i)
                v.tensor_tensor(ksb[:, :, 0:J], ksb[:, :, 0:J], dd[:, :, :], ALU.add).then_inc(kev, 1)


def ssm_scan(nc, m, A, O):
    GQ, PQ = G // 4, PAIR // 4
    with ExitStack() as ctx:
        sb = lambda name, shape: ctx.enter_context(nc.sbuf_tensor(name, shape, F32))
        us = sb("sc_us", [SCH, 2, GQ, T, J])
        uT = sb("sc_uT", [P, 2, GQ, COLS])
        z = sb("sc_z", [P, 4, PQ, COLS])
        hh = sb("sc_h", [P, 2, 2, PQ, COLS])
        y = [m.u[:, GQ * q:GQ * (q + 1), :, :].rearrange("c g t i -> c (g t i)").rearrange("c (t n) -> c t n", t=T)
             for q in range(4)]
        ys = [us[:, q % 2, :, :, :].rearrange("c g t i -> c (g t i)").rearrange("c (t n) -> c t n", t=T)
              for q in range(4)]
        last = sb("sc_last", [P, 4, PAIR])
        lastT = m.tokqi[0:PAIR, :, :].rearrange("q a n -> q (a n)").rearrange("q (a n) -> q a n", a=4)
        usd, usl = m.sem("sc_us_stored"), [m.sem(f"sc_us_loaded{i}") for i in range(2)]
        up, ue, zp, chain, hr, yp, ye, ypt, zte, fin, fp, fe, fst, zero = (m.sem("sc_" + n) for n in (
            "u_transposed", "u_copied", "z_psum", "dve_chain", "h_ready", "y_psum", "y_gelu", "y_transposed",
            "zT_copied", "last_ready", "last_transposed", "last_copied", "last_stored", "zeroed"))
        zc = m.sem("sc_z_copied")
        with nc.Block() as block:
            @block.sync
            def _(sp):
                sp.dma_start(m.us_dram, m.us[:, :]).then_inc(usd, 16)
                sp.wait_ge(usd, 16)
                for q in range(4):
                    if q >= 2:
                        sp.wait_ge(ypt, q - 1)
                    for g in range(GQ):
                        c = q * P + g * J
                        sp.dma_start(us[:, q % 2, g, :, :], m.us_dram.rearrange("(c s) n -> c s n", s=T)[:, :, c:c + J]) \
                            .then_inc(usl[q % 2], 16)
                sp.wait_ge(fe, 1)
                for j, o in enumerate((O.ssm_re_prompt, O.ssm_im_prompt, O.ssm_re_sample, O.ssm_im_sample)):
                    sp.dma_start(o[0, 0].rearrange("(q g) p -> q (g p)", g=2), lastT[:, j, :]).then_inc(fst, 16)
                sp.wait_ge(fst, 64)

            @block.tensor
            def _(pe):
                pe.wait_ge(zero, 1)
                for q in range(4):
                    pe.wait_ge(usl[q % 2], 16 * GQ * (q // 2 + 1))
                    if q:
                        pe.wait_ge(ye, q)
                        pe.wait_ge(zte, q)
                    for g in range(GQ):
                        src = m.u[:, GQ * q + g, :, :].rearrange("c t j -> c (t j)")
                        nc.tensor.transpose(m.ps[:, g // 4, (g % 4) * P:(g % 4 + 1) * P], src, m.ident[:, :])
                    for g in range(GQ):
                        i = nc.tensor.transpose(m.ps[:, 2, g * SCH:(g + 1) * SCH], us[:, q % 2, g, :, :].rearrange("c t j -> c (t j)"),
                                                m.ident[0:SCH, 0:SCH])
                    i.then_inc(up, 1)
                    pe.wait_ge(ue, q + 1)
                    for c in range(2):
                        for n in range(PQ):
                            for g in range(2):
                                i = nc.tensor.matmul(
                                    m.ps[ST * g:ST * (g + 1), 4 + 2 * c + n // 2, (n % 2) * COLS:(n % 2 + 1) * COLS],
                                    m.W[:, c, PQ * q + n, ST * g:ST * (g + 1)], uT[:, q % 2, 2 * n + g, :], start=True, stop=True)
                    i.then_inc(zp, 1)
                    pe.wait_ge(hr, q + 1)
                    for smp in range(2):
                        lo, rows, bank = ((0, NCH, 0), (S0, SCH, 2))[smp]
                        for g in range(GQ):
                            h = slice(ST * (g % 2), ST * (g % 2 + 1))
                            out = m.ps[0:rows, bank + g % 2, (g // 2) * P:(g // 2 + 1) * P]
                            nc.tensor.matmul(out, uT[:, q % 2, g, lo + 1:lo + 1 + rows], m.M[:, GQ * q + g, :],
                                             start=True, stop=False)
                            for c in range(2):
                                i = nc.tensor.matmul(out, hh[h, q % 2, c, g // 2, lo:lo + rows],
                                                     m.V[h, c, PQ * q + g // 2, 1:T + 1, :].rearrange("p t i -> p (t i)"),
                                                     start=False, stop=c == 1)
                    i.then_inc(yp, 1)
                    pe.wait_ge(ye, q + 1)
                    for t in range(T):
                        nc.tensor.transpose(m.ps[:, 4 + t // 4, (t % 4) * P:(t % 4 + 1) * P], y[q][:, t, :], m.ident[:, :])
                    for t in range(T):
                        i = nc.tensor.transpose(m.ps[:, 6, t * SCH:(t + 1) * SCH], ys[q][:, t, :], m.ident[0:SCH, 0:SCH])
                    i.then_inc(ypt, 1)
                pe.wait_ge(fin, 1)
                for j in range(4):
                    i = nc.tensor.transpose(m.ps[0:PAIR, 7, j * P:(j + 1) * P], last[:, j, :], m.ident[:, :])
                i.then_inc(fp, 1)

            @block.scalar
            def _(act):
                for q in range(4):
                    act.wait_ge(yp, q + 1)
                    for x in range(2):
                        src = lambda b, r: m.ps[0:r, b + x, :].rearrange("c (g t i) -> c t g i", g=4, t=T)
                        dst = lambda o: o.rearrange("c t (g i) -> c t g i", i=J)[:, :, x:GQ:2, :]
                        nc.scalar.activation(dst(y[q]), src(0, P), ACT.Gelu_apprx_tanh)
                        i = nc.scalar.activation(dst(ys[q]), src(2, SCH), ACT.Gelu_apprx_tanh)
                    i.then_inc(ye, 1)

            @block.vector
            def _(dve):
                step = Chain(dve, chain)
                v = nc.vector
                for b in range(2):
                    v.memset(uT[:, b, :, 0], 0.0)
                    i = v.memset(uT[:, b, :, S0], 0.0)
                i.then_inc(zero, 1)
                for q in range(4):
                    dve.wait_ge(up, q + 1)
                    for x in range(2):
                        v.tensor_copy(uT[:, q % 2, 4 * x:4 * x + 4, 1:NCH + 1], m.ps[:, x, :].rearrange("p (g c) -> p g c", g=4))
                    v.tensor_copy(uT[:, q % 2, :, S0 + 1:COLS],
                                  m.ps[:, 2, 0:GQ * SCH].rearrange("p (g c) -> p g c", g=GQ)).then_inc(ue, 1)
                    dve.wait_ge(zp, q + 1)
                    zr, zi, tr, ti = (z[:, j, :, :] for j in range(4))
                    for c in range(2):
                        step(v.tensor_copy(z[:, c, :, :].rearrange("p (a b) c -> p a (b c)", a=2),
                                           m.ps[:, 4 + 2 * c:6 + 2 * c, 0:2 * COLS]))
                    qs = slice(PQ * q, PQ * (q + 1))
                    step(v.tensor_copy(z[:, 0:2, :, S0], m.h0[:, :, qs]))
                    rc, rs = m.rot[:, 0, qs, :], m.rot[:, 1, qs, :]
                    step(v.tensor_tensor(tr, zr, rc, ALU.mult))
                    step(v.tensor_tensor(ti, zi, rs, ALU.mult))
                    step(v.tensor_tensor(tr, tr, ti, ALU.add))
                    step(v.tensor_tensor(ti, zi, rc, ALU.mult))
                    step(v.tensor_tensor(zr, zr, rs, ALU.mult))
                    step(v.tensor_tensor(ti, ti, zr, ALU.subtract))
                    flat = lambda a: a.rearrange("p q c -> p (q c)")
                    dec = flat(m.decay[:, qs, :])
                    step(v.tensor_tensor_scan(flat(zr), dec, flat(tr), 0.0, ALU.mult, ALU.add))
                    step(v.tensor_tensor_scan(flat(zi), dec, flat(ti), 0.0, ALU.mult, ALU.add))
                    hre, him = hh[:, q % 2, 0, :, :], hh[:, q % 2, 1, :, :]
                    step(v.tensor_tensor(hre, zr, rc, ALU.mult))
                    step(v.tensor_tensor(ti, zi, rs, ALU.mult))
                    step(v.tensor_tensor(hre, hre, ti, ALU.subtract))
                    step(v.tensor_tensor(him, zi, rc, ALU.mult))
                    step(v.tensor_tensor(ti, zr, rs, ALU.mult))
                    step(v.tensor_tensor(him, him, ti, ALU.add))
                    v.tensor_copy(last[:, 0:2, qs], hh[:, q % 2, :, :, NCH])
                    v.tensor_copy(last[:, 2:4, qs], hh[:, q % 2, :, :, COLS - 1]).then_inc(hr, 1)
                    dve.wait_ge(ypt, q + 1)
                    for x in range(2):
                        v.tensor_copy(m.zT[:, q, 0:SEQ].rearrange("p (c t) -> p t c", t=T)[:, 4 * x:4 * x + 4, :],
                                      m.ps[:, 4 + x, :].rearrange("p (t c) -> p t c", t=4))
                    v.tensor_copy(m.zT[:, q, SEQ:NT].rearrange("p (c t) -> p t c", t=T),
                                  m.ps[:, 6, 0:T * SCH].rearrange("p (t c) -> p t c", t=T)).then_inc(zte, 1)
                dve.wait_ge(hr, 4)
                v.tensor_copy(last[:, :, 0:1], last[:, :, 0:1]).then_inc(fin, 1)
                dve.wait_ge(fp, 1)
                v.tensor_copy(lastT[:, :, :].rearrange("q a n -> q (a n)"), m.ps[0:PAIR, 7, :]).then_inc(fe, 1)


SEL = range(2, PT)
SC_COL = {t: P * sum(j + 1 for j in range(2, t)) for t in SEL}
SC_SAMPLE = P * sum(j + 1 for j in SEL)
SC_W = SC_SAMPLE + PAST + DEC
MK_COL = {t: P * sum(j + 1 for j in range(t)) for t in range(PT)}
MK_SAMPLE = P * sum(j + 1 for j in range(PT))
MK_W = MK_SAMPLE + PAST + DEC


def keys_of(t):
    return (P * (t + 1), MK_COL[t]) if t < PT else (PAST + DEC, MK_SAMPLE)


def pieces(n, size=1024):
    return [(k, min(size, n - k)) for k in range(0, n, size)]


def index_scores(nc, m):
    units = [(t, k, w) for t in SEL for k, w in pieces(P * (t + 1))] + [(PT, k, w) for k, w in pieces(PAST + DEC)]
    with ExitStack() as ctx:
        relu = ctx.enter_context(nc.sbuf_tensor("ix_relu", [P, 4, 1024], F32))
        ps, free, rl, acc, chain = (m.sem("ix_" + n) for n in ("psum", "psum_free", "relu", "added", "dve_chain"))
        with nc.Block() as block:
            @block.tensor
            def _(pe):
                n = 0
                for t, k0, w in units:
                    r = rows_of(t)
                    src = m.kiT if t < PT else m.kiTs
                    for h in range(IH):
                        q = slice(ID * (h % 4), ID * (h % 4 + 1))
                        if n >= 4:
                            pe.wait_ge(rl, n - 3)
                        for c, (k, x) in enumerate(pieces(w, 512)):
                            i = nc.tensor.matmul(m.ps[0:r, 2 * (h % 4) + c, 0:x], m.qiT[q, h // 4, t * P:t * P + r],
                                                 src[q, k0 + k:k0 + k + x], start=True, stop=True)
                        i.then_inc(ps, 1)
                        n += 1

            @block.scalar
            def _(act):
                n = 0
                for t, k0, w in units:
                    r = rows_of(t)
                    for h in range(IH):
                        act.wait_ge(ps, n + 1)
                        if n >= 4:
                            act.wait_ge(acc, n - 3)
                        src = m.ps[0:r, 2 * (h % 4):2 * (h % 4) + 2, :].rearrange("p b n -> p (b n)")
                        nc.scalar.activation(relu[0:r, n % 4, 0:w], src[:, 0:w], ACT.Relu).then_inc(rl, 1)
                        n += 1

            @block.vector
            def _(dve):
                step = Chain(dve, chain)
                n = 0
                for t, k0, w in units:
                    r = rows_of(t)
                    c = (SC_COL[t] if t < PT else SC_SAMPLE) + k0
                    sc = m.sc[0:r, c:c + w]
                    for h in range(IH):
                        dve.wait_ge(rl, n + 1)
                        wt = m.wi[0:r, t, h:h + 1]
                        if h == 0:
                            i = nc.vector.tensor_scalar(sc, relu[0:r, n % 4, 0:w], wt, None, ALU.mult)
                        else:
                            i = nc.vector.scalar_tensor_tensor(sc, relu[0:r, n % 4, 0:w], wt, sc, ALU.mult, ALU.add)
                        i.then_inc(acc, 1)
                        dve.wait_ge(acc, n + 1)
                        n += 1
                    if t < PT:
                        nc.vector.memset(m.sc[0:DEC, c + w - DEC:c + w], NEG)


def select_keys(nc, m):
    NL = len(SEL) + 1
    lists = [(P, SC_COL[t], P * (t + 1), MK_COL[t]) for t in SEL] + [(DEC, SC_SAMPLE, PAST + DEC, MK_SAMPLE)]
    with ExitStack() as ctx:
        sb = lambda name, shape, dt=F32: ctx.enter_context(nc.sbuf_tensor(name, shape, dt))
        thr = sb("tk_thr", [P, NL], I32)
        cand = sb("tk_cand", [P, NL], I32)
        neg = sb("tk_neg", [P, NL])
        negi = sb("tk_negi", [P, NL], I32)
        take = sb("tk_take", [P, NL], I32)
        cnt = sb("tk_cnt", [P, NL])
        bit = sb("tk_bit", [P, 1], I32)
        hits = sb("tk_hits", [P, PAST + DEC], BF16)
        eq = sb("tk_eq", [P, PAST + DEC])
        pre = sb("tk_pre", [P, PAST + DEC])
        chain, loop, done, dup = m.sem("tk_chain"), m.sem("tk_loop"), m.sem("tk_mask_ready"), m.sem("tk_mask_copied")
        with nc.Block() as block:
            @block.vector
            def _(dve):
                step = Chain(dve, chain)
                v = nc.vector

                def count(j, scalar):
                    r, c, w, _ = lists[j]
                    return v.tensor_scalar(hits[0:r, 0:w], m.sc[0:r, c:c + w], scalar, 0.0, ALU.is_ge, ALU.add,
                                           accum_out=cnt[0:r, j:j + 1])

                step(v.memset(cnt[:, :], 0.0))
                for j in range(NL):
                    step(count(j, 0.0))
                step(v.tensor_scalar(neg[:, :], cnt[:, :], TOPK - 0.5, None, ALU.is_lt))
                step(v.tensor_copy(negi[:, :], neg[:, :]))
                step(v.tensor_scalar(thr[:, :], negi[:, :], 31, None, ALU.logical_shift_left))
                step(v.memset(bit[:, :], 1 << 30))
                STEPS = NL + 4
                with dve.Fori(0, 31) as i:
                    at = STEPS * i
                    v.tensor_tensor(cand[:, :], thr[:, :], bit[:, :].broadcast_to([P, NL]), ALU.bitwise_or).then_inc(loop, 1)
                    dve.wait_ge(loop, at + 1)
                    for j in range(NL):
                        r = lists[j][0]
                        count(j, cand[0:r, j:j + 1].bitcast(F32)).then_inc(loop, 1)
                        dve.wait_ge(loop, at + 2 + j)
                    v.scalar_tensor_tensor(take[:, :], cnt[:, :], TOPK - 0.5, neg[:, :], ALU.is_ge, ALU.not_equal).then_inc(loop, 1)
                    dve.wait_ge(loop, at + STEPS - 2)
                    v.tensor_scalar(bit[:, :], bit[:, :], 1, None, ALU.logical_shift_right).then_inc(loop, 1)
                    v.copy_predicated(thr[:, :], take[:, :], cand[:, :]).then_inc(loop, 1)
                    dve.wait_ge(loop, at + STEPS)
                step(v.tensor_tensor(thr[:, :], thr[:, :], negi[:, :], ALU.add))
                for j, (r, c, w, mc) in enumerate(lists):
                    sc, mk, tf = m.sc[0:r, c:c + w], m.mask[0:r, mc:mc + w], thr[0:r, j:j + 1].bitcast(F32)
                    e, p, need = eq[0:r, 0:w], pre[0:r, 0:w], cnt[0:r, j:j + 1]
                    step(v.tensor_scalar(mk, sc, tf, 0.0, ALU.is_gt, ALU.add, accum_out=need))
                    step(v.tensor_scalar(need, need, -1.0, float(TOPK), ALU.mult, ALU.add))
                    step(v.tensor_scalar(e, sc, tf, None, ALU.is_equal))
                    step(v.tensor_tensor_scan(p, m.ones[0:r, 0:1].broadcast_to([r, w]), e, 0.0, ALU.mult, ALU.add))
                    step(v.scalar_tensor_tensor(e, p, need, e, ALU.is_le, ALU.mult))
                    step(v.scalar_tensor_tensor(mk, e, -1.0, mk, ALU.add, ALU.add))
                    step(v.tensor_scalar(mk, mk, -NEG, None, ALU.mult))
                step(v.memset(m.mask[:, 0:3 * P], 0.0))
                for t in range(2):
                    c = MK_COL[t] + P * (t + 1)
                    i = v.memset(m.mask[0:DEC, c - DEC:c], NEG)
                    if t:
                        i.then_inc(done, 1)
                    else:
                        step(i)

            @block.sync
            def _(sp):
                sp.wait_ge(done, 1)
                sp.dma_start(m.mask[DEC:P, MK_SAMPLE:MK_W], m.mask[0:DEC, MK_SAMPLE:MK_W]).then_inc(dup, 16)
                sp.wait_ge(dup, 16)


def attention(nc, m):
    units = [(t, h) for t in range(PT) for h in range(H)] + [(PT, h) for h in range(H // 2)]
    NU = len(units)
    chunks = [pieces(keys_of(t)[0]) for t, _ in units]
    blocks = [pieces(keys_of(t)[0], P) for t, _ in units]
    groups = [[b[i:i + 4] for i in range(0, len(b), 4)] for b in blocks]
    c_at = [sum(map(len, chunks[:u])) for u in range(NU + 1)]
    g_at = [sum(map(len, groups[:u])) for u in range(NU + 1)]
    SCALE = HD ** -0.5
    with ExitStack() as ctx:
        sb = lambda name, shape, dt=F32: ctx.enter_context(nc.sbuf_tensor(name, shape, dt))
        qb = sb("at_qb", [P, 4, P])
        s = sb("at_s", [P, 2, PAST + DEC])
        pT = sb("at_pT", [P, 2, CB + 1, P])
        mx = sb("at_mx", [P, 4, 4])
        nb = sb("at_nb", [P, NU])
        sm = sb("at_sum", [P, NU])
        rs = sb("at_rsum", [P, NU])
        o = sb("at_o", [P, 2, 512])
        os_ = sb("at_os", [P, 4, HD])
        qz, sp_, sd, mxr, nbr, er, tp, te, pv, oc, rr, otp, ote, osr, osm = (m.sem("at_" + n) for n in (
            "qb_ready", "s_psum", "s_masked", "max_ready", "bias_ready", "exp_ready", "p_transposed", "p_copied",
            "pv_psum", "o_copied", "recip_ready", "o_transposed", "oT_copied", "os_ready", "os_moved"))
        with nc.Block() as block:
            @block.tensor
            def _(pe):
                def scores(u):
                    t, h = units[u]
                    r = rows_of(t)
                    for c, (k0, w) in enumerate(chunks[u]):
                        n = c_at[u] + c
                        if n >= 2:
                            pe.wait_ge(sd, n - 1)
                        for b, (k, x) in enumerate(pieces(w, 512)):
                            out = m.ps[:, 2 * (n % 2) + b, 0:x]
                            if t < PT:
                                half = slice(HD * (h % 2), HD * (h % 2 + 1))
                                i = nc.tensor.matmul(out, m.qT[half, h // 2, t * P:(t + 1) * P],
                                                     m.kT[half, k0 + k:k0 + k + x], start=True, stop=True)
                            else:
                                i = nc.tensor.matmul(out, qb[:, h, :], m.kTs[:, k0 + k:k0 + k + x], start=True, stop=True)
                        i.then_inc(sp_, 1)

                def transposes(u):
                    pe.wait_ge(er, u + 1)
                    for g, bs in enumerate(groups[u]):
                        n = g_at[u] + g
                        if n >= 2:
                            pe.wait_ge(te, n - 1)
                        for j, (k, x) in enumerate(bs):
                            i = nc.tensor.transpose(m.ps[0:x, 4 + n % 2, j * P:(j + 1) * P], s[:, u % 2, k:k + x], m.ident[:, :])
                        i.then_inc(tp, 1)

                def values(u):
                    t, h = units[u]
                    pe.wait_ge(te, g_at[u + 1])
                    if h == 0 and t:
                        pe.wait_ge(oc, t)
                    src = m.v if t < PT else m.vs
                    for b, (k, x) in enumerate(blocks[u]):
                        i = nc.tensor.matmul(m.ps[:, 6, h * HD:(h + 1) * HD], pT[0:x, u % 2, b, :], src[0:x, b, :],
                                             start=b == 0, stop=b == len(blocks[u]) - 1)
                    i.then_inc(pv, 1)

                def output(t):
                    pe.wait_ge(oc, t + 1)
                    r = rows_of(t)
                    if t == PT:
                        pe.wait_ge(osm, 32)
                    if t:
                        pe.wait_ge(ote, t)
                    for j in range(4):
                        i = nc.tensor.transpose(m.ps[:, 7, j * P:j * P + r], o[0:r, t % 2, j * P:(j + 1) * P], m.ident[0:r, 0:r])
                    i.then_inc(otp, 1)

                pe.wait_ge(qz, 4)
                scores(0)
                for u in range(NU + 1):
                    if u + 1 < NU:
                        scores(u + 1)
                    if u < NU:
                        transposes(u)
                    if u:
                        values(u - 1)
                        t, h = units[u - 1]
                        if h == 1 and t:
                            output(t - 1)
                output(PT)

            @block.vector
            def _(dve):
                v = nc.vector

                def normalise(t):
                    first = t * H
                    n = H if t < PT else H // 2
                    dve.wait_ge(pv, first + n)
                    v.reciprocal(rs[:, first:first + n], sm[:, first:first + n]).then_inc(rr, 1)
                    dve.wait_ge(rr, t + 1)
                    if t >= 2:
                        dve.wait_ge(otp, t - 1)
                    dst = o[:, t % 2, :].rearrange("p (h d) -> p h d", d=HD) if t < PT else os_[:, :, :]
                    v.tensor_tensor(dst, m.ps[:, 6, 0:n * HD].rearrange("p (h d) -> p h d", d=HD),
                                    bc(rs[:, first:first + n], 2, HD), ALU.mult).then_inc(oc, 1)

                def place(t):
                    dve.wait_ge(otp, t + 1)
                    r = rows_of(t)
                    v.tensor_copy(m.attnT[:, :, t * P:t * P + r],
                                  m.ps[:, 7, :].rearrange("p (j t) -> p j t", t=P)[:, :, 0:r]).then_inc(ote, 1)

                v.memset(qb[:, :, :], 0.0).then_inc(qz, 1)
                dve.wait_ge(qz, 1)
                for x in range(2):
                    half = slice(HD * x, HD * (x + 1))
                    v.tensor_copy(qb[half, :, DEC * x:DEC * (x + 1)], m.qT[half, :, SEQ:NT]).then_inc(qz, 1)
                v.memset(sm[:, :], 0.0).then_inc(qz, 1)
                for u, (t, h) in enumerate(units):
                    mc = keys_of(t)[1]
                    if u >= 2:
                        dve.wait_ge(tp, g_at[u - 1])
                    for c, (k0, w) in enumerate(chunks[u]):
                        n = c_at[u] + c
                        dve.wait_ge(sp_, n + 1)
                        src = m.ps[:, 2 * (n % 2):2 * (n % 2) + 2, :].rearrange("p b n -> p (b n)")[:, 0:w]
                        v.tensor_tensor_reduce(out=s[:, u % 2, k0:k0 + w], in0=src, in1=m.mask[:, mc + k0:mc + k0 + w],
                                               scale=1.0, scalar=-3.0e38, op0=ALU.add, op1=ALU.max,
                                               accum_out=mx[:, u % 4, c:c + 1]).then_inc(sd, 1)
                    dve.wait_ge(sd, c_at[u + 1])
                    v.tensor_reduce(mx[:, u % 4, 3:4], mx[:, u % 4, 0:len(chunks[u])], AX.X, ALU.max).then_inc(mxr, 1)
                    dve.wait_ge(mxr, u + 1)
                    v.tensor_scalar(nb[:, u:u + 1], mx[:, u % 4, 3:4], -SCALE, None, ALU.mult).then_inc(nbr, 1)
                    if h == 1 and t:
                        normalise(t - 1)
                    if h == 3 and t:
                        place(t - 1)
                normalise(PT)
                place(PT)

            @block.scalar
            def _(act):
                def copies(u):
                    for g, bs in enumerate(groups[u]):
                        n = g_at[u] + g
                        act.wait_ge(tp, n + 1)
                        if u >= 2 and g == 0:
                            act.wait_ge(pv, u - 1)
                        x = bs[-1][1]
                        if x == P:
                            i = nc.scalar.copy(pT[:, u % 2, 4 * g:4 * g + len(bs), :].rearrange("p b n -> p (b n)"),
                                               m.ps[:, 4 + n % 2, 0:len(bs) * P])
                        else:
                            i = nc.scalar.copy(pT[0:x, u % 2, 4 * g, :], m.ps[0:x, 4 + n % 2, 0:P])
                        i.then_inc(te, 1)

                for u, (t, h) in enumerate(units):
                    n = keys_of(t)[0]
                    act.wait_ge(nbr, u + 1)
                    nc.scalar.activation(s[:, u % 2, 0:n], s[:, u % 2, 0:n], ACT.Exp, bias=nb[:, u:u + 1], scale=SCALE,
                                         accum_out=sm[:, u:u + 1]).then_inc(er, 1)
                    if u:
                        copies(u - 1)
                copies(NU - 1)

            @block.sync
            def _(sp):
                sp.wait_ge(oc, TILES)
                dst = o[0:DEC, PT % 2, :].rearrange("p (j x d) -> p j x d", j=4, x=2)
                for x in range(2):
                    sp.dma_start(dst[:, :, x, :], os_[DEC * x:DEC * (x + 1), :, :]).then_inc(osm, 16)
                sp.wait_ge(osm, 32)


def load_q(nc, m):
    ld = m.sem("q_reloaded")
    with nc.Block() as block:
        @block.sync
        def _(sp):
            sp.dma_start(m.qT[:, :, :], m.q_dram).then_inc(ld, 16)
            sp.wait_ge(ld, 16)


SPANS = ((0, 512), (512, 512), (1024, DEC))


def merge(nc, m, A):
    GB, AT, GA, GG, GV = range(5)
    NB = 3
    units = [(c, lo, n) for c in range(KD) for lo, n in SPANS]
    with ExitStack() as ctx:
        sb = lambda name, shape: ctx.enter_context(nc.sbuf_tensor(name, shape, F32))
        w = sb("mg_w", [P, NB, 28, P])
        sg = sb("mg_sig", [P, 2, 3, 512])
        ob = sb("mg_ob", [P, 2, 512])
        tt = sb("mg_t", [P, 2, 512])
        wl = [m.sem(f"mg_w_loaded{i}") for i in range(NB)]
        ps, sgr, dv = m.sem("mg_psum"), m.sem("mg_sigmoids"), m.sem("mg_dve_chain")
        kp = lambda a: a.rearrange("(k p) n -> p k n", p=P)
        parts = ((GB, 0, KD, kp(A.w_in), OFF_GB, m.hT), (AT, 8, 4, kp(A.w_attn_out), 0, m.attnT),
                 (GA, 12, KD, kp(A.w_in), OFF_GA, m.hT), (GG, 20, 4, kp(A.w_glu), D, m.zT),
                 (GV, 24, 4, kp(A.w_glu), 0, m.zT))
        with nc.Block() as block:
            @block.sync
            def _(sp):
                for c in range(KD):
                    if c >= NB:
                        sp.wait_ge(ps, 5 * 3 * (c - NB + 1))
                    for _, at, n, src, off, _ in parts:
                        sp.dma_start(w[:, c % NB, at:at + n, :], src[:, :, off + c * P:off + (c + 1) * P]).then_inc(wl[c % NB], 16)

            @block.tensor
            def _(pe):
                for u, (c, lo, n) in enumerate(units):
                    if u % 3 == 0:
                        pe.wait_ge(wl[c % NB], 80 * (c // NB + 1))
                    for j, at, nk, _, _, rhs in parts:
                        seq = 5 * u + j
                        if seq >= 8:
                            pu, pj = divmod(seq - 8, 5)
                            if pj in (AT, GV):
                                pe.wait_ge(dv, 4 * pu + (1 if pj == AT else 2))
                            else:
                                pe.wait_ge(sgr, 3 * pu + {GB: 1, GA: 2, GG: 3}[pj])
                        for k in range(nk):
                            i = nc.tensor.matmul(m.ps[:, seq % 8, 0:n], w[:, c % NB, at + k, :], rhs[:, k, lo:lo + n],
                                                 start=k == 0, stop=k == nk - 1)
                        i.then_inc(ps, 1)

            @block.scalar
            def _(act):
                for u, (c, lo, n) in enumerate(units):
                    if u >= 2:
                        act.wait_ge(dv, 4 * (u - 1))
                    for x, j in enumerate((GB, GA, GG)):
                        act.wait_ge(ps, 5 * u + j + 1)
                        nc.scalar.activation(sg[:, u % 2, x, 0:n], m.ps[:, (5 * u + j) % 8, 0:n], ACT.Sigmoid).then_inc(sgr, 1)

            @block.vector
            def _(dve):
                step = Chain(dve, dv)
                v = nc.vector
                for u, (c, lo, n) in enumerate(units):
                    bank = lambda j: m.ps[:, (5 * u + j) % 8, 0:n]
                    o, t, sgs = ob[:, u % 2, 0:n], tt[:, u % 2, 0:n], [sg[:, u % 2, x, 0:n] for x in range(3)]
                    dve.wait_ge(ps, 5 * u + AT + 1)
                    dve.wait_ge(sgr, 3 * u + 1)
                    step(v.tensor_tensor(o, bank(AT), sgs[0], ALU.mult))
                    dve.wait_ge(ps, 5 * u + GV + 1)
                    dve.wait_ge(sgr, 3 * u + 3)
                    step(v.tensor_tensor(t, bank(GV), sgs[2], ALU.mult))
                    step(v.tensor_tensor(t, t, sgs[1], ALU.mult))
                    step(v.tensor_tensor(m.mergedT[:, c, lo:lo + n], t, o, ALU.add))


def load_mod_rows(nc, m, dst, first, name):
    ld = m.sem(name)
    with nc.Block() as block:
        @block.sync
        def _(sp):
            for i, j in enumerate(first):
                for s in range(2):
                    sp.dma_start(dst[:, i, s, :], m.mod_dram[s:s + 1, j * D:(j + 1) * D].broadcast_to([P, D])).then_inc(ld, 16)
            sp.wait_ge(ld, 32 * len(first))


def output_projection(nc, m, A):
    with ExitStack() as ctx:
        sb = lambda name, shape: ctx.enter_context(nc.sbuf_tensor(name, shape, F32))
        x = sb("op_x", [P, 2, D])
        xa = sb("op_xa", [P, 2, D])
        h2 = sb("op_h2", [P, 2, D])
        sq = sb("op_sq", [P, D])
        h2T = sb("op_h2T", [P, 2, KD, P])
        wr = sb("op_wr", [P, KD, NG + NE])
        st = sb("op_st", [P, TILES, 4])
        wl, xl = m.sem("op_w_loaded"), [m.sem(f"op_x_loaded{i}") for i in range(2)]
        x1s, h2s = ([m.sem(f"op_{n}_stored{i}") for i in range(2)] for n in ("x1", "h2"))
        pm, dm, pa, sqr, msr, rtr, rcp, hm, hr, tp, te, rp, re, one = (m.sem("op_" + n) for n in (
            "psum", "gated", "x1_ready", "squared", "mean", "root", "recip", "h2_scaled", "h2_ready",
            "transposed", "h2T_ready", "router_psum", "logits", "scale_ready"))
        g1 = m.modA[:, 0, :, :]
        sc2 = m.modA[:, 1, :, :]
        sh2 = m.modB[:, 0, :, :]
        with nc.Block() as block:
            @block.sync
            def _(sp):
                wo = A.w_out.rearrange("(k p) n -> p k n", p=P)
                for k in range(KD):
                    sp.dma_start(m.wout[:, k, :], wo[:, k, :]).then_inc(wl, 16)
                sp.dma_start(wr[:, :, 0:NG], A.w_route_group.rearrange("(k p) n -> p k n", p=P)).then_inc(wl, 16)
                sp.dma_start(wr[:, :, NG:], A.w_route_expert.rearrange("(k p) n -> p k n", p=P)).then_inc(wl, 16)
                for t in range(TILES + 1):
                    if t < TILES:
                        r = rows_of(t)
                        if t >= 2:
                            sp.wait_ge(pa, t - 1)
                        src = A.x_prompt[0, t * P:(t + 1) * P, :] if t < PT else A.x_sample[0, :, :]
                        sp.dma_start(x[0:r, t % 2, :], src).then_inc(xl[t % 2], 16)
                    if t:
                        u = t - 1
                        r = rows_of(u)
                        sp.wait_ge(pa, u + 1)
                        sp.dma_start(m.x1_dram[u * P:u * P + r, :], xa[0:r, u % 2, :]).then_inc(x1s[u % 2], 16)
                        sp.wait_ge(hr, u + 1)
                        sp.dma_start(m.h2_dram[u * P:u * P + r, :], h2[0:r, u % 2, :]).then_inc(h2s[u % 2], 16)
                for i in range(2):
                    sp.wait_ge(x1s[i], 16 * ((TILES + 1 - i) // 2))
                    sp.wait_ge(h2s[i], 16 * ((TILES + 1 - i) // 2))

            @block.tensor
            def _(pe):
                def main(t):
                    r = rows_of(t)
                    if t >= 2:
                        pe.wait_ge(dm, t - 1)
                    for n in range(2):
                        for k in range(KD):
                            i = nc.tensor.matmul(m.ps[0:r, 2 * (t % 2) + n, :], m.mergedT[:, k, t * P:t * P + r],
                                                 m.wout[:, k, n * 512:(n + 1) * 512], start=k == 0, stop=k == KD - 1)
                    i.then_inc(pm, 1)

                def transposes(t):
                    r = rows_of(t)
                    pe.wait_ge(hr, t + 1)
                    if t:
                        pe.wait_ge(te, t)
                    for k in range(KD):
                        i = nc.tensor.transpose(m.ps[:, 4 + k // 4, (k % 4) * P:(k % 4) * P + r],
                                                h2[0:r, t % 2, k * P:(k + 1) * P], m.ident[0:r, 0:r])
                    i.then_inc(tp, 1)

                def route(t):
                    r = rows_of(t)
                    pe.wait_ge(te, t + 1)
                    if t >= 2:
                        pe.wait_ge(re, t - 1)
                    for k in range(KD):
                        i = nc.tensor.matmul(m.ps[0:r, 6 + t % 2, 0:NG + NE], h2T[:, t % 2, k, 0:r], wr[:, k, :],
                                             start=k == 0, stop=k == KD - 1)
                    i.then_inc(rp, 1)

                pe.wait_ge(wl, 16 * (KD + 2))
                for t in range(TILES + 2):
                    if t < TILES:
                        main(t)
                    if 1 <= t <= TILES:
                        transposes(t - 1)
                    if t >= 2:
                        route(t - 2)

            @block.gpsimd
            def _(pool):
                for t in range(TILES):
                    r = rows_of(t)
                    pool.wait_ge(dm, t + 1)
                    pool.wait_ge(xl[t % 2], 16 * (t // 2 + 1))
                    nc.gpsimd.tensor_tensor(xa[0:r, t % 2, :], xa[0:r, t % 2, :], x[0:r, t % 2, :], ALU.add).then_inc(pa, 1)
                    pool.wait_ge(hm, t + 1)
                    nc.gpsimd.tensor_tensor(h2[0:r, t % 2, :], h2[0:r, t % 2, :], sh2[0:r, int(t == PT), :],
                                            ALU.add).then_inc(hr, 1)

            @block.scalar
            def _(act):
                for t in range(TILES):
                    r = rows_of(t)
                    act.wait_ge(pa, t + 1)
                    if t:
                        act.wait_ge(sqr, t)
                    nc.scalar.activation(sq[0:r, :], xa[0:r, t % 2, :], ACT.Square, accum_out=st[0:r, t, 0:1]).then_inc(sqr, 1)
                    act.wait_ge(msr, t + 1)
                    nc.scalar.activation(st[0:r, t, 2:3], st[0:r, t, 1:2], ACT.Sqrt).then_inc(rtr, 1)
                    act.wait_ge(tp, t + 1)
                    if t >= 2:
                        act.wait_ge(rp, t - 1)
                    nc.scalar.copy(h2T[:, t % 2, :, 0:r].rearrange("p (b k) r -> p b k r", b=2),
                                   m.ps[:, 4:6, :].rearrange("p b (k r) -> p b k r", r=P)[:, :, :, 0:r]).then_inc(te, 1)

            @block.vector
            def _(dve):
                v = nc.vector

                def gated(t):
                    r = rows_of(t)
                    dve.wait_ge(pm, t + 1)
                    if t >= 2:
                        dve.wait_ge(x1s[t % 2], 16 * (t // 2))
                        dve.wait_ge(hm, t - 1)
                    v.tensor_tensor(xa[0:r, t % 2, :].rearrange("p (b n) -> p b n", b=2),
                                    m.ps[0:r, 2 * (t % 2):2 * (t % 2) + 2, :],
                                    g1[0:r, int(t == PT), :].rearrange("p (b n) -> p b n", b=2), ALU.mult).then_inc(dm, 1)

                def logits(t):
                    dve.wait_ge(rp, t + 1)
                    r = rows_of(t)
                    v.tensor_copy(m.logits[0:r, t, :], m.ps[0:r, 6 + t % 2, 0:NG + NE]).then_inc(re, 1)

                v.tensor_scalar(sc2, sc2, 1.0, None, ALU.add).then_inc(one, 1)
                v.memset(m.logits[:, :, :], 0.0).then_inc(one, 1)
                dve.wait_ge(one, 2)
                gated(0)
                for t in range(TILES):
                    r = rows_of(t)
                    if t + 1 < TILES:
                        gated(t + 1)
                    dve.wait_ge(sqr, t + 1)
                    v.tensor_scalar(st[0:r, t, 1:2], st[0:r, t, 0:1], 1.0 / D, EPS, ALU.mult, ALU.add).then_inc(msr, 1)
                    dve.wait_ge(rtr, t + 1)
                    v.reciprocal(st[0:r, t, 3:4], st[0:r, t, 2:3]).then_inc(rcp, 1)
                    dve.wait_ge(rcp, t + 1)
                    if t >= 2:
                        dve.wait_ge(tp, t - 1)
                        dve.wait_ge(h2s[t % 2], 16 * (t // 2))
                    v.scalar_tensor_tensor(h2[0:r, t % 2, :], xa[0:r, t % 2, :], st[0:r, t, 3:4], sc2[0:r, int(t == PT), :],
                                           ALU.mult, ALU.mult).then_inc(hm, 1)
                    if t:
                        logits(t - 1)
                logits(PT)


def routing(nc, m, A):
    LT = MAXT + 3
    with ExitStack() as ctx:
        sb = lambda name, shape, dt=F32: ctx.enter_context(nc.sbuf_tensor(name, shape, dt))
        bias = sb("rt_bias", [P, NG + NE])
        s4 = sb("rt_s4", [P, 8, TILES, 4])
        s16 = sb("rt_s16", [P, 4, TILES, NG, EPG])
        s1 = sb("rt_s1", [P, 12, TILES])
        base = sb("rt_base", [P, TILES + 1, NE])
        tot = sb("rt_tot", [P, TILES, NE])
        ex = sb("rt_experts", [P, 4, NE])
        ti = sb("rt_tiles", [P, LT])
        te = sb("rt_te", [P, 2, LT])
        cmp = sb("rt_cmp", [P, LT, NE])
        iota = sb("rt_iota", [P, LT], I32)
        spare = sb("rt_spare", [MAXT * 2, P], I32)
        rows = sb("rt_rows", [MAXT * 2, P], I32)
        rowsf = sb("rt_rowsf", [MAXT * 2, P])
        tok = sb("rt_tok", [P, 2, TILES], I32)
        ids = sb("rt_ids", [P, 3, MAXT * 2])
        bl, io, chain, ex1, ex2, ea, mr, pp, zs, sr, sct, rl, rf, rp = (m.sem("rt_" + n) for n in (
            "bias_loaded", "iotas", "dve_chain", "exp_group", "exp_expert", "exps", "choices_ready", "psum",
            "table_zeroed", "slots_ready", "scattered", "rows_loaded", "rows_float", "rows_psum"))
        eq, ohg, e1, e2, oh1, oh2, gl, free4 = (s4[:, j] for j in range(8))
        gm, gs, gw, v1, v2, dd, aa, den, w1 = (s1[:, j, :] for j in range(9))
        free = s1[:, 9, :]
        with nc.Block() as block:
            @block.sync
            def _(sp):
                sp.dma_start(bias[:, 0:NG], A.b_route_group.broadcast_to([P, NG])).then_inc(bl, 16)
                sp.dma_start(bias[:, NG:], A.b_route_expert.broadcast_to([P, NE])).then_inc(bl, 16)
                sp.wait_ge(io, 3)
                sp.dma_start(m.tok_dram.rearrange("(a p) o -> a (p o)", p=P), spare[:, :]).then_inc(zs, 16)
                sp.wait_ge(sct, 16 * 2 * TILES)
                sp.dma_start(rows[:, :], m.tok_dram.rearrange("(a p) o -> a (p o)", p=P)).then_inc(rl, 16)

            @block.gpsimd
            def _(pool):
                nc.gpsimd.iota(iota[:, :], [[1, LT]], base=0, channel_multiplier=0).then_inc(io, 1)
                nc.gpsimd.iota(tok[:, :, :], [[NT, 2], [P, TILES]], base=0, channel_multiplier=1).then_inc(io, 1)
                nc.gpsimd.iota(spare[:, :], [[1, P]], base=2 * NT, channel_multiplier=P).then_inc(io, 1)
                pool.wait_ge(io, 3)
                pool.wait_ge(zs, 16)
                pool.wait_ge(sr, 1)
                for t in range(TILES):
                    r = rows_of(t)
                    for c in range(2):
                        nc.gpsimd.indirect_dma_start(
                            out=m.tok_dram, out_offset=bass.IndirectOffsetOnAxis(ap=m.slot[0:r, c, t:t + 1], axis=0),
                            in_=tok[0:r, c, t:t + 1], in_offset=None).then_inc(sct, 16)

            @block.scalar
            def _(act):
                act.wait_ge(ex1, 1)
                nc.scalar.activation(e1, gl, ACT.Exp).then_inc(ea, 1)
                act.wait_ge(ex2, 1)
                nc.scalar.activation(aa, dd, ACT.Exp).then_inc(ea, 1)

            @block.tensor
            def _(pe):
                pe.wait_ge(mr, 1)
                mm = s16[:, 2].rearrange("p t g j -> p (t g j)")
                nc.tensor.matmul(m.ps[:, 0, 0:TILES * NE], m.tri[:, :], mm, start=True, stop=True)
                nc.tensor.matmul(m.ps[:, 1, 0:TILES * NE], m.ones[:, :], mm, start=True, stop=True).then_inc(pp, 1)
                pe.wait_ge(rf, 1)
                nc.tensor.transpose(m.ps[:, 2, 0:MAXT * 2], rowsf[:, :], m.ident[0:MAXT * 2, 0:MAXT * 2]).then_inc(rp, 1)

            @block.vector
            def _(dve):
                v = nc.vector
                step = Chain(dve, chain)
                tt, ts = v.tensor_tensor, v.tensor_scalar

                def first_of_highest(values, highest, oh):
                    step(v.tensor_reduce(highest, values, AX.X, ALU.max))
                    step(tt(oh, values, bc(highest, 2, 4), ALU.is_equal))
                    step(ts(free, oh[:, :, 0], -1.0, 1.0, ALU.mult, ALU.add))
                    for j in range(1, 4):
                        step(tt(oh[:, :, j], oh[:, :, j], free, ALU.mult))
                        step(tt(free, free, oh[:, :, j], ALU.subtract))

                lg = m.logits
                dve.wait_ge(bl, 32)
                step(tt(lg[:, :, :], lg[:, :, :], bc(bias[:, :], 1, TILES), ALU.add))
                groups = lg[:, :, 0:NG]
                first_of_highest(groups, gm, ohg)
                tt(gl, groups, bc(gm, 2, 4), ALU.subtract).then_inc(ex1, 1)
                prod = s16[:, 0]
                step(tt(prod, lg[:, :, NG:].rearrange("p t (g j) -> p t g j", g=NG), bc(ohg, 3, EPG), ALU.mult))
                step(v.tensor_reduce(e2, prod.rearrange("p t g j -> p t j g"), AX.X, ALU.add))
                first_of_highest(e2, v1, oh1)
                step(v.scalar_tensor_tensor(e2, oh1, NEG, e2, ALU.mult, ALU.add))
                first_of_highest(e2, v2, oh2)
                tt(dd, v2, v1, ALU.subtract).then_inc(ex2, 1)
                dve.wait_ge(ea, 2)
                step(v.tensor_reduce(gs, e1, AX.X, ALU.add))
                step(ts(den, aa, 1.0, None, ALU.add))
                step(tt(den, den, gs, ALU.mult))
                step(v.reciprocal(m.wt[:, 0, :], den))
                step(tt(m.wt[:, 1, :], m.wt[:, 0, :], aa, ALU.mult))
                for c, oh in enumerate((oh1, oh2)):
                    step(tt(s16[:, c], bc(ohg, 3, EPG), bc(oh, 2, NG), ALU.mult))
                    step(v.memset(s16[DEC:P, c, PT, :, :], 0.0))
                tt(s16[:, 2], s16[:, 0], s16[:, 1], ALU.add).then_inc(mr, 1)
                dve.wait_ge(pp, 1)
                fl = lambda a: a.rearrange("p t g j -> p (t g j)")
                step(v.tensor_copy(tot[:, :, :].rearrange("p t e -> p (t e)"), m.ps[:, 1, 0:TILES * NE]))
                step(v.memset(base[:, 0, :], 0.0))
                for t in range(TILES):
                    step(tt(base[:, t + 1, :], base[:, t, :], tot[:, t, :], ALU.add))
                count, tiles, done, start = (ex[:, j, :] for j in range(4))
                step(ts(tiles, base[:, TILES, :], 0.0, None, ALU.is_gt))
                for j in range(1, -(-NT // SLOTS)):
                    step(v.scalar_tensor_tensor(tiles, base[:, TILES, :], float(j * SLOTS), tiles, ALU.is_gt, ALU.add))
                step(v.tensor_tensor_scan(done, m.ones[:, 0:NE], tiles, 0.0, ALU.mult, ALU.add))
                step(tt(start, done, tiles, ALU.subtract))
                step(ts(start, start, float(SLOTS), None, ALU.mult))
                step(tt(tot[:, :, :], base[:, 0:TILES, :], bc(start, 1, TILES), ALU.add))
                step(tt(tot[:, :, :].rearrange("p t e -> p (t e)"), tot[:, :, :].rearrange("p t e -> p (t e)"),
                        m.ps[:, 0, 0:TILES * NE], ALU.add))
                for c in range(2):
                    step(tt(s16[:, c].rearrange("p t g j -> p t (g j)"), s16[:, c].rearrange("p t g j -> p t (g j)"),
                            tot[:, :, :], ALU.mult))
                    step(v.tensor_reduce(s1[:, 10 + c, :], s16[:, c].rearrange("p t g j -> p t (g j)"), AX.X, ALU.add))
                v.tensor_copy(m.slot[:, :, :], s1[:, 10:12, :]).then_inc(sr, 1)
                dve.wait_ge(io, 3)
                step(v.tensor_copy(ti[:, :], iota[:, :]))
                step(tt(cmp[:, :, :], bc(ti[:, :], 2, NE), bc(done, 1, LT), ALU.is_ge))
                step(v.tensor_reduce(te[:, 0, :], cmp[:, :, :], AX.X, ALU.add))
                step(ts(m.tile_expert[:, :], te[:, 0, :], float(NE - 1), None, ALU.min))
                step(ts(te[:, 1, 0:1], done[:, NE - 1:NE], 0.5, -0.25, ALU.mult, ALU.add))
                step(ts(te[:, 1, 0:1], te[:, 1, 0:1], ROUND, None, ALU.add))
                step(ts(te[:, 1, 0:1], te[:, 1, 0:1], -ROUND, None, ALU.add))
                step(tt(te[:, 1, 1:2], te[:, 1, 0:1], te[:, 1, 0:1], ALU.add))
                step(tt(te[:, 1, 1:2], te[:, 1, 1:2], done[:, NE - 1:NE], ALU.is_lt))
                step(tt(m.pairs[:, :], te[:, 1, 0:1], te[:, 1, 1:2], ALU.add))
                dve.wait_ge(rl, 16)
                v.tensor_copy(rowsf[:, :], rows[:, :]).then_inc(rf, 1)
                dve.wait_ge(rp, 1)
                step(v.tensor_copy(ids[:, 0, :], m.ps[:, 2, 0:MAXT * 2]))
                step(v.tensor_copy(m.slot_row[:, 0:MAXT * 2], ids[:, 0, :]))
                step(ts(ids[:, 1, :], ids[:, 0, :], NT - 0.5, -float(NT), ALU.is_ge, ALU.mult))
                step(tt(ids[:, 1, :], ids[:, 1, :], ids[:, 0, :], ALU.add))
                step(ts(ids[:, 2, :], ids[:, 1, :], NT - 0.5, None, ALU.is_lt))
                step(v.memset(m.slot_token[:, :], 0))
                step(tt(m.slot_token[:, 0:MAXT * 2], ids[:, 1, :], ids[:, 2, :], ALU.mult))


def experts(nc, m, A):
    with ExitStack() as ctx:
        sb = lambda name, shape, dt=F32: ctx.enter_context(nc.sbuf_tensor(name, shape, dt))
        wg = sb("ex_wg", [P, 2, KD, FD])
        wu = sb("ex_wu", [P, 2, KD, FD])
        wd = sb("ex_wd", [P, 2, 2, D])
        idx = sb("ex_idx", [P, 2, 2], I32)
        row = sb("ex_row", [P, 2, 2], I32)
        xg = sb("ex_x", [P, 2, 2, D])
        xT = sb("ex_xT", [P, 2, KD, SLOTS])
        sl = sb("ex_silu", [P, 2, SLOTS])
        hid = sb("ex_hid", [P, 2, 2, SLOTS])
        yo = sb("ex_y", [P, 2, 2, D])
        wl, gl, ys = ([m.sem(f"ex_{n}{i}") for i in range(2)] for n in ("w_loaded", "x_gathered", "y_stored"))
        ic, rc, tp, xed, xea, gp, slr, hr, dn, yea, yed = (m.sem("ex_" + n) for n in (
            "index_copied", "row_copied", "x_transposed", "xT_by_dve", "xT_by_act", "gate_up_psum", "silu_ready", "hid_ready",
            "down_psum", "y_by_act", "y_by_dve"))

        idle = sb("ex_idle", [1, 7])
        begun, idle_set = m.sem("ex_begun"), m.sem("ex_idle_set")

        def wait(engine, sem, value):
            if not (isinstance(value, int) and value <= 0):
                engine.wait_ge(sem, value)

        def wait_alone(place, sem, value):
            nc.gpsimd.wait_ge(sem, value)
            nc.gpsimd.tensor_tensor(idle[:, place:place + 1], idle[:, 0:1], idle[:, 0:1], ALU.add)

        def run(engine, body, before=None, after=None):
            pairs = engine.value_load(m.pairs[0:1, 0:1], min_val=2, max_val=MAXT // 2)
            if before:
                before()
            body(0)
            with engine.Fori(1, pairs) as i:
                body(i)
            if after:
                after(pairs)

        with nc.Block() as block:
            @block.sync
            def _(sp):
                def weights(i, b):
                    e = sp.value_load(m.tile_expert[0:1, bass.ds(2 * i + b, 1)], min_val=0, max_val=NE - 1)
                    for dst, src in ((wg, A.w_gate), (wu, A.w_up), (wd, A.w_down)):
                        sp.dma_start(dst[:, b, :, :], src[bass.ds(e, 1), :, :].rearrange("o (k p) n -> p (o k) n", p=P)) \
                            .then_inc(wl[b], 16)

                def body(i):
                    for b in range(2):
                        sp.wait_ge(dn, 4 * (2 * i + b) + 4)
                        weights(i + 1, b)

                run(sp, body, lambda: (weights(0, 0), weights(0, 1)))

            @block.gpsimd
            def _(pool):
                def gather(i, b):
                    n = 2 * i + b
                    wait(pool, tp, 4 * n - 4)
                    nc.gpsimd.tensor_copy(idx[:, b, :], m.slot_token[:, bass.ds(2 * n, 2)]).then_inc(ic, 1)
                    wait_alone(1 + b, ic, n + 1)
                    for a in range(2):
                        nc.gpsimd.indirect_dma_start(
                            out=xg[:, b, a, :], out_offset=None, in_=m.h2_dram,
                            in_offset=bass.IndirectOffsetOnAxis(ap=idx[:, b, a:a + 1], axis=0)).then_inc(gl[b], 16)

                def scatter(i, b):
                    n = 2 * i + b
                    wait(pool, ys[b], 32 * i)
                    nc.gpsimd.tensor_copy(row[:, b, :], m.slot_row[:, bass.ds(2 * n, 2)]).then_inc(rc, 1)
                    pool.wait_ge(rc, n + 1)
                    for a, ready in enumerate((yea, yed)):
                        wait_alone(3 + 2 * b + a, ready, 2 * n + 2)
                        nc.gpsimd.indirect_dma_start(
                            out=m.y_dram, out_offset=bass.IndirectOffsetOnAxis(ap=row[:, b, a:a + 1], axis=0),
                            in_=yo[:, b, a, :], in_offset=None).then_inc(ys[b], 16)

                def body(i):
                    gather(i, 1)
                    scatter(i, 0)
                    gather(i + 1, 0)
                    scatter(i, 1)

                def after(pairs):
                    for b in range(2):
                        pool.wait_ge(ys[b], 32 * pairs)
                        pool.wait_ge(wl[b], 48 * pairs + 48)

                nc.gpsimd.memset(idle[:, 0:1], 0.0).then_inc(idle_set, 1)
                pool.wait_ge(idle_set, 1)
                run(pool, body, lambda: gather(0, 0), after)

            @block.tensor
            def _(pe):
                def transposes(i, b):
                    n = 2 * i + b
                    pe.wait_ge(gl[b], 32 * i + 32)
                    for q in range(4):
                        wait(pe, (xed, xea)[q % 2], 2 * n + q // 2)
                        for k in range(2):
                            for a in range(2):
                                j = nc.tensor.transpose(m.ps[:, q % 2, SLOTS * k + P * a:SLOTS * k + P * (a + 1)],
                                                        xg[:, b, a, P * (2 * q + k):P * (2 * q + k + 1)], m.ident[:, :])
                        j.then_inc(tp, 1)

                def gate_up(i, b):
                    n = 2 * i + b
                    pe.wait_ge(wl[b], 48 * i + 48)
                    pe.wait_ge(xed, 2 * n + 2)
                    pe.wait_ge(xea, 2 * n + 2)
                    for f in range(2):
                        wait(pe, hr, 2 * n - 1 + f)
                        for x, w in enumerate((wg, wu)):
                            for k in range(KD):
                                j = nc.tensor.matmul(m.ps[:, 2 + f, SLOTS * x:SLOTS * (x + 1)],
                                                     w[:, b, k, P * f:P * (f + 1)], xT[:, b, k, :],
                                                     start=k == 0, stop=k == KD - 1)
                        j.then_inc(gp, 1)

                def down(i, b):
                    n = 2 * i + b
                    pe.wait_ge(hr, 2 * n + 2)
                    for a in range(2):
                        wait(pe, (yea, yed)[a], 2 * n)
                        for c in range(2):
                            for f in range(2):
                                j = nc.tensor.matmul(m.ps[:, 4 + 2 * a + c, :], hid[:, b, f, P * a:P * (a + 1)],
                                                     wd[:, b, f, 512 * c:512 * (c + 1)], start=f == 0, stop=f == 1)
                            j.then_inc(dn, 1)

                def body(i):
                    gate_up(i, 0)
                    transposes(i, 1)
                    down(i, 0)
                    gate_up(i, 1)
                    transposes(i + 1, 0)
                    down(i, 1)

                run(pe, body, lambda: transposes(0, 0))

            @block.scalar
            def _(act):
                def xts(i, b):
                    for q in (1, 3):
                        act.wait_ge(tp, 4 * (2 * i + b) + q + 1)
                        nc.scalar.copy(xT[:, b, 2 * q:2 * q + 2, :].rearrange("p k n -> p (k n)"), m.ps[:, 1, :]).then_inc(xea, 1)

                def half(i, b):
                    n = 2 * i + b
                    for f in range(2):
                        act.wait_ge(gp, 2 * n + f + 1)
                        wait(act, hr, 2 * n - 1 + f)
                        nc.scalar.activation(sl[:, f, :], m.ps[:, 2 + f, 0:SLOTS], ACT.Silu).then_inc(slr, 1)
                    xts(i + b, 1 - b)
                    wait(act, ys[b], 32 * i)
                    for c in range(2):
                        act.wait_ge(dn, 4 * n + c + 1)
                        nc.scalar.copy(yo[:, b, 0, 512 * c:512 * (c + 1)], m.ps[:, 4 + c, :]).then_inc(yea, 1)

                act.wait_ge(begun, 1)
                run(act, lambda i: (half(i, 0), half(i, 1)), lambda: xts(0, 0))

            @block.vector
            def _(dve):
                v = nc.vector

                def xts(i, b):
                    for q in (0, 2):
                        dve.wait_ge(tp, 4 * (2 * i + b) + q + 1)
                        v.tensor_copy(xT[:, b, 2 * q:2 * q + 2, :].rearrange("p k n -> p (k n)"), m.ps[:, 0, :]).then_inc(xed, 1)

                def half(i, b):
                    n = 2 * i + b
                    for f in range(2):
                        dve.wait_ge(slr, 2 * n + f + 1)
                        v.tensor_tensor(hid[:, b, f, :], sl[:, f, :], m.ps[:, 2 + f, SLOTS:2 * SLOTS], ALU.mult).then_inc(hr, 1)
                    xts(i + b, 1 - b)
                    wait(dve, ys[b], 32 * i)
                    for c in range(2):
                        dve.wait_ge(dn, 4 * n + c + 3)
                        v.tensor_copy(yo[:, b, 1, 512 * c:512 * (c + 1)], m.ps[:, 6 + c, :]).then_inc(yed, 1)

                v.memset(sl[:, :, :], 0.0).then_inc(begun, 1)
                dve.wait_ge(begun, 1)
                run(dve, lambda i: (half(i, 0), half(i, 1)), lambda: xts(0, 0))


def combine(nc, m, A, O):
    with ExitStack() as ctx:
        sb = lambda name, shape: ctx.enter_context(nc.sbuf_tensor(name, shape, F32))
        NB = 2
        y = sb("cb_y", [P, NB, 2, D])
        x1 = sb("cb_x1", [P, NB, D])
        o = sb("cb_o", [P, NB, D])
        yl, xl, os_ = ([m.sem(f"cb_{n}{i}") for i in range(NB)] for n in ("y_loaded", "x1_loaded", "stored"))
        chain, orr = m.sem("cb_dve_chain"), m.sem("cb_out_ready")
        with nc.Block() as block:
            @block.vector
            def _(dve):
                step = Chain(dve, chain)
                v = nc.vector
                for t in range(TILES):
                    r, b = rows_of(t), t % NB
                    dve.wait_ge(yl[b], 32 * (t // NB + 1))
                    y1, y2, dst = y[0:r, b, 0, :], y[0:r, b, 1, :], o[0:r, b, :]
                    step(v.tensor_scalar(y1, y1, m.wt[0:r, 0, t:t + 1], None, ALU.mult))
                    step(v.scalar_tensor_tensor(y1, y2, m.wt[0:r, 1, t:t + 1], y1, ALU.mult, ALU.add))
                    step(v.tensor_tensor(y1, y1, m.modB[0:r, 1, int(t == PT), :], ALU.mult))
                    dve.wait_ge(xl[b], 16 * (t // NB + 1))
                    if t >= NB:
                        dve.wait_ge(os_[b], 16 * (t // NB))
                    v.tensor_tensor(dst, y1, x1[0:r, b, :], ALU.add).then_inc(orr, 1)

            @block.sync
            def _(sp):
                for t in range(TILES + 1):
                    if t < TILES:
                        r, b = rows_of(t), t % NB
                        if t >= NB:
                            sp.wait_ge(orr, t - NB + 1)
                        for c in range(2):
                            sp.dma_start(y[0:r, b, c, :], m.y_dram[c * NT + t * P:c * NT + t * P + r, :]).then_inc(yl[b], 16)
                        sp.dma_start(x1[0:r, b, :], m.x1_dram[t * P:t * P + r, :]).then_inc(xl[b], 16)
                    if t:
                        u = t - 1
                        sp.wait_ge(orr, u + 1)
                        dst = O.y_prompt[0, u * P:(u + 1) * P, :] if u < PT else O.y_sample[0, :, :]
                        sp.dma_start(dst, o[0:rows_of(u), u % NB, :]).then_inc(os_[u % NB], 16)
                for i in range(NB):
                    sp.wait_ge(os_[i], 16 * ((TILES - i + NB - 1) // NB))


def fresh_semaphores(nc, m):
    nc.clear_and_free_semaphores(m.sems)
    nc.all_engine_barrier()
    m.sems = []


def new_semaphore(nc, m, name):
    m.sems.append(nc.alloc_semaphore(name))
    return m.sems[-1]


def program(nc, A, O):
    ctx = ExitStack()
    m = Mem()
    m.sems = []
    m.sem = lambda name: new_semaphore(nc, m, name)
    with ctx:
        def sb(name, shape, dt=F32):
            return ctx.enter_context(nc.sbuf_tensor(name, shape, dt))
        m.ps = ctx.enter_context(nc.psum_tensor("ps", [P, 8, 512], F32))
        m.ident = sb("ident", [P, P])
        m.ones = sb("ones", [P, P])
        m.tri = sb("tri", [P, P])
        m.cT = sb("cT", [P, KD, 2])
        m.mod_dram = nc.dram_tensor("mod", [2, 6 * D], F32, kind="Internal").ap()
        m.sh1 = sb("sh1", [P, KD, 2])
        m.sc1 = sb("sc1", [P, KD, 2])
        m.hT = sb("hT", [P, KD, NT])
        constants(nc, m, A)
        with nc.sbuf_tensor("modrow", [2, 2 * D], F32) as m.modrow:
            adaln(nc, m, A, 0, 4, "a")
            mod_columns(nc, m)
        norm_in(nc, m, A)
        m.q_dram = nc.dram_tensor("q_dram", [P, 4, NT], F32, kind="Internal").ap()
        m.qiT = sb("qiT", [P, 2, NT])
        m.kT = sb("kT", [P, NT])
        m.kiT = sb("kiT", [P, NT])
        m.v = sb("v", [P, PT, HD])
        m.vs = sb("vs", [P, CB + 1, HD])
        m.wi = sb("wi", [P, TILES, IH])
        m.tokqi = sb("tokqi", [P, 2, IH * ID])
        m.zT = sb("zT", [P, 4, NT])
        m.x1_dram = nc.dram_tensor("x1_dram", [NT, D], F32, kind="Internal").ap()
        m.h2_dram = nc.dram_tensor("h2_dram", [NT, D], F32, kind="Internal").ap()
        m.y_dram = nc.dram_tensor("y_dram", [2 * NT + MAXT * SLOTS, D], F32, kind="Internal").ap()
        m.tok_dram = nc.dram_tensor("tok_dram", [MAXT * SLOTS, 1], I32, kind="Internal").ap()
        m.us_dram = nc.dram_tensor("us_dram", [DEC, 512], F32, kind="Internal").ap()
        with nc.sbuf_tensor("u", [P, G, T, J], F32) as m.u, nc.sbuf_tensor("us", [DEC, 512], F32) as m.us:
            with nc.sbuf_tensor("qT", [P, 4, NT], F32) as m.qT:
                project(nc, m, A, O)
            with ExitStack() as ssm:
                ssb = lambda name, shape: ssm.enter_context(nc.sbuf_tensor(name, shape, F32))
                m.M = ssb("M", [P, G, P])
                m.V = ssb("V", [P, 2, PAIR, T + 1, J])
                m.W = ssb("W", [P, 2, PAIR, P])
                m.rot = ssb("rot", [P, 2, PAIR, COLS])
                m.decay = ssb("decay", [P, PAIR, COLS])
                m.r8 = ssb("r8", [P, PAIR])
                m.h0 = ssb("h0", [P, 2, PAIR])
                ssm_parameters(nc, m, A)
                ssm_scan(nc, m, A, O)
        fresh_semaphores(nc, m)
        m.attnT = sb("attnT", [P, 4, NT])
        with ExitStack() as at:
            asb = lambda name, shape, dt=F32: at.enter_context(nc.sbuf_tensor(name, shape, dt))
            m.mask = asb("mask", [P, MK_W], BF16)
            m.kTs = asb("kTs", [P, PAST + DEC])
            with nc.sbuf_tensor("kiTs", [P, PAST + DEC], F32) as m.kiTs, nc.sbuf_tensor("sc", [P, SC_W], F32) as m.sc:
                cache_keys(nc, m, A)
                index_scores(nc, m)
                select_keys(nc, m)
            m.qT = asb("qT2", [P, 4, NT])
            load_q(nc, m)
            attention(nc, m)
        with nc.sbuf_tensor("modrow2", [2, 4 * D], F32) as m.modrow:
            adaln(nc, m, A, 4, 12, "b")
        m.logits = sb("logits", [P, TILES, NG + NE])
        with nc.sbuf_tensor("mergedT", [P, KD, NT], F32) as m.mergedT:
            merge(nc, m, A)
            flat = lambda a: a[:, :, :].rearrange("p k n -> p (k n)")
            m.wout = flat(m.hT)[:, 0:KD * D].rearrange("p (k n) -> p k n", k=KD)
            m.modA = flat(m.zT)[:, 0:4 * D].rearrange("p (a s n) -> p a s n", a=2, s=2)
            m.modB = flat(m.attnT)[:, 0:4 * D].rearrange("p (a s n) -> p a s n", a=2, s=2)
            fresh_semaphores(nc, m)
            load_mod_rows(nc, m, m.modA, (2, 4), "modA_loaded")
            load_mod_rows(nc, m, m.modB, (3, 5), "modB_loaded")
            output_projection(nc, m, A)
        m.wt = sb("choice_weight", [P, 2, TILES])
        m.slot = sb("slot", [P, 2, TILES], I32)
        m.slot_row = sb("slot_row", [P, MAXT * 2], I32)
        m.slot_token = sb("slot_token", [P, MAXT * 2 + 4], I32)
        m.tile_expert = sb("tile_expert", [P, MAXT + 3], I32)
        m.pairs = sb("pairs", [P, 1], I32)
        routing(nc, m, A)
        experts(nc, m, A)
        combine(nc, m, A, O)


_INS = ['x_prompt', 'x_sample', 'cache_k', 'cache_v', 'cache_kidx', 'state_ssm_re', 'state_ssm_im',
        'c_prompt', 'c_sample', 'w_ada', 'b_ada', 'w_in', 'ssm_a_re', 'ssm_a_im', 'ssm_log_dt',
        'ssm_b_re', 'ssm_b_im', 'ssm_c_re', 'ssm_c_im', 'ssm_d', 'w_glu', 'q_gain', 'k_gain', 'kidx_gain',
        'w_attn_out', 'w_out', 'w_route_group', 'b_route_group', 'w_route_expert', 'b_route_expert',
        'w_gate', 'w_up', 'w_down']
_LAYERED = {n for n in _INS if n.startswith(('w_', 'cache', 'state', 'ssm'))}
_OUTS = [('y_prompt', (1, SEQ, D)), ('y_sample', (1, DEC, D)),
         ('k_prompt', (1, 1, SEQ, HD)), ('v_prompt', (1, 1, SEQ, HD)), ('kidx_prompt', (1, 1, SEQ, ID)),
         ('ssm_re_prompt', (1, 1, G, ST)), ('ssm_im_prompt', (1, 1, G, ST)),
         ('k_sample', (1, 1, DEC, HD)), ('v_sample', (1, 1, DEC, HD)), ('kidx_sample', (1, 1, DEC, ID)),
         ('ssm_re_sample', (1, 1, G, ST)), ('ssm_im_sample', (1, 1, G, ST))]


class Args:
    pass


def kernel(**inputs):
    import numpy as _np
    import concourse.bacc as _bacc
    from concourse.bass_utils import run_bass_kernel_spmd as _run

    nc = _bacc.Bacc("TRN2", target_bir_lowering=False, num_devices=1)
    arrays, ins, outs = {}, Args(), Args()
    for name in _INS:
        a = _np.ascontiguousarray(inputs[name])
        arrays[f"in_{name}"] = a
        ap = nc.dram_tensor(f"in_{name}", a.shape, F32, kind="ExternalInput").ap()
        vars(ins)[name] = ap[0] if name in _LAYERED else ap
    for name, shape in _OUTS:
        vars(outs)[name] = nc.dram_tensor(f"out_{name}", shape, F32, kind="ExternalOutput").ap()
    program(nc, ins, outs)
    r = _run(nc, [arrays], core_ids=[0])
    return tuple(r.results[0][f"out_{name}"] for name, _ in _OUTS)
```

```python
import math
from contextlib import ExitStack

import concourse.bass as bass
from concourse import mybir

F32 = mybir.dt.float32
BF16 = mybir.dt.bfloat16
I32 = mybir.dt.int32
U32 = mybir.dt.uint32
ALU = mybir.AluOpType
ACT = mybir.ActivationFunctionType
AX = mybir.AxisListType

P = 128
D = 1024
KD = D // P
SEQ, DEC = 1024, 64
NT = SEQ + DEC
PT = SEQ // P
TILES = PT + 1
PAST = 2048
CB = PAST // P
NS = PAST + DEC
EPS = 1e-6
NEG = -1e30
H, HD = 8, 64
IH, ID = 8, 32
TOPK = 256
G, ST, J = 32, 64, 16
PAIR = G // 2
T = 8
NCH = SEQ // T
SCH = DEC // T
COLS = NCH + 1 + SCH + 1
S0 = NCH + 1
NG, EPG, NE, FD = 4, 4, 16, 256
SLOTS = 256
MAXT = (2 * NT + NE * (SLOTS - 1)) // SLOTS
MAXT += MAXT % 2
OFF_U, OFF_Q, OFF_R, OFF_GA, OFF_GB = 0, 512, 1024, 1448, 2472
RW = OFF_GA - OFF_R
TW = 512 + RW
K0, V0, QI0, KI0, WI0 = 512, 576, 640, 896, 928


def rows_of(t):
    return P if t < PT else DEC


class Chain:

    def __init__(self, engine, sem):
        self.engine, self.sem, self.n = engine, sem, 0

    def __call__(self, instruction):
        instruction.then_inc(self.sem, 1)
        self.n += 1
        self.engine.wait_ge(self.sem, self.n)


class Mem:
    pass


def constants(nc, m, A):
    made = m.sem("constants_made")
    with nc.Block() as block:
        @block.gpsimd
        def _(pool):
            step = Chain(pool, made)
            step(nc.gpsimd.memset(m.ident[:, :], 0.0))
            step(nc.gpsimd.affine_select(out=m.ident[:, :], in_=m.ident[:, :], compare_op=ALU.not_equal,
                                         fill=1.0, base=0, pattern=[[-1, P]], channel_multiplier=1))
            nc.gpsimd.memset(m.ones[:, :], 1.0)
            step(nc.gpsimd.memset(m.tri[:, :], 1.0))
            step(nc.gpsimd.affine_select(out=m.tri[:, :], in_=m.tri[:, :], compare_op=ALU.is_gt,
                                         fill=0.0, base=0, pattern=[[1, P]], channel_multiplier=-1))


def adaln(nc, m, A, first, last, tag):
    with ExitStack() as ctx:
        n = last - first
        NB = 3
        w = ctx.enter_context(nc.sbuf_tensor("wada" + tag, [P, NB, KD, 512], F32))
        b = ctx.enter_context(nc.sbuf_tensor("bada" + tag, [1, n * 512], F32))
        row = m.modrow
        stored = m.sem("ada_row_stored" + tag)
        c16 = ctx.enter_context(nc.sbuf_tensor("c16" + tag, [2 * KD, P], F32))
        w_in = [m.sem(f"ada_w_loaded{i}{tag}") for i in range(NB)]
        c_in = m.sem("ada_c_loaded" + tag)
        c_t = m.sem("ada_c_transposed" + tag)
        c_s = m.sem("ada_c_silu" + tag)
        ps = m.sem("ada_psum_ready" + tag)
        free = m.sem("ada_psum_free" + tag)
        wsrc = A.w_ada.rearrange("(k p) n -> p k n", p=P)
        with nc.Block() as block:
            @block.sync
            def _(sp):
                sp.dma_start(c16[0:KD, :], A.c_prompt.rearrange("o (k p) -> (o k) p", p=P)).then_inc(c_in, 16)
                sp.dma_start(c16[KD:2 * KD, :], A.c_sample.rearrange("o (k p) -> (o k) p", p=P)).then_inc(c_in, 16)
                sp.dma_start(b[:, :], A.b_ada[:, first * 512:last * 512]).then_inc(c_in, 16)
                for i in range(n):
                    if i >= NB:
                        sp.wait_ge(ps, i - NB + 1)
                    sp.dma_start(w[:, i % NB, :, :], wsrc[:, :, (first + i) * 512:(first + i + 1) * 512]) \
                        .then_inc(w_in[i % NB], 16)
                sp.wait_ge(free, n)
                sp.dma_start(m.mod_dram[:, first * 512:last * 512], row[0:2, 0:n * 512]).then_inc(stored, 16)
                sp.wait_ge(stored, 16)

            @block.tensor
            def _(pe):
                pe.wait_ge(c_in, 48)
                nc.tensor.transpose(m.ps[:, 7, 0:2 * KD], c16[:, :], m.ident[0:2 * KD, 0:2 * KD]).then_inc(c_t, 1)
                pe.wait_ge(c_s, 1)
                for i in range(n):
                    pe.wait_ge(w_in[i % NB], 16 * (i // NB + 1))
                    if i >= 2:
                        pe.wait_ge(free, i - 1)
                    for k in range(KD):
                        nc.tensor.matmul(m.ps[0:2, i % 2, :], m.cT[:, k, :], w[:, i % NB, k, :],
                                         start=k == 0, stop=False)
                    nc.tensor.matmul(m.ps[0:2, i % 2, :], m.ones[0:1, 0:2], b[0:1, i * 512:(i + 1) * 512],
                                     start=False, stop=True).then_inc(ps, 1)

            @block.scalar
            def _(act):
                act.wait_ge(c_t, 1)
                nc.scalar.activation(m.cT[:, :, :].rearrange("p k s -> p s k"),
                                     m.ps[:, 7, 0:2 * KD].rearrange("p (s k) -> p s k", s=2), ACT.Silu).then_inc(c_s, 1)

            @block.vector
            def _(dve):
                for i in range(n):
                    dve.wait_ge(ps, i + 1)
                    nc.vector.tensor_copy(row[0:2, i * 512:(i + 1) * 512],
                                          m.ps[0:2, i % 2, :]).then_inc(free, 1)


def mod_columns(nc, m):
    tr = m.sem("modcol_transposed")
    with nc.Block() as block:
        @block.tensor
        def _(pe):
            for j in range(2 * KD):
                i = nc.tensor.transpose(m.ps[:, 0, 2 * j:2 * j + 2], m.modrow[0:2, j * P:(j + 1) * P], m.ident[0:2, 0:2])
            i.then_inc(tr, 1)

        @block.vector
        def _(dve):
            dve.wait_ge(tr, 1)
            nc.vector.tensor_copy(m.sh1[:, :, :], m.ps[:, 0, 0:2 * KD].rearrange("p (k s) -> p k s", s=2))
            nc.vector.tensor_scalar(m.sc1[:, :, :], m.ps[:, 0, 2 * KD:4 * KD].rearrange("p (k s) -> p k s", s=2),
                                    1.0, None, ALU.add)


def norm_in(nc, m, A):
    with ExitStack() as ctx:
        NB = 3
        x = ctx.enter_context(nc.sbuf_tensor("n1_x", [P, NB, D], F32))
        xn = ctx.enter_context(nc.sbuf_tensor("n1_xn", [P, 2, D], F32))
        junk = ctx.enter_context(nc.sbuf_tensor("n1_sq", [P, D], F32))
        st = ctx.enter_context(nc.sbuf_tensor("n1_st", [P, TILES, 4], F32))
        x_in = [m.sem(f"n1_x_loaded{i}") for i in range(NB)]
        sq, ms, sr, chain = m.sem("n1_sumsq"), m.sem("n1_meansq"), m.sem("n1_root"), m.sem("n1_dve_chain")
        xnr, tr, ev, sqc = m.sem("n1_xn_ready"), m.sem("n1_transposed"), m.sem("n1_evacuated"), m.sem("n1_act_chain")
        with nc.Block() as block:
            @block.sync
            def _(sp):
                for t in range(TILES):
                    r = rows_of(t)
                    if t >= NB:
                        sp.wait_ge(xnr, t - NB + 1)
                    src = A.x_prompt[0, t * P:(t + 1) * P, :] if t < PT else A.x_sample[0, :, :]
                    sp.dma_start(x[0:r, t % NB, :], src).then_inc(x_in[t % NB], 16)

            @block.scalar
            def _(act):
                for t in range(TILES):
                    r = rows_of(t)
                    act.wait_ge(x_in[t % NB], 16 * (t // NB + 1))
                    if t:
                        act.wait_ge(sq, t)
                    nc.scalar.activation(junk[0:r, :], x[0:r, t % NB, :], ACT.Square,
                                         accum_out=st[0:r, t, 0:1]).then_inc(sq, 1)
                    act.wait_ge(ms, t + 1)
                    nc.scalar.activation(st[0:r, t, 2:3], st[0:r, t, 1:2], ACT.Sqrt).then_inc(sr, 1)

            @block.vector
            def _(dve):
                def evacuate(t):
                    r, s = rows_of(t), int(t == PT)
                    dve.wait_ge(tr, t + 1)
                    for k in range(KD):
                        i = nc.vector.tensor_scalar(m.hT[:, k, t * P:t * P + r],
                                                    m.ps[:, 2 * (t % 2) + k // 4, (k % 4) * P:(k % 4) * P + r],
                                                    m.sc1[:, k, s:s + 1], m.sh1[:, k, s:s + 1], ALU.mult, ALU.add)
                    i.then_inc(ev, 1)

                step = Chain(dve, chain)
                for t in range(TILES):
                    r = rows_of(t)
                    dve.wait_ge(sq, t + 1)
                    nc.vector.tensor_scalar(st[0:r, t, 1:2], st[0:r, t, 0:1], 1.0 / D, EPS, ALU.mult, ALU.add).then_inc(ms, 1)
                    dve.wait_ge(sr, t + 1)
                    step(nc.vector.reciprocal(st[0:r, t, 3:4], st[0:r, t, 2:3]))
                    if t >= 2:
                        dve.wait_ge(tr, t - 1)
                    nc.vector.tensor_scalar(xn[0:r, t % 2, :], x[0:r, t % NB, :], st[0:r, t, 3:4], None,
                                            ALU.mult).then_inc(xnr, 1)
                    if t:
                        evacuate(t - 1)
                evacuate(PT)

            @block.tensor
            def _(pe):
                for t in range(TILES):
                    r = rows_of(t)
                    pe.wait_ge(xnr, t + 1)
                    if t >= 2:
                        pe.wait_ge(ev, t - 1)
                    for k in range(KD):
                        i = nc.tensor.transpose(m.ps[:, 2 * (t % 2) + k // 4, (k % 4) * P:(k % 4) * P + r],
                                                xn[0:r, t % 2, k * P:(k + 1) * P], m.ident[0:r, 0:r])
                    i.then_inc(tr, 1)


def bc(ap, axis, n):
    shape = list(ap.shape)
    return ap.unsqueeze(axis).broadcast_to(shape[:axis] + [n] + shape[axis:])


def project(nc, m, A, O):
    with ExitStack() as ctx:
        sb = lambda name, shape: ctx.enter_context(nc.sbuf_tensor(name, shape, F32))
        w = sb("pj_w", [P, KD, 512 + 512 + RW])
        tok = sb("pj_tok", [P, 2, TW])
        sq = sb("pj_sq", [P, 608])
        st = sb("pj_st", [P, TILES, 4, 10])
        qn = sb("pj_qn", [P, 2, 512])
        kk = sb("pj_kk", [P, 2, 2, HD])
        ki4 = sb("pj_ki4", [P, 2, 4, ID])
        gk = sb("pj_gk", [P, HD])
        gki = sb("pj_gki", [P, ID])
        gqr = sb("pj_gqr", [2, HD])
        gq = sb("pj_gq", [P, 1])
        wl, gl = m.sem("pj_weights_loaded"), m.sem("pj_gains_loaded")
        qr, tokr, sqr, msr, rtr = (m.sem("pj_" + n) for n in ("qr_psum", "tok_copied", "squared", "mean", "root"))
        nr, tr, ev, chain = (m.sem("pj_" + n) for n in ("normalised", "transposed", "evacuated", "dve_chain"))
        up, ue, red = (m.sem("pj_" + n) for n in ("u_psum", "u_copied", "reduced"))
        vst = [m.sem(f"pj_v_stored{i}") for i in range(2)]
        kst = [m.sem(f"pj_k_stored{i}") for i in range(2)]
        gqt, gqe, qst = m.sem("pj_gq_transposed"), m.sem("pj_gq_copied"), m.sem("pj_q_stored")
        wsrc = A.w_in.rearrange("(k p) n -> p k n", p=P)
        with nc.Block() as block:
            @block.sync
            def _(sp):
                sp.dma_start(w[:, :, 512:1024], wsrc[:, :, 512:1024]).then_inc(wl, 16)
                sp.dma_start(w[:, :, 1024:1024 + RW], wsrc[:, :, 1024:OFF_GA]).then_inc(wl, 16)
                sp.dma_start(w[:, :, 0:512], wsrc[:, :, 0:512]).then_inc(wl, 16)
                sp.dma_start(gk[:, :], A.k_gain.broadcast_to([P, HD])).then_inc(gl, 16)
                sp.dma_start(gki[:, :], A.kidx_gain.broadcast_to([P, ID])).then_inc(gl, 16)
                sp.dma_start(gqr[:, :], A.q_gain.broadcast_to([2, HD])).then_inc(gl, 16)
                for t in range(TILES):
                    r = rows_of(t)
                    sl = slice(t * P, t * P + r)
                    vo = O.v_prompt[0, 0, sl, :] if t < PT else O.v_sample[0, 0, :, :]
                    ko = O.k_prompt[0, 0, sl, :] if t < PT else O.k_sample[0, 0, :, :]
                    kio = O.kidx_prompt[0, 0, sl, :] if t < PT else O.kidx_sample[0, 0, :, :]
                    sp.wait_ge(tokr, t + 1)
                    sp.dma_start(vo, tok[0:r, t % 2, V0:V0 + HD]).then_inc(vst[t % 2], 16)
                    sp.wait_ge(nr, t + 1)
                    sp.dma_start(ko, kk[0:r, t % 2, 0, :]).then_inc(kst[t % 2], 16)
                    sp.dma_start(kio, ki4[0:r, t % 2, 0, :]).then_inc(kst[t % 2], 16)
                sp.wait_ge(ev, TILES)
                sp.dma_start(m.q_dram, m.qT[:, :, :]).then_inc(qst, 16)
                sp.wait_ge(qst, 16)
                for i in range(2):
                    n = (TILES + 1 - i) // 2
                    sp.wait_ge(vst[i], 16 * n)
                    sp.wait_ge(kst[i], 32 * n)

            @block.tensor
            def _(pe):
                def transposes(t):
                    r = rows_of(t)
                    pe.wait_ge(nr, t + 1)
                    if t:
                        pe.wait_ge(ev, t)
                    for j in range(8):
                        src = (qn[0:r, t % 2, j * P:(j + 1) * P] if j < 4 else
                               m.tokqi[0:r, t % 2, (j - 4) * P:(j - 3) * P] if j < 6 else
                               (kk, ki4)[j - 6][0:r, t % 2, :, :].rearrange("p a d -> p (a d)"))
                        i = nc.tensor.transpose(m.ps[:, 6 + j // 4, (j % 4) * P:(j % 4) * P + r], src, m.ident[0:r, 0:r])
                    i.then_inc(tr, 1)

                pe.wait_ge(gl, 48)
                nc.tensor.transpose(m.ps[0:HD, 7, 0:2], gqr[:, :], m.ident[0:2, 0:2]).then_inc(gqt, 1)
                pe.wait_ge(gqe, 1)
                pe.wait_ge(wl, 48)
                for t in range(TILES):
                    r = rows_of(t)
                    if t >= 2:
                        pe.wait_ge(sqr, t - 1)
                    for k in range(KD):
                        nc.tensor.matmul(m.ps[0:r, 2 * (t % 2), :], m.hT[:, k, t * P:t * P + r], w[:, k, 512:1024],
                                         start=k == 0, stop=k == KD - 1)
                    for k in range(KD):
                        i = nc.tensor.matmul(m.ps[0:r, 2 * (t % 2) + 1, 0:RW], m.hT[:, k, t * P:t * P + r],
                                             w[:, k, 1024:1024 + RW], start=k == 0, stop=k == KD - 1)
                    i.then_inc(qr, 1)
                    if t >= 2:
                        pe.wait_ge(ue, t - 1)
                    for k in range(KD):
                        lhs = m.hT[:, k, t:SEQ:T] if t < T else m.hT[:, k, SEQ:NT]
                        i = nc.tensor.matmul(m.ps[0:r, 4 + t % 2, :], lhs, w[:, k, 0:512], start=k == 0, stop=k == KD - 1)
                    i.then_inc(up, 1)
                    if t:
                        transposes(t - 1)
                transposes(PT)

            @block.scalar
            def _(act):
                act.wait_ge(gqt, 1)
                nc.scalar.copy(gq[0:HD, :], m.ps[0:HD, 7, 0:1])
                nc.scalar.copy(gq[HD:P, :], m.ps[0:HD, 7, 1:2]).then_inc(gqe, 1)
                for t in range(TILES):
                    r = rows_of(t)
                    act.wait_ge(qr, t + 1)
                    if t >= 2:
                        act.wait_ge(nr, t - 1)
                        act.wait_ge(vst[t % 2], 16 * (t // 2))
                        act.wait_ge(tr, t - 1)
                    b = 2 * (t % 2)
                    nc.scalar.copy(tok[0:r, t % 2, 0:512], m.ps[0:r, b, :])
                    nc.scalar.copy(m.tokqi[0:r, t % 2, :], m.ps[0:r, b + 1, 128:384])
                    nc.scalar.copy(tok[0:r, t % 2, 512:TW], m.ps[0:r, b + 1, 0:RW]).then_inc(tokr, 1)
                    if t:
                        act.wait_ge(red, t)
                    nc.scalar.activation(sq[0:r, 0:512], m.ps[0:r, b, :], ACT.Square)
                    nc.scalar.activation(sq[0:r, 512:576], m.ps[0:r, b + 1, 0:64], ACT.Square)
                    nc.scalar.activation(sq[0:r, 576:608], m.ps[0:r, b + 1, 384:416], ACT.Square).then_inc(sqr, 1)
                    act.wait_ge(msr, t + 1)
                    nc.scalar.activation(st[0:r, t, 2, :], st[0:r, t, 1, :], ACT.Sqrt).then_inc(rtr, 1)
                    act.wait_ge(up, t + 1)
                    src = m.ps[0:r, 4 + t % 2, :]
                    if t < T:
                        i = nc.scalar.copy(m.u[:, :, t, :], src.rearrange("c (g j) -> c g j", j=J))
                    else:
                        i = nc.scalar.copy(m.us[:, :], src)
                    i.then_inc(ue, 1)

            @block.vector
            def _(dve):
                step = Chain(dve, chain)

                def evacuate(t):
                    r = rows_of(t)
                    sl = slice(t * P, t * P + r)
                    dve.wait_ge(tr, t + 1)
                    a = m.ps[:, 6, :].rearrange("p (j t) -> p j t", t=P)
                    b = m.ps[:, 7, :].rearrange("p (j t) -> p j t", t=P)
                    nc.vector.tensor_scalar(m.qT[:, :, sl], a[:, :, 0:r], gq[:, 0:1], None, ALU.mult)
                    nc.vector.tensor_copy(m.qiT[:, :, sl], b[:, 0:2, 0:r])
                    nc.vector.tensor_copy(m.kT[:, sl], b[:, 2, 0:r])
                    nc.vector.tensor_copy(m.kiT[:, sl], b[:, 3, 0:r]).then_inc(ev, 1)

                dve.wait_ge(gl, 48)
                dve.wait_ge(gqe, 1)
                for t in range(TILES):
                    r = rows_of(t)
                    dve.wait_ge(sqr, t + 1)
                    ss, ms, rt, rs = (st[0:r, t, j, :] for j in range(4))
                    nc.vector.tensor_reduce(ss[:, 0:9], sq[0:r, 0:576].rearrange("p (h d) -> p h d", d=HD), AX.X, ALU.add)
                    i = nc.vector.tensor_reduce(ss[:, 9:10], sq[0:r, 576:608], AX.X, ALU.add)
                    i.then_inc(red, 1)
                    dve.wait_ge(red, t + 1)
                    nc.vector.tensor_scalar(ms[:, 0:9], ss[:, 0:9], 1.0 / HD, EPS, ALU.mult, ALU.add)
                    nc.vector.tensor_scalar(ms[:, 9:10], ss[:, 9:10], 1.0 / ID, EPS, ALU.mult, ALU.add).then_inc(msr, 1)
                    dve.wait_ge(rtr, t + 1)
                    step(nc.vector.reciprocal(rs, rt))
                    if t >= 2:
                        dve.wait_ge(tr, t - 1)
                        dve.wait_ge(kst[t % 2], 32 * (t // 2))
                    row = tok[0:r, t % 2, :]
                    nc.vector.tensor_tensor(qn[0:r, t % 2, :].rearrange("p (h d) -> p h d", d=HD),
                                            row[:, 0:512].rearrange("p (h d) -> p h d", d=HD),
                                            bc(rs[:, 0:8], 2, HD), ALU.mult)
                    nc.vector.scalar_tensor_tensor(kk[0:r, t % 2, :, :], bc(row[:, K0:K0 + HD], 1, 2), rs[:, 8:9],
                                                   bc(gk[0:r, :], 1, 2), ALU.mult, ALU.mult)
                    nc.vector.scalar_tensor_tensor(ki4[0:r, t % 2, :, :], bc(row[:, KI0:KI0 + ID], 1, 4), rs[:, 9:10],
                                                   bc(gki[0:r, :], 1, 4), ALU.mult, ALU.mult)
                    nc.vector.tensor_scalar(m.wi[0:r, t, :], row[:, WI0:WI0 + IH], (IH * ID) ** -0.5, None, ALU.mult)
                    vd = m.v[:, t, :] if t < PT else m.vs[0:DEC, CB, :]
                    nc.vector.tensor_copy(vd, row[:, V0:V0 + HD]).then_inc(nr, 1)
                    if t:
                        evacuate(t - 1)
                evacuate(PT)


def cache_keys(nc, m, A):
    with ExitStack() as ctx:
        sb = lambda name, shape: ctx.enter_context(nc.sbuf_tensor(name, shape, F32))
        ck = sb("ck_k", [P, CB, HD])
        cki = sb("ck_ki", [P, CB, ID])
        kk = sb("ck_kk", [P, CB, 2, HD])
        ki4 = sb("ck_ki4", [P, CB, 4, ID])
        ld, dup, tr, ev = (m.sem("ck_" + n) for n in ("loaded", "repeated", "transposed", "evacuated"))
        with nc.Block() as block:
            @block.sync
            def _(sp):
                sp.dma_start(ck[:, :, :], A.cache_k[0].rearrange("(b p) d -> p b d", p=P)).then_inc(ld, 16)
                sp.dma_start(cki[:, :, :], A.cache_kidx[0].rearrange("(b p) d -> p b d", p=P)).then_inc(ld, 16)
                sp.dma_start(m.vs[:, 0:CB, :], A.cache_v[0].rearrange("(b p) d -> p b d", p=P)).then_inc(ld, 16)

            @block.vector
            def _(dve):
                dve.wait_ge(ld, 48)
                nc.vector.tensor_copy(m.kTs[:, PAST:], m.kT[:, SEQ:NT])
                nc.vector.tensor_copy(m.kiTs[:, PAST:], m.kiT[:, SEQ:NT])
                nc.vector.tensor_copy(kk[:, :, :, :], bc(ck[:, :, :], 2, 2))
                nc.vector.tensor_copy(ki4[:, :, :, :], bc(cki[:, :, :], 2, 4)).then_inc(dup, 1)
                for g in range(2 * CB // 4):
                    dve.wait_ge(tr, g + 1)
                    dst = (m.kTs, m.kiTs)[g // 4][:, (g % 4) * 512:(g % 4 + 1) * 512]
                    nc.vector.tensor_copy(dst, m.ps[:, g % 4, :]).then_inc(ev, 1)

            @block.tensor
            def _(pe):
                pe.wait_ge(dup, 1)
                for g in range(2 * CB // 4):
                    if g >= 4:
                        pe.wait_ge(ev, g - 3)
                    for j in range(4):
                        b = (g % 4) * 4 + j
                        src = (kk, ki4)[g // 4][:, b, :, :].rearrange("p a d -> p (a d)")
                        i = nc.tensor.transpose(m.ps[:, g % 4, j * P:(j + 1) * P], src, m.ident[:, :])
                    i.then_inc(tr, 1)


ADA_FIRST = 4
TWO_PI_HI = 6.28125
TWO_PI_MID = 0.0019350051879882812
TWO_PI_LO = 2 * math.pi - TWO_PI_HI - TWO_PI_MID
ROUND = 1.5 * 2.0 ** 23
PI_BELOW = 3.1415925


class ComplexSteps:

    def __init__(self, nc, step):
        self.nc, self.step = nc, step

    def mul(self, out_re, out_im, a_re, a_im, b_re, b_im, tmp, negate_im=False):
        v, step = self.nc.vector, self.step
        step(v.tensor_tensor(tmp, a_re, b_re, ALU.mult))
        step(v.tensor_tensor(out_re, a_im, b_im, ALU.mult))
        step(v.tensor_tensor(out_re, tmp, out_re, ALU.subtract))
        step(v.tensor_tensor(tmp, a_re, b_im, ALU.mult))
        step(v.tensor_tensor(out_im, a_im, b_re, ALU.mult))
        step(v.tensor_tensor(out_im, tmp, out_im, ALU.add))
        if negate_im:
            step(v.tensor_scalar(out_im, out_im, -1.0, None, ALU.mult))


def ssm_parameters(nc, m, A):
    AC = 256
    ada = range(2 * D // AC, 6 * D // AC)
    wada = A.w_ada.rearrange("(k p) n -> p k n", p=P)
    with ExitStack() as ctx:
        sb = lambda name, shape: ctx.enter_context(nc.sbuf_tensor(name, shape, F32))
        rows = sb("sp_rows", [PAIR, 5, P])
        ldt = sb("sp_logdt", [PAIR, 2])
        prm = sb("sp_prm", [P, 5, PAIR])
        cin = sb("sp_c", [P, 2, 2, P])
        cT = sb("sp_cT", [P, 2, PAIR, J])
        b = sb("sp_b", [P, 2, PAIR, J])
        bb = sb("sp_bb", [P, 2, PAIR, J])
        s = sb("sp_small", [P, 24, PAIR])
        pw = sb("sp_powers", [P, 2, PAIR, T + 1])
        idle = m.zT[:, :, :].rearrange("p a n -> p (a n)")
        wt = idle[:, 0:2 * PAIR * P].rearrange("p (c q t j) -> p c q t j", c=2, q=PAIR, t=T)
        tmp = sb("sp_tmp", [P, PAIR * NCH // 2])
        ksb = idle[0:J, 0:G * P].rearrange("j (g n) -> j g n", g=G)
        dd = m.tokqi[0:J, :, :].rearrange("j a n -> j (a n)").rearrange("j (g i) -> j g i", g=G)
        ld, lc = m.sem("sp_loaded"), m.sem("sp_c_loaded")
        ldp, chain, tr, trd = m.sem("sp_dt_rows"), m.sem("sp_dve_chain"), m.sem("sp_transposed"), m.sem("sp_copied")
        a1, a2, a3, th, trig = m.sem("sp_dt"), m.sem("sp_decays"), m.sem("sp_adt"), m.sem("sp_angles"), m.sem("sp_trig")
        aw = sb("sp_ada_w", [P, 2, KD, AC])
        ab = sb("sp_ada_b", [1, 2, AC])
        arow = idle[0:2, G * P:G * P + AC]
        awl = [m.sem(f"sp_ada_w_loaded{i}") for i in range(2)]
        ast, aps, aev = m.sem("sp_ada_stored"), m.sem("sp_ada_psum"), m.sem("sp_ada_copied")
        wtr, wps, wev, kps, kev, mz, mst, bbr = (m.sem("sp_" + n) for n in (
            "wt_ready", "w_psum", "w_copied", "k_psum", "k_ready", "m_zeroed", "m_stored", "bb_ready"))
        (dt, adt, ang, ang8, dec, n1, r1, sn, cs, n8, rr8, sn8, cs8, num, den, rden, t1, cr, ci, ab1, ab8) = \
            (s[:, j, :] for j in range(21))
        ar, ai, h0r, h0i, ldtT = (prm[:, j, :] for j in range(5))
        with nc.Block() as block:
            @block.sync
            def _(sp):
                for j, a in enumerate((A.ssm_a_re, A.ssm_a_im)):
                    sp.dma_start(rows[:, j, :], a.rearrange("(q g) p -> q (g p)", g=2)).then_inc(ld, 16)
                for j, a in enumerate((A.state_ssm_re, A.state_ssm_im)):
                    sp.dma_start(rows[:, 2 + j, :], a[0].rearrange("(q g) p -> q (g p)", g=2)).then_inc(ld, 16)
                sp.dma_start(ldt[:, :], A.ssm_log_dt.rearrange("(q g) -> q g", g=2)).then_inc(ld, 16)
                for j, a in enumerate((A.ssm_b_re, A.ssm_b_im)):
                    sp.dma_start(b[:, j, :, :], a.rearrange("(q g) p j -> (g p) q j", g=2)).then_inc(lc, 16)
                for j, a in enumerate((A.ssm_c_re, A.ssm_c_im)):
                    for q in range(PAIR):
                        dst = cin[J * (q % 8):J * (q % 8 + 1), j, q // 8, :].rearrange("j (g p) -> j g p", g=2)
                        sp.dma_start(dst, a[2 * q:2 * q + 2].rearrange("g j p -> j g p")).then_inc(lc, 16)
                sp.dma_start(dd[:, :, :].rearrange("j g i -> j (g i)"),
                             A.ssm_d.rearrange("(o n) -> o n", o=1).broadcast_to([J, 512])).then_inc(lc, 16)
                for i, j in enumerate(ada):
                    if i >= 2:
                        sp.wait_ge(aps, i - 1)
                    sp.dma_start(aw[:, i % 2, :, :], wada[:, :, j * AC:(j + 1) * AC]).then_inc(awl[i % 2], 16)
                    sp.dma_start(ab[:, i % 2, :], A.b_ada[:, j * AC:(j + 1) * AC]).then_inc(awl[i % 2], 16)
                sp.wait_ge(mz, 1)
                sp.wait_ge(kev, 1)
                for p in range(T):
                    sp.dma_start(m.M[J * p:J * (p + 1), :, J * p:P], ksb[:, :, 0:P - J * p]).then_inc(mst, 16)
                sp.wait_ge(mst, 16 * T)

            @block.gpsimd
            def _(pool):
                nc.gpsimd.memset(m.M[:, :, :], 0.0).then_inc(mz, 1)

            @block.tensor
            def _(pe):
                pe.wait_ge(ldp, 1)
                for j in range(5):
                    nc.tensor.transpose(m.ps[:, 0, PAIR * j:PAIR * (j + 1)], rows[:, j, :], m.ident[0:PAIR, 0:PAIR])
                pe.wait_ge(lc, 16 * (3 + 2 * PAIR))
                for j in range(4):
                    i = nc.tensor.transpose(m.ps[:, 1, P * j:P * (j + 1)], cin[:, j // 2, j % 2, :], m.ident[:, :])
                i.then_inc(tr, 1)
                for i, j in enumerate(ada):
                    pe.wait_ge(awl[i % 2], 32 * (i // 2 + 1))
                    if i >= 2:
                        pe.wait_ge(aev, i - 1)
                    for k in range(KD):
                        nc.tensor.matmul(m.ps[0:2, 6 + i % 2, 0:AC], m.cT[:, k, :], aw[:, i % 2, k, :], start=k == 0, stop=False)
                    nc.tensor.matmul(m.ps[0:2, 6 + i % 2, 0:AC], m.ones[0:1, 0:2], ab[0:1, i % 2, :],
                                     start=False, stop=True).then_inc(aps, 1)
                pe.wait_ge(aev, len(ada))
                pe.wait_ge(wtr, 1)
                for x in range(8):
                    for y in range(4):
                        n = 4 * x + y
                        i = nc.tensor.transpose(m.ps[:, x, P * y:P * (y + 1)],
                                                wt[:, n // PAIR, n % PAIR, :, :].rearrange("p t j -> p (t j)"), m.ident[:, :])
                    i.then_inc(wps, 1)
                pe.wait_ge(bbr, 1)
                for x in range(4):
                    pe.wait_ge(wev, 2 * x + 2)
                    for g in range(8 * x, 8 * x + 8):
                        h = slice(ST * (g % 2), ST * (g % 2 + 1))
                        y = (g % 8) // 2
                        for c in range(2):
                            i = nc.tensor.matmul(m.ps[0:J, 2 * x + g % 2, P * y:P * (y + 1)], bb[h, c, g // 2, :],
                                                 m.V[h, c, g // 2, 0:T, :].rearrange("p t i -> p (t i)"),
                                                 start=c == 0, stop=c == 1)
                    i.then_inc(kps, 1)

            @block.scalar
            def _(act):
                act.wait_ge(trd, 1)
                nc.scalar.activation(dt, ldtT, ACT.Exp).then_inc(a1, 1)
                act.wait_ge(a3, 1)
                nc.scalar.activation(dec, adt, ACT.Exp)
                nc.scalar.activation(m.r8[:, :], adt, ACT.Exp, scale=float(T)).then_inc(a2, 1)
                act.wait_ge(th, 1)
                nc.scalar.activation(sn, r1, ACT.Sin)
                nc.scalar.activation(cs, ab1, ACT.Sin)
                nc.scalar.activation(sn8, rr8, ACT.Sin)
                nc.scalar.activation(cs8, ab8, ACT.Sin).then_inc(trig, 1)
                for i, j in enumerate(ada):
                    act.wait_ge(aps, i + 1)
                    if i:
                        act.wait_ge(ast, 16 * i)
                    nc.scalar.copy(arow, m.ps[0:2, 6 + i % 2, 0:AC]).then_inc(aev, 1)
                    act.wait_ge(aev, i + 1)
                    nc.scalar.dma_start(m.mod_dram[:, j * AC:(j + 1) * AC], arow).then_inc(ast, 16)
                act.wait_ge(ast, 16 * len(ada))

            @block.vector
            def _(dve):
                step = Chain(dve, chain)
                cx = ComplexSteps(nc, step)
                v = nc.vector
                dve.wait_ge(ld, 80)
                v.tensor_copy(rows[:, 4, :].rearrange("q (g p) -> q g p", g=2), bc(ldt[:, :], 2, ST)).then_inc(ldp, 1)
                dve.wait_ge(tr, 1)
                v.tensor_copy(prm[:, :, :], m.ps[:, 0, 0:5 * PAIR].rearrange("p (a q) -> p a q", a=5)).then_inc(trd, 1)
                step(v.tensor_copy(cT[:, :, :, :].rearrange("p a q j -> p (a q j)"), m.ps[:, 1, :]))
                dve.wait_ge(trd, 1)
                dve.wait_ge(a1, 1)
                v.tensor_tensor(adt, ar, dt, ALU.mult).then_inc(a3, 1)
                step(v.tensor_tensor(ang, ai, dt, ALU.mult))
                step(v.tensor_scalar(ang8, ang, float(T), None, ALU.mult))
                for angle, turns, red, quarter in ((ang, n1, r1, ab1), (ang8, n8, rr8, ab8)):
                    step(v.tensor_scalar(turns, angle, 1.0 / (2 * math.pi), ROUND, ALU.mult, ALU.add))
                    step(v.tensor_scalar(turns, turns, -ROUND, None, ALU.add))
                    step(v.scalar_tensor_tensor(red, turns, -TWO_PI_HI, angle, ALU.mult, ALU.add))
                    step(v.scalar_tensor_tensor(red, turns, -TWO_PI_MID, red, ALU.mult, ALU.add))
                    step(v.scalar_tensor_tensor(red, turns, -TWO_PI_LO, red, ALU.mult, ALU.add))
                    step(v.tensor_scalar(red, red, PI_BELOW, -PI_BELOW, ALU.min, ALU.max))
                    step(v.scalar_tensor_tensor(quarter, red, -1.0, red, ALU.mult, ALU.max))
                    i = v.tensor_scalar(quarter, quarter, -1.0, math.pi / 2, ALU.mult, ALU.add)
                    if angle is ang:
                        step(i)
                i.then_inc(th, 1)
                dve.wait_ge(trig, 1)
                dve.wait_ge(a2, 1)
                pr, pi = pw[:, 0, :, :], pw[:, 1, :, :]
                v.memset(pr[:, :, 0], 1.0)
                v.memset(pi[:, :, 0], 0.0)
                step(v.tensor_tensor(pr[:, :, 1], dec, cs, ALU.mult))
                step(v.tensor_tensor(pi[:, :, 1], dec, sn, ALU.mult))
                for n in (1, 2, 4):
                    tv = tmp[:, 0:PAIR * n].rearrange("p (q n) -> p q n", n=n)
                    cx.mul(pr[:, :, n + 1:2 * n + 1], pi[:, :, n + 1:2 * n + 1], pr[:, :, 1:n + 1], pi[:, :, 1:n + 1],
                           pr[:, :, n:n + 1].broadcast_to([P, PAIR, n]), pi[:, :, n:n + 1].broadcast_to([P, PAIR, n]), tv)
                lr, li = pr[:, :, 1], pi[:, :, 1]
                step(v.tensor_scalar(num, lr, -1.0, None, ALU.add))
                step(v.tensor_tensor(den, ar, ar, ALU.mult))
                step(v.tensor_tensor(t1, ai, ai, ALU.mult))
                step(v.tensor_tensor(den, den, t1, ALU.add))
                step(v.reciprocal(rden, den))
                step(v.tensor_tensor(cr, num, ar, ALU.mult))
                step(v.tensor_tensor(t1, li, ai, ALU.mult))
                step(v.tensor_tensor(cr, cr, t1, ALU.add))
                step(v.tensor_tensor(cr, cr, rden, ALU.mult))
                step(v.tensor_tensor(ci, li, ar, ALU.mult))
                step(v.tensor_tensor(t1, num, ai, ALU.mult))
                step(v.tensor_tensor(ci, ci, t1, ALU.subtract))
                step(v.tensor_tensor(ci, ci, rden, ALU.mult))
                dve.wait_ge(lc, 16 * (3 + 2 * PAIR))
                tv = tmp[:, 0:PAIR * J].rearrange("p (q j) -> p q j", j=J)
                cx.mul(bb[:, 0, :, :], bb[:, 1, :, :], bc(cr, 2, J), bc(ci, 2, J), b[:, 0, :, :], b[:, 1, :, :], tv)
                for q4 in range(4):
                    q = slice(4 * q4, 4 * q4 + 4)
                    tv = tmp[:, 0:4 * T * J].rearrange("p (q t j) -> p q t j", q=4, t=T)
                    rev = pw[:, :, q, T - 1::-1]
                    cx.mul(wt[:, 0, q], wt[:, 1, q], bc(rev[:, 0], 3, J), bc(rev[:, 1], 3, J),
                           bc(bb[:, 0, q, :], 2, T), bc(bb[:, 1, q, :], 2, T), tv)
                v.tensor_copy(s[:, 21, 0:1], wt[:, 0, 0, 0, 0:1]).then_inc(wtr, 1)
                for q4 in range(4):
                    q = slice(4 * q4, 4 * q4 + 4)
                    tv = tmp[:, 0:4 * (T + 1) * J].rearrange("p (q t j) -> p q t j", q=4, t=T + 1)
                    cx.mul(m.V[:, 0, q], m.V[:, 1, q], bc(pr[:, q, :], 3, J), bc(pi[:, q, :], 3, J),
                           bc(cT[:, 0, q, :], 2, T + 1), bc(cT[:, 1, q, :], 2, T + 1), tv, negate_im=True)
                v.tensor_copy(s[:, 22, 0:1], wt[:, 0, 0, 0, 0:1]).then_inc(bbr, 1)
                for x in range(8):
                    dve.wait_ge(wps, x + 1)
                    v.tensor_copy(m.W[:, x // 4, 4 * (x % 4):4 * (x % 4) + 4, :].rearrange("p q n -> p (q n)"),
                                  m.ps[:, x, :]).then_inc(wev, 1)
                tc, ts = m.rot[:, 0, :, :], m.rot[:, 1, :, :]
                v.memset(tc[:, :, 0], 1.0)
                v.memset(ts[:, :, 0], 0.0)
                step(v.tensor_copy(tc[:, :, 1], cs8))
                step(v.tensor_copy(ts[:, :, 1], sn8))
                n = 1
                while n < NCH:
                    tv = tmp[:, 0:PAIR * n].rearrange("p (q n) -> p q n", n=n)
                    cx.mul(tc[:, :, n + 1:2 * n + 1], ts[:, :, n + 1:2 * n + 1], tc[:, :, 1:n + 1], ts[:, :, 1:n + 1],
                           tc[:, :, n:n + 1].broadcast_to([P, PAIR, n]), ts[:, :, n:n + 1].broadcast_to([P, PAIR, n]), tv)
                    n *= 2
                v.tensor_copy(m.rot[:, :, :, S0:COLS], m.rot[:, :, :, 0:COLS - S0])
                step(v.tensor_copy(m.decay[:, :, :], bc(m.r8[:, :], 2, COLS)))
                v.memset(m.decay[:, :, 0], 0.0)
                v.memset(m.decay[:, :, S0], 0.0)
                v.tensor_copy(m.h0[:, :, :], prm[:, 2:4, :])
                i = v.tensor_tensor(dd[:, :, :], dd[:, :, :], bc(m.ident[0:J, 0:J], 1, G), ALU.mult)
                step(i)
                for x in range(8):
                    dve.wait_ge(kps, x // 2 + 1)
                    g0 = 8 * (x // 2) + x % 2
                    i = v.tensor_copy(ksb[:, g0:min(g0 + 8, G):2, :], m.ps[0:J, x, :].rearrange("j (g n) -> j g n", n=P))
                step(i)
                v.tensor_tensor(ksb[:, :, 0:J], ksb[:, :, 0:J], dd[:, :, :], ALU.add).then_inc(kev, 1)


def ssm_scan(nc, m, A, O):
    GQ, PQ = G // 4, PAIR // 4
    with ExitStack() as ctx:
        sb = lambda name, shape: ctx.enter_context(nc.sbuf_tensor(name, shape, F32))
        us = sb("sc_us", [SCH, GQ, T, J])
        uT = sb("sc_uT", [P, 2, GQ, COLS])
        z = sb("sc_z", [P, 4, PQ, COLS])
        hh = sb("sc_h", [P, 2, 2, PQ, COLS])
        yso = sb("sc_ys", [SCH, T, P])
        y = [m.u[:, GQ * q:GQ * (q + 1), :, :].rearrange("c g t i -> c (g t i)").rearrange("c (t n) -> c t n", t=T)
             for q in range(4)]
        h1 = sb("sc_seen", [P, 1])
        last = sb("sc_last", [P, 4, PAIR])
        lastT = m.tokqi[0:PAIR, :, :].rearrange("q a n -> q (a n)").rearrange("q (a n) -> q a n", a=4)
        usd, usl = m.sem("sc_us_stored"), m.sem("sc_us_loaded")
        up, ue, zp, chain, hr, yp, ye, ypt, zte, fin, fp, fe, fst, zero = (m.sem("sc_" + n) for n in (
            "u_transposed", "u_copied", "z_psum", "dve_chain", "h_ready", "y_psum", "y_gelu", "y_transposed",
            "zT_copied", "last_ready", "last_transposed", "last_copied", "last_stored", "zeroed"))
        zc = m.sem("sc_z_copied")
        with nc.Block() as block:
            @block.sync
            def _(sp):
                sp.dma_start(m.us_dram, m.us[:, :]).then_inc(usd, 16)
                sp.wait_ge(usd, 16)
                for q in range(4):
                    if q:
                        sp.wait_ge(up, q)
                    for g in range(GQ):
                        c = q * P + g * J
                        sp.dma_start(us[:, g, :, :], m.us_dram.rearrange("(c s) n -> c s n", s=T)[:, :, c:c + J]) \
                            .then_inc(usl, 16)
                sp.wait_ge(fe, 1)
                for j, o in enumerate((O.ssm_re_prompt, O.ssm_im_prompt, O.ssm_re_sample, O.ssm_im_sample)):
                    sp.dma_start(o[0, 0].rearrange("(q g) p -> q (g p)", g=2), lastT[:, j, :]).then_inc(fst, 16)
                sp.wait_ge(fst, 64)

            @block.tensor
            def _(pe):
                def inputs(q):
                    pe.wait_ge(usl, 16 * GQ * (q + 1))
                    if q:
                        pe.wait_ge(zc, q)
                    for g in range(GQ):
                        src = m.u[:, GQ * q + g, :, :].rearrange("c t j -> c (t j)")
                        nc.tensor.transpose(m.ps[:, g // 4, (g % 4) * P:(g % 4 + 1) * P], src, m.ident[:, :])
                    for g in range(GQ):
                        i = nc.tensor.transpose(m.ps[:, 2, g * SCH:(g + 1) * SCH], us[:, g, :, :].rearrange("c t j -> c (t j)"),
                                                m.ident[0:SCH, 0:SCH])
                    i.then_inc(up, 1)
                    pe.wait_ge(ue, q + 1)
                    for c in range(2):
                        for n in range(PQ):
                            x = PQ * c + n
                            for g in range(2):
                                i = nc.tensor.matmul(
                                    m.ps[ST * g:ST * (g + 1), x // 3, (x % 3) * COLS:(x % 3 + 1) * COLS],
                                    m.W[:, c, PQ * q + n, ST * g:ST * (g + 1)], uT[:, q % 2, 2 * n + g, :], start=True, stop=True)
                    i.then_inc(zp, 1)

                def outputs(q):
                    pe.wait_ge(hr, q + 1)
                    if q:
                        pe.wait_ge(zte, q)
                    for smp in range(2):
                        lo, rows, bank = ((0, NCH, 3), (S0, SCH, 5))[smp]
                        for g in range(GQ):
                            h = slice(ST * (g % 2), ST * (g % 2 + 1))
                            out = m.ps[0:rows, bank + g % 2, (g // 2) * P:(g // 2 + 1) * P]
                            nc.tensor.matmul(out, uT[:, q % 2, g, lo + 1:lo + 1 + rows], m.M[:, GQ * q + g, :],
                                             start=True, stop=False)
                            for c in range(2):
                                i = nc.tensor.matmul(out, hh[h, q % 2, c, g // 2, lo:lo + rows],
                                                     m.V[h, c, PQ * q + g // 2, 1:T + 1, :].rearrange("p t i -> p (t i)"),
                                                     start=False, stop=c == 1)
                    i.then_inc(yp, 1)
                    pe.wait_ge(ye, q + 1)
                    for t in range(T):
                        nc.tensor.transpose(m.ps[:, 3 + t // 4, (t % 4) * P:(t % 4 + 1) * P], y[q][:, t, :], m.ident[:, :])
                    for t in range(T):
                        i = nc.tensor.transpose(m.ps[:, 5, t * SCH:(t + 1) * SCH], yso[:, t, :], m.ident[0:SCH, 0:SCH])
                    i.then_inc(ypt, 1)

                pe.wait_ge(zero, 1)
                inputs(0)
                inputs(1)
                for q in range(4):
                    outputs(q)
                    if q + 2 < 4:
                        inputs(q + 2)
                pe.wait_ge(fin, 1)
                for j in range(4):
                    i = nc.tensor.transpose(m.ps[0:PAIR, 7, j * P:(j + 1) * P], last[:, j, :], m.ident[:, :])
                i.then_inc(fp, 1)

            @block.scalar
            def _(act):
                def inputs(q):
                    act.wait_ge(up, q + 1)
                    for x in range(2):
                        nc.scalar.copy(uT[:, q % 2, 4 * x:4 * x + 4, 1:NCH + 1], m.ps[:, x, :].rearrange("p (g c) -> p g c", g=4))
                    nc.scalar.copy(uT[:, q % 2, :, S0 + 1:COLS],
                                   m.ps[:, 2, 0:GQ * SCH].rearrange("p (g c) -> p g c", g=GQ)).then_inc(ue, 1)

                act.wait_ge(zero, 1)
                inputs(0)
                inputs(1)
                for q in range(4):
                    act.wait_ge(yp, q + 1)
                    for x in range(2):
                        src = lambda b, r: m.ps[0:r, b + x, :].rearrange("c (g t i) -> c t g i", g=4, t=T)
                        dst = lambda o: o.rearrange("c t (g i) -> c t g i", i=J)[:, :, x:GQ:2, :]
                        nc.scalar.activation(dst(y[q]), src(3, P), ACT.Gelu_apprx_tanh)
                        i = nc.scalar.activation(dst(yso[:, :, :]), src(5, SCH), ACT.Gelu_apprx_tanh)
                    i.then_inc(ye, 1)
                    act.wait_ge(ypt, q + 1)
                    for x in range(2):
                        nc.scalar.copy(m.zT[:, q, 0:SEQ].rearrange("p (c t) -> p t c", t=T)[:, 4 * x:4 * x + 4, :],
                                       m.ps[:, 3 + x, :].rearrange("p (t c) -> p t c", t=4))
                    nc.scalar.copy(m.zT[:, q, SEQ:NT].rearrange("p (c t) -> p t c", t=T),
                                   m.ps[:, 5, 0:T * SCH].rearrange("p (t c) -> p t c", t=T)).then_inc(zte, 1)
                    if q + 2 < 4:
                        inputs(q + 2)

            @block.vector
            def _(dve):
                step = Chain(dve, chain)
                v = nc.vector
                for b in range(2):
                    v.memset(uT[:, b, :, 0], 0.0)
                    i = v.memset(uT[:, b, :, S0], 0.0)
                i.then_inc(zero, 1)
                for q in range(4):
                    dve.wait_ge(zp, q + 1)
                    zr, zi, tr, ti = (z[:, j, :, :] for j in range(4))
                    zf = z[:, 0:2, :, :].rearrange("p a q c -> p (a q c)")
                    step(v.tensor_copy(zf[:, 0:6 * COLS].rearrange("p (b c) -> p b c", b=2), m.ps[:, 0:2, 0:3 * COLS]))
                    step(v.tensor_copy(zf[:, 6 * COLS:8 * COLS], m.ps[:, 2, 0:2 * COLS]))
                    v.tensor_copy(h1[:, 0:1], zf[:, 8 * COLS - 1:8 * COLS]).then_inc(zc, 1)
                    qs = slice(PQ * q, PQ * (q + 1))
                    step(v.tensor_copy(z[:, 0:2, :, S0], m.h0[:, :, qs]))
                    rc, rs = m.rot[:, 0, qs, :], m.rot[:, 1, qs, :]
                    step(v.tensor_tensor(tr, zr, rc, ALU.mult))
                    step(v.tensor_tensor(ti, zi, rs, ALU.mult))
                    step(v.tensor_tensor(tr, tr, ti, ALU.add))
                    step(v.tensor_tensor(ti, zi, rc, ALU.mult))
                    step(v.tensor_tensor(zr, zr, rs, ALU.mult))
                    step(v.tensor_tensor(ti, ti, zr, ALU.subtract))
                    flat = lambda a: a.rearrange("p q c -> p (q c)")
                    dec = flat(m.decay[:, qs, :])
                    step(v.tensor_tensor_scan(flat(zr), dec, flat(tr), 0.0, ALU.mult, ALU.add))
                    step(v.tensor_tensor_scan(flat(zi), dec, flat(ti), 0.0, ALU.mult, ALU.add))
                    if q >= 2:
                        dve.wait_ge(yp, q - 1)
                    hre, him = hh[:, q % 2, 0, :, :], hh[:, q % 2, 1, :, :]
                    step(v.tensor_tensor(hre, zr, rc, ALU.mult))
                    step(v.tensor_tensor(ti, zi, rs, ALU.mult))
                    step(v.tensor_tensor(hre, hre, ti, ALU.subtract))
                    step(v.tensor_tensor(him, zi, rc, ALU.mult))
                    step(v.tensor_tensor(ti, zr, rs, ALU.mult))
                    step(v.tensor_tensor(him, him, ti, ALU.add))
                    v.tensor_copy(last[:, 0:2, qs], hh[:, q % 2, :, :, NCH])
                    v.tensor_copy(last[:, 2:4, qs], hh[:, q % 2, :, :, COLS - 1]).then_inc(hr, 1)
                dve.wait_ge(hr, 4)
                v.tensor_copy(last[:, :, 0:1], last[:, :, 0:1]).then_inc(fin, 1)
                dve.wait_ge(fp, 1)
                v.tensor_copy(lastT[:, :, :].rearrange("q a n -> q (a n)"), m.ps[0:PAIR, 7, :]).then_inc(fe, 1)


SEL = range(2, PT)
SC_COL = {t: P * sum(j + 1 for j in range(2, t)) for t in SEL}
SC_SAMPLE = P * sum(j + 1 for j in SEL)
SC_W = SC_SAMPLE + PAST + DEC
MK_COL = {t: P * sum(j + 1 for j in range(t)) for t in range(PT)}
MK_SAMPLE = P * sum(j + 1 for j in range(PT))
MK_W = MK_SAMPLE + PAST + DEC


def keys_of(t):
    return (P * (t + 1), MK_COL[t]) if t < PT else (PAST + DEC, MK_SAMPLE)


def pieces(n, size=1024):
    return [(k, min(size, n - k)) for k in range(0, n, size)]


def index_scores(nc, m):
    units = [(t, k, w) for t in SEL for k, w in pieces(P * (t + 1))] + [(PT, k, w) for k, w in pieces(PAST + DEC)]
    with ExitStack() as ctx:
        relu = ctx.enter_context(nc.sbuf_tensor("ix_relu", [P, 4, 1024], F32))
        ps, free, rl, acc, chain = (m.sem("ix_" + n) for n in ("psum", "psum_free", "relu", "added", "dve_chain"))
        with nc.Block() as block:
            @block.tensor
            def _(pe):
                n = 0
                for t, k0, w in units:
                    r = rows_of(t)
                    src = m.kiT if t < PT else m.kiTs
                    for h in range(IH):
                        q = slice(ID * (h % 4), ID * (h % 4 + 1))
                        if n >= 4:
                            pe.wait_ge(rl, n - 3)
                        for c, (k, x) in enumerate(pieces(w, 512)):
                            i = nc.tensor.matmul(m.ps[0:r, 2 * (h % 4) + c, 0:x], m.qiT[q, h // 4, t * P:t * P + r],
                                                 src[q, k0 + k:k0 + k + x], start=True, stop=True)
                        i.then_inc(ps, 1)
                        n += 1

            @block.scalar
            def _(act):
                n = 0
                for t, k0, w in units:
                    r = rows_of(t)
                    for h in range(IH):
                        act.wait_ge(ps, n + 1)
                        if n >= 4:
                            act.wait_ge(acc, n - 3)
                        src = m.ps[0:r, 2 * (h % 4):2 * (h % 4) + 2, :].rearrange("p b n -> p (b n)")
                        nc.scalar.activation(relu[0:r, n % 4, 0:w], src[:, 0:w], ACT.Relu).then_inc(rl, 1)
                        n += 1

            @block.vector
            def _(dve):
                step = Chain(dve, chain)
                n = 0
                for t, k0, w in units:
                    r = rows_of(t)
                    c = (SC_COL[t] if t < PT else SC_SAMPLE) + k0
                    sc = m.sc[0:r, c:c + w]
                    for h in range(IH):
                        dve.wait_ge(rl, n + 1)
                        wt = m.wi[0:r, t, h:h + 1]
                        if h == 0:
                            i = nc.vector.tensor_scalar(sc, relu[0:r, n % 4, 0:w], wt, None, ALU.mult)
                        else:
                            i = nc.vector.scalar_tensor_tensor(sc, relu[0:r, n % 4, 0:w], wt, sc, ALU.mult, ALU.add)
                        i.then_inc(acc, 1)
                        dve.wait_ge(acc, n + 1)
                        n += 1
                    if t < PT:
                        nc.vector.memset(m.sc[0:DEC, c + w - DEC:c + w], NEG)


SPANS = ((0, 512), (512, 512), (1024, DEC))


def select_keys_and_gates(nc, m, A):
    GB, GA, GG, GV = range(4)
    NB = 2
    units = [(c, lo, n) for c in range(KD) for lo, n in SPANS]
    kp = lambda a: a.rearrange("(k p) n -> p k n", p=P)
    parts = ((GB, 0, KD, kp(A.w_in), OFF_GB, m.hT), (GA, 8, KD, kp(A.w_in), OFF_GA, m.hT),
             (GG, 16, 4, kp(A.w_glu), D, m.zT), (GV, 20, 4, kp(A.w_glu), 0, m.zT))
    NL = len(SEL) + 1
    lists = [(P, SC_COL[t], P * (t + 1), MK_COL[t]) for t in SEL] + [(DEC, SC_SAMPLE, PAST + DEC, MK_SAMPLE)]
    with ExitStack() as ctx:
        sb = lambda name, shape, dt=F32: ctx.enter_context(nc.sbuf_tensor(name, shape, dt))
        thr = sb("tk_thr", [P, NL], I32)
        cand = sb("tk_cand", [P, NL], I32)
        neg = sb("tk_neg", [P, NL])
        negi = sb("tk_negi", [P, NL], I32)
        take = sb("tk_take", [P, NL], I32)
        cnt = sb("tk_cnt", [P, NL])
        bit = sb("tk_bit", [P, 1], I32)
        hits = sb("tk_hits", [P, PAST + DEC], BF16)
        eq = sb("tk_eq", [P, PAST + DEC])
        pre = sb("tk_pre", [P, PAST + DEC])
        w = sb("gt_w", [P, NB, 24, P])
        sga = sb("gt_sig_a", [P, 2, 512])
        sgg = sb("gt_sig_g", [P, 2, 512])
        gv = sb("gt_value", [P, 2, 512])
        gb = sb("gt_sig_b", [P, 2, NT])
        left = m.qiT
        chain, loop, done, dup = m.sem("tk_chain"), m.sem("tk_loop"), m.sem("tk_mask_ready"), m.sem("tk_mask_copied")
        wl, st = ([m.sem(f"gt_{n}{i}") for i in range(2)] for n in ("w_loaded", "stored"))
        ql = m.sem("gt_q_loaded")
        ps, ev, pc = m.sem("gt_psum"), m.sem("gt_from_psum"), m.sem("gt_pool_chain")
        with nc.Block() as block:
            @block.sync
            def _(sp):
                def load(c):
                    for _, at, n, src, off, _ in parts:
                        sp.dma_start(w[:, c % NB, at:at + n, :], src[:, :, off + c * P:off + (c + 1) * P]).then_inc(wl[c % NB], 16)

                load(0)
                load(1)
                sp.dma_start(m.attnT[:, :, :], m.q_dram).then_inc(ql, 16)
                for c in range(KD):
                    if c + NB < KD:
                        sp.wait_ge(ps, 12 * (c + 1))
                        load(c + NB)
                    sp.wait_ge(ev, 12 * (c + 1))
                    sp.wait_ge(pc, 6 * (c + 1))
                    sp.dma_start(m.gb_dram[:, c, :], gb[:, c % 2, :]).then_inc(st[c % 2], 16)
                    sp.dma_start(m.left_dram[:, c, :], left[:, c % 2, :]).then_inc(st[c % 2], 16)
                sp.wait_ge(done, 1)
                sp.dma_start(m.mask[DEC:P, MK_SAMPLE:MK_W], m.mask[0:DEC, MK_SAMPLE:MK_W]).then_inc(dup, 16)
                sp.wait_ge(dup, 16)
                sp.wait_ge(ql, 16)
                for i in range(2):
                    sp.wait_ge(st[i], 32 * KD // 2)

            @block.tensor
            def _(pe):
                for u, (c, lo, n) in enumerate(units):
                    if u % 3 == 0:
                        pe.wait_ge(wl[c % NB], 64 * (c // NB + 1))
                    for j, at, nk, _, _, rhs in parts:
                        seq = 4 * u + j
                        if seq >= 8:
                            pe.wait_ge(ev, seq - 7)
                        for k in range(nk):
                            i = nc.tensor.matmul(m.ps[:, seq % 8, 0:n], w[:, c % NB, at + k, :], rhs[:, k, lo:lo + n],
                                                 start=k == 0, stop=k == nk - 1)
                        i.then_inc(ps, 1)

            @block.scalar
            def _(act):
                for u, (c, lo, n) in enumerate(units):
                    if u % 3 == 0 and c >= 2:
                        act.wait_ge(st[c % 2], 32 * (c // 2))
                    if u >= 2:
                        act.wait_ge(pc, 2 * (u - 1))
                    for j, dst in ((GB, gb[:, c % 2, lo:lo + n]), (GA, sga[:, u % 2, 0:n]), (GG, sgg[:, u % 2, 0:n])):
                        act.wait_ge(ps, 4 * u + j + 1)
                        nc.scalar.activation(dst, m.ps[:, (4 * u + j) % 8, 0:n], ACT.Sigmoid).then_inc(ev, 1)
                    act.wait_ge(ps, 4 * u + GV + 1)
                    nc.scalar.copy(gv[:, u % 2, 0:n], m.ps[:, (4 * u + GV) % 8, 0:n]).then_inc(ev, 1)

            @block.gpsimd
            def _(pool):
                step = Chain(pool, pc)
                for u, (c, lo, n) in enumerate(units):
                    pool.wait_ge(ev, 4 * u + 4)
                    if u % 3 == 0 and c >= 2:
                        pool.wait_ge(st[c % 2], 32 * (c // 2))
                    step(nc.gpsimd.tensor_tensor(gv[:, u % 2, 0:n], gv[:, u % 2, 0:n], sgg[:, u % 2, 0:n], ALU.mult))
                    step(nc.gpsimd.tensor_tensor(left[:, c % 2, lo:lo + n], gv[:, u % 2, 0:n], sga[:, u % 2, 0:n], ALU.mult))

            @block.vector
            def _(dve):
                step = Chain(dve, chain)
                v = nc.vector

                def count(j, scalar):
                    r, c, w, _ = lists[j]
                    return v.tensor_scalar(hits[0:r, 0:w], m.sc[0:r, c:c + w], scalar, 0.0, ALU.is_ge, ALU.add,
                                           accum_out=cnt[0:r, j:j + 1])

                step(v.memset(cnt[:, :], 0.0))
                for j in range(NL):
                    step(count(j, 0.0))
                step(v.tensor_scalar(neg[:, :], cnt[:, :], TOPK - 0.5, None, ALU.is_lt))
                step(v.tensor_copy(negi[:, :], neg[:, :]))
                step(v.tensor_scalar(thr[:, :], negi[:, :], 31, None, ALU.logical_shift_left))
                step(v.memset(bit[:, :], 1 << 30))
                STEPS = NL + 4
                with dve.Fori(0, 31) as i:
                    at = STEPS * i
                    v.tensor_tensor(cand[:, :], thr[:, :], bit[:, :].broadcast_to([P, NL]), ALU.bitwise_or).then_inc(loop, 1)
                    dve.wait_ge(loop, at + 1)
                    for j in range(NL):
                        r = lists[j][0]
                        count(j, cand[0:r, j:j + 1].bitcast(F32)).then_inc(loop, 1)
                        dve.wait_ge(loop, at + 2 + j)
                    v.scalar_tensor_tensor(take[:, :], cnt[:, :], TOPK - 0.5, neg[:, :], ALU.is_ge, ALU.not_equal).then_inc(loop, 1)
                    dve.wait_ge(loop, at + STEPS - 2)
                    v.tensor_scalar(bit[:, :], bit[:, :], 1, None, ALU.logical_shift_right).then_inc(loop, 1)
                    v.copy_predicated(thr[:, :], take[:, :], cand[:, :]).then_inc(loop, 1)
                    dve.wait_ge(loop, at + STEPS)
                step(v.tensor_tensor(thr[:, :], thr[:, :], negi[:, :], ALU.add))
                for j, (r, c, w, mc) in enumerate(lists):
                    sc, mk, tf = m.sc[0:r, c:c + w], m.mask[0:r, mc:mc + w], thr[0:r, j:j + 1].bitcast(F32)
                    e, p, need = eq[0:r, 0:w], pre[0:r, 0:w], cnt[0:r, j:j + 1]
                    step(v.tensor_scalar(mk, sc, tf, 0.0, ALU.is_gt, ALU.add, accum_out=need))
                    step(v.tensor_scalar(need, need, -1.0, float(TOPK), ALU.mult, ALU.add))
                    step(v.tensor_scalar(e, sc, tf, None, ALU.is_equal))
                    step(v.tensor_tensor_scan(p, m.ones[0:r, 0:1].broadcast_to([r, w]), e, 0.0, ALU.mult, ALU.add))
                    step(v.scalar_tensor_tensor(e, p, need, e, ALU.is_le, ALU.mult))
                    step(v.scalar_tensor_tensor(mk, e, -1.0, mk, ALU.add, ALU.add))
                    step(v.tensor_scalar(mk, mk, -NEG, None, ALU.mult))
                step(v.memset(m.mask[:, 0:3 * P], 0.0))
                for t in range(2):
                    c = MK_COL[t] + P * (t + 1)
                    i = v.memset(m.mask[0:DEC, c - DEC:c], NEG)
                    if t:
                        i.then_inc(done, 1)
                    else:
                        step(i)


def attention(nc, m, A):
    order = range(PT, -1, -1)
    units = [(p, t, h) for p, t in enumerate(order) for h in range(H // 2 if t == PT else H)]
    first = [units.index((p, t, 0)) for p, t in enumerate(order)]
    NU = len(units)
    chunks = [pieces(keys_of(t)[0]) for _, t, _ in units]
    blocks = [pieces(keys_of(t)[0], P) for _, t, _ in units]
    groups = [[b[i:i + 4] for i in range(0, len(b), 4)] for b in blocks]
    c_at = [sum(map(len, chunks[:u])) for u in range(NU + 1)]
    g_at = [sum(map(len, groups[:u])) for u in range(NU + 1)]
    SCALE = HD ** -0.5
    with ExitStack() as ctx:
        sb = lambda name, shape, dt=F32: ctx.enter_context(nc.sbuf_tensor(name, shape, dt))
        qb = sb("at_qb", [P, 4, P])
        s = sb("at_s", [P, 3, PAST + DEC])
        pT = sb("at_pT", [P, 2, CB + 1, P])
        mx = sb("at_mx", [P, 4, 4])
        nb = sb("at_nb", [P, NU])
        sm = sb("at_sum", [P, NU])
        rs = sb("at_rsum", [P, NU])
        o = sb("at_o", [P, 2, 512])
        os_ = sb("at_os", [P, 4, HD])
        wol = m.sem("at_w_out_loaded")
        qz, sp_, sd, mxr, nbr, er, tp, te, pv, oc, rr, otp, ote, osr, osm = (m.sem("at_" + n) for n in (
            "qb_ready", "s_psum", "s_masked", "max_ready", "bias_ready", "exp_ready", "p_transposed", "p_copied",
            "pv_psum", "o_copied", "recip_ready", "o_transposed", "oT_copied", "os_ready", "os_moved"))
        with nc.Block() as block:
            @block.tensor
            def _(pe):
                def scores(u):
                    _, t, h = units[u]
                    for c, (k0, w) in enumerate(chunks[u]):
                        n = c_at[u] + c
                        if n >= 2:
                            pe.wait_ge(sd, n - 1)
                        for b, (k, x) in enumerate(pieces(w, 512)):
                            out = m.ps[:, 2 * (n % 2) + b, 0:x]
                            if t < PT:
                                half = slice(HD * (h % 2), HD * (h % 2 + 1))
                                i = nc.tensor.matmul(out, m.attnT[half, h // 2, t * P:(t + 1) * P],
                                                     m.kT[half, k0 + k:k0 + k + x], start=True, stop=True)
                            else:
                                i = nc.tensor.matmul(out, qb[:, h, :], m.kTs[:, k0 + k:k0 + k + x], start=True, stop=True)
                        i.then_inc(sp_, 1)

                def transposes(u):
                    pe.wait_ge(er, u + 1)
                    for g, bs in enumerate(groups[u]):
                        n = g_at[u] + g
                        if n >= 2:
                            pe.wait_ge(te, n - 1)
                        for j, (k, x) in enumerate(bs):
                            i = nc.tensor.transpose(m.ps[0:x, 4 + n % 2, j * P:(j + 1) * P], s[:, u % 3, k:k + x], m.ident[:, :])
                        i.then_inc(tp, 1)

                def values(u):
                    p, t, h = units[u]
                    pe.wait_ge(te, g_at[u + 1])
                    if h == 0 and p:
                        pe.wait_ge(oc, p)
                    src = m.v if t < PT else m.vs
                    for b, (k, x) in enumerate(blocks[u]):
                        i = nc.tensor.matmul(m.ps[:, 6, h * HD:(h + 1) * HD], pT[0:x, u % 2, b, :], src[0:x, b, :],
                                             start=b == 0, stop=b == len(blocks[u]) - 1)
                    i.then_inc(pv, 1)

                def output(p):
                    pe.wait_ge(oc, p + 1)
                    r = rows_of(order[p])
                    if order[p] == PT:
                        pe.wait_ge(osm, 32)
                    if p:
                        pe.wait_ge(ote, p)
                    for j in range(4):
                        i = nc.tensor.transpose(m.ps[:, 7, j * P:j * P + r], o[0:r, p % 2, j * P:(j + 1) * P], m.ident[0:r, 0:r])
                    i.then_inc(otp, 1)

                pe.wait_ge(qz, 4)
                scores(0)
                scores(1)
                for u in range(NU + 1):
                    if u + 2 < NU:
                        scores(u + 2)
                    if u < NU:
                        transposes(u)
                    if u:
                        values(u - 1)
                        p, _, h = units[u - 1]
                        if h == 3 and p:
                            output(p - 1)
                output(PT)

            @block.vector
            def _(dve):
                v = nc.vector

                def normalise(p):
                    a, n = first[p], H // 2 if order[p] == PT else H
                    dve.wait_ge(pv, a + n)
                    v.reciprocal(rs[:, a:a + n], sm[:, a:a + n]).then_inc(rr, 1)
                    dve.wait_ge(rr, p + 1)
                    if p >= 2:
                        dve.wait_ge(otp, p - 1)
                    dst = os_[:, :, :] if order[p] == PT else o[:, p % 2, :].rearrange("p (h d) -> p h d", d=HD)
                    v.tensor_tensor(dst, m.ps[:, 6, 0:n * HD].rearrange("p (h d) -> p h d", d=HD),
                                    bc(rs[:, a:a + n], 2, HD), ALU.mult).then_inc(oc, 1)

                def place(p):
                    dve.wait_ge(otp, p + 1)
                    t, r = order[p], rows_of(order[p])
                    v.tensor_copy(m.attnT[:, :, t * P:t * P + r],
                                  m.ps[:, 7, :].rearrange("p (j t) -> p j t", t=P)[:, :, 0:r]).then_inc(ote, 1)

                v.memset(qb[:, :, :], 0.0).then_inc(qz, 1)
                dve.wait_ge(qz, 1)
                for x in range(2):
                    half = slice(HD * x, HD * (x + 1))
                    v.tensor_copy(qb[half, :, DEC * x:DEC * (x + 1)], m.attnT[half, :, SEQ:NT]).then_inc(qz, 1)
                v.memset(sm[:, :], 0.0).then_inc(qz, 1)
                for u, (p, t, h) in enumerate(units):
                    mc = keys_of(t)[1]
                    if u >= 3:
                        dve.wait_ge(tp, g_at[u - 2])
                    for c, (k0, w) in enumerate(chunks[u]):
                        n = c_at[u] + c
                        dve.wait_ge(sp_, n + 1)
                        src = m.ps[:, 2 * (n % 2):2 * (n % 2) + 2, :].rearrange("p b n -> p (b n)")[:, 0:w]
                        v.tensor_tensor_reduce(out=s[:, u % 3, k0:k0 + w], in0=src, in1=m.mask[:, mc + k0:mc + k0 + w],
                                               scale=1.0, scalar=-3.0e38, op0=ALU.add, op1=ALU.max,
                                               accum_out=mx[:, u % 4, c:c + 1]).then_inc(sd, 1)
                    dve.wait_ge(sd, c_at[u + 1])
                    v.tensor_reduce(mx[:, u % 4, 3:4], mx[:, u % 4, 0:len(chunks[u])], AX.X, ALU.max).then_inc(mxr, 1)
                    dve.wait_ge(mxr, u + 1)
                    v.tensor_scalar(nb[:, u:u + 1], mx[:, u % 4, 3:4], -SCALE, None, ALU.mult).then_inc(nbr, 1)
                    if h == 2 and p:
                        normalise(p - 1)
                    if h == 5 and p:
                        place(p - 1)
                normalise(PT)
                place(PT)

            @block.scalar
            def _(act):
                def copies(u):
                    for g, bs in enumerate(groups[u]):
                        n = g_at[u] + g
                        act.wait_ge(tp, n + 1)
                        if u >= 2 and g == 0:
                            act.wait_ge(pv, u - 1)
                        x = bs[-1][1]
                        if x == P:
                            i = nc.scalar.copy(pT[:, u % 2, 4 * g:4 * g + len(bs), :].rearrange("p b n -> p (b n)"),
                                               m.ps[:, 4 + n % 2, 0:len(bs) * P])
                        else:
                            i = nc.scalar.copy(pT[0:x, u % 2, 4 * g, :], m.ps[0:x, 4 + n % 2, 0:P])
                        i.then_inc(te, 1)

                for u, (_, t, _) in enumerate(units):
                    n = keys_of(t)[0]
                    act.wait_ge(nbr, u + 1)
                    nc.scalar.activation(s[:, u % 3, 0:n], s[:, u % 3, 0:n], ACT.Exp, bias=nb[:, u:u + 1], scale=SCALE,
                                         accum_out=sm[:, u:u + 1]).then_inc(er, 1)
                    if u:
                        copies(u - 1)
                copies(NU - 1)

            @block.sync
            def _(sp):
                def load_next():
                    wo = A.w_out.rearrange("(k p) n -> p k n", p=P)
                    for k in range(KD):
                        sp.dma_start(m.wout[:, k, :], wo[:, k, :]).then_inc(wol, 16)
                    load_mod_rows(m, sp, m.modA, (2, 4), wol)

                sp.wait_ge(oc, 1)
                dst = o[0:DEC, 0, :].rearrange("p (j x d) -> p j x d", j=4, x=2)
                for x in range(2):
                    sp.dma_start(dst[:, :, x, :], os_[DEC * x:DEC * (x + 1), :, :]).then_inc(osm, 16)
                load_next()
                sp.wait_ge(osm, 32)
                sp.wait_ge(wol, 16 * KD + 64)


def merge(nc, m, A):
    NB = 3
    units = [(c, lo, n) for c in range(KD) for lo, n in SPANS]
    with ExitStack() as ctx:
        sb = lambda name, shape: ctx.enter_context(nc.sbuf_tensor(name, shape, F32))
        w = sb("mg_w", [P, 4, D])
        gb = sb("mg_gb", [P, NB, NT])
        tt = sb("mg_t", [P, 2, 512])
        wl, gl = m.sem("mg_w_loaded"), [m.sem(f"mg_gate_loaded{i}") for i in range(NB)]
        ps, dv, mbl = m.sem("mg_psum"), m.sem("mg_dve_chain"), m.sem("mg_mod_loaded")
        with nc.Block() as block:
            @block.sync
            def _(sp):
                sp.dma_start(w[:, :, :], A.w_attn_out.rearrange("(k p) n -> p k n", p=P)).then_inc(wl, 16)
                for c in range(KD):
                    if c >= NB:
                        sp.wait_ge(dv, 6 * (c - NB + 1))
                    sp.dma_start(gb[:, c % NB, :], m.gb_dram[:, c, :]).then_inc(gl[c % NB], 16)
                    sp.dma_start(m.mergedT[:, c, :], m.left_dram[:, c, :]).then_inc(gl[c % NB], 16)
                load_mod_rows(m, sp, m.shift2, (3,), mbl)
                sp.wait_ge(mbl, 32)

            @block.tensor
            def _(pe):
                pe.wait_ge(wl, 16)
                for u, (c, lo, n) in enumerate(units):
                    if u >= 8:
                        pe.wait_ge(dv, 2 * (u - 8) + 1)
                    for k in range(4):
                        i = nc.tensor.matmul(m.ps[:, u % 8, 0:n], w[:, k, c * P:(c + 1) * P], m.attnT[:, k, lo:lo + n],
                                             start=k == 0, stop=k == 3)
                    i.then_inc(ps, 1)

            @block.vector
            def _(dve):
                step = Chain(dve, dv)
                v = nc.vector
                for u, (c, lo, n) in enumerate(units):
                    t, out = tt[:, u % 2, 0:n], m.mergedT[:, c, lo:lo + n]
                    if u % 3 == 0:
                        dve.wait_ge(gl[c % NB], 32 * (c // NB + 1))
                    dve.wait_ge(ps, u + 1)
                    step(v.tensor_tensor(t, m.ps[:, u % 8, 0:n], gb[:, c % NB, lo:lo + n], ALU.mult))
                    step(v.tensor_tensor(out, t, out, ALU.add))


def load_mod_rows(m, engine, dst, first, sem):
    for i, j in enumerate(first):
        for s in range(2):
            engine.dma_start(dst[:, i, s, :], m.mod_dram[s:s + 1, j * D:(j + 1) * D].broadcast_to([P, D])).then_inc(sem, 16)


def output_projection(nc, m, A):
    with ExitStack() as ctx:
        sb = lambda name, shape: ctx.enter_context(nc.sbuf_tensor(name, shape, F32))
        x = sb("op_x", [P, 2, D])
        xa = sb("op_xa", [P, 2, D])
        h2 = sb("op_h2", [P, 2, D])
        sq = sb("op_sq", [P, D])
        h2T = sb("op_h2T", [P, 2, KD, P])
        wr = sb("op_wr", [P, KD, NG + NE])
        st = sb("op_st", [P, TILES, 4])
        wl, xl = m.sem("op_w_loaded"), [m.sem(f"op_x_loaded{i}") for i in range(2)]
        x1s, h2s = ([m.sem(f"op_{n}_stored{i}") for i in range(2)] for n in ("x1", "h2"))
        pm, dm, pa, sqr, msr, rtr, rcp, hm, hr, tp, te, rp, re, one = (m.sem("op_" + n) for n in (
            "psum", "gated", "x1_ready", "squared", "mean", "root", "recip", "h2_scaled", "h2_ready",
            "transposed", "h2T_ready", "router_psum", "logits", "scale_ready"))
        g2l = m.sem("op_gate2_loaded")
        g1 = m.modA[:, 0, :, :]
        sc2 = m.modA[:, 1, :, :]
        sh2 = m.shift2[:, 0, :, :]
        with nc.Block() as block:
            @block.sync
            def _(sp):
                sp.dma_start(wr[:, :, 0:NG], A.w_route_group.rearrange("(k p) n -> p k n", p=P)).then_inc(wl, 16)
                sp.dma_start(wr[:, :, NG:], A.w_route_expert.rearrange("(k p) n -> p k n", p=P)).then_inc(wl, 16)
                for t in range(TILES + 1):
                    if t < TILES:
                        r = rows_of(t)
                        if t >= 2:
                            sp.wait_ge(pa, t - 1)
                        src = A.x_prompt[0, t * P:(t + 1) * P, :] if t < PT else A.x_sample[0, :, :]
                        sp.dma_start(x[0:r, t % 2, :], src).then_inc(xl[t % 2], 16)
                    if t:
                        u = t - 1
                        r = rows_of(u)
                        sp.wait_ge(pa, u + 1)
                        sp.dma_start(m.x1_dram[u * P:u * P + r, :], xa[0:r, u % 2, :]).then_inc(x1s[u % 2], 16)
                        sp.wait_ge(hr, u + 1)
                        sp.dma_start(m.h2_dram[u * P:u * P + r, :], h2[0:r, u % 2, :]).then_inc(h2s[u % 2], 16)
                load_mod_rows(m, sp, m.gate2, (5,), g2l)
                sp.wait_ge(g2l, 32)
                for i in range(2):
                    sp.wait_ge(x1s[i], 16 * ((TILES + 1 - i) // 2))
                    sp.wait_ge(h2s[i], 16 * ((TILES + 1 - i) // 2))

            @block.tensor
            def _(pe):
                def main(t):
                    r = rows_of(t)
                    if t >= 2:
                        pe.wait_ge(dm, t - 1)
                    for n in range(2):
                        for k in range(KD):
                            i = nc.tensor.matmul(m.ps[0:r, 2 * (t % 2) + n, :], m.mergedT[:, k, t * P:t * P + r],
                                                 m.wout[:, k, n * 512:(n + 1) * 512], start=k == 0, stop=k == KD - 1)
                    i.then_inc(pm, 1)

                def transposes(t):
                    r = rows_of(t)
                    pe.wait_ge(hr, t + 1)
                    if t:
                        pe.wait_ge(te, t)
                    for k in range(KD):
                        i = nc.tensor.transpose(m.ps[:, 4 + k // 4, (k % 4) * P:(k % 4) * P + r],
                                                h2[0:r, t % 2, k * P:(k + 1) * P], m.ident[0:r, 0:r])
                    i.then_inc(tp, 1)

                def route(t):
                    r = rows_of(t)
                    pe.wait_ge(te, t + 1)
                    if t >= 2:
                        pe.wait_ge(re, t - 1)
                    for k in range(KD):
                        i = nc.tensor.matmul(m.ps[0:r, 6 + t % 2, 0:NG + NE], h2T[:, t % 2, k, 0:r], wr[:, k, :],
                                             start=k == 0, stop=k == KD - 1)
                    i.then_inc(rp, 1)

                pe.wait_ge(wl, 32)
                for t in range(TILES + 2):
                    if t < TILES:
                        main(t)
                    if 1 <= t <= TILES:
                        transposes(t - 1)
                    if t >= 2:
                        route(t - 2)

            @block.gpsimd
            def _(pool):
                for t in range(TILES):
                    r = rows_of(t)
                    pool.wait_ge(dm, t + 1)
                    pool.wait_ge(xl[t % 2], 16 * (t // 2 + 1))
                    nc.gpsimd.tensor_tensor(xa[0:r, t % 2, :], xa[0:r, t % 2, :], x[0:r, t % 2, :], ALU.add).then_inc(pa, 1)
                    pool.wait_ge(hm, t + 1)
                    nc.gpsimd.tensor_tensor(h2[0:r, t % 2, :], h2[0:r, t % 2, :], sh2[0:r, int(t == PT), :],
                                            ALU.add).then_inc(hr, 1)

            @block.scalar
            def _(act):
                for t in range(TILES):
                    r = rows_of(t)
                    act.wait_ge(pa, t + 1)
                    if t:
                        act.wait_ge(sqr, t)
                    nc.scalar.activation(sq[0:r, :], xa[0:r, t % 2, :], ACT.Square, accum_out=st[0:r, t, 0:1]).then_inc(sqr, 1)
                    act.wait_ge(msr, t + 1)
                    nc.scalar.activation(st[0:r, t, 2:3], st[0:r, t, 1:2], ACT.Sqrt).then_inc(rtr, 1)
                    act.wait_ge(tp, t + 1)
                    if t >= 2:
                        act.wait_ge(rp, t - 1)
                    nc.scalar.copy(h2T[:, t % 2, :, 0:r].rearrange("p (b k) r -> p b k r", b=2),
                                   m.ps[:, 4:6, :].rearrange("p b (k r) -> p b k r", r=P)[:, :, :, 0:r]).then_inc(te, 1)

            @block.vector
            def _(dve):
                v = nc.vector

                def gated(t):
                    r = rows_of(t)
                    dve.wait_ge(pm, t + 1)
                    if t >= 2:
                        dve.wait_ge(x1s[t % 2], 16 * (t // 2))
                        dve.wait_ge(hm, t - 1)
                    v.tensor_tensor(xa[0:r, t % 2, :].rearrange("p (b n) -> p b n", b=2),
                                    m.ps[0:r, 2 * (t % 2):2 * (t % 2) + 2, :],
                                    g1[0:r, int(t == PT), :].rearrange("p (b n) -> p b n", b=2), ALU.mult).then_inc(dm, 1)

                def logits(t):
                    dve.wait_ge(rp, t + 1)
                    r = rows_of(t)
                    v.tensor_copy(m.logits[0:r, t, :], m.ps[0:r, 6 + t % 2, 0:NG + NE]).then_inc(re, 1)

                v.tensor_scalar(sc2, sc2, 1.0, None, ALU.add).then_inc(one, 1)
                v.memset(m.logits[:, :, :], 0.0).then_inc(one, 1)
                dve.wait_ge(one, 2)
                for t in range(TILES):
                    r = rows_of(t)
                    gated(t)
                    dve.wait_ge(sqr, t + 1)
                    v.tensor_scalar(st[0:r, t, 1:2], st[0:r, t, 0:1], 1.0 / D, EPS, ALU.mult, ALU.add).then_inc(msr, 1)
                    dve.wait_ge(rtr, t + 1)
                    v.reciprocal(st[0:r, t, 3:4], st[0:r, t, 2:3]).then_inc(rcp, 1)
                    dve.wait_ge(rcp, t + 1)
                    if t >= 2:
                        dve.wait_ge(tp, t - 1)
                        dve.wait_ge(h2s[t % 2], 16 * (t // 2))
                    v.scalar_tensor_tensor(h2[0:r, t % 2, :], xa[0:r, t % 2, :], st[0:r, t, 3:4], sc2[0:r, int(t == PT), :],
                                           ALU.mult, ALU.mult).then_inc(hm, 1)
                    if t:
                        logits(t - 1)
                logits(PT)


def routing(nc, m, A):
    LT = MAXT + 3
    with ExitStack() as ctx:
        sb = lambda name, shape, dt=F32: ctx.enter_context(nc.sbuf_tensor(name, shape, dt))
        bias = sb("rt_bias", [P, NG + NE])
        s4 = sb("rt_s4", [P, 8, TILES, 4])
        s16 = sb("rt_s16", [P, 4, TILES, NG, EPG])
        s1 = sb("rt_s1", [P, 12, TILES])
        base = sb("rt_base", [P, TILES + 1, NE])
        tot = sb("rt_tot", [P, TILES, NE])
        ex = sb("rt_experts", [P, 4, NE])
        ti = sb("rt_tiles", [P, LT])
        te = sb("rt_te", [P, 2, LT])
        cmp = sb("rt_cmp", [P, LT, NE])
        iota = sb("rt_iota", [P, LT], I32)
        spare = sb("rt_spare", [MAXT * 2, P], I32)
        rows = sb("rt_rows", [MAXT * 2, P], I32)
        rowsf = sb("rt_rowsf", [MAXT * 2, P])
        tok = sb("rt_tok", [P, 2, TILES], I32)
        ids = sb("rt_ids", [P, 3, MAXT * 2])
        bl, io, chain, ex1, ex2, ea, mr, pp, zs, sr, sct, rl, rf, rp = (m.sem("rt_" + n) for n in (
            "bias_loaded", "iotas", "dve_chain", "exp_group", "exp_expert", "exps", "choices_ready", "psum",
            "table_zeroed", "slots_ready", "scattered", "rows_loaded", "rows_float", "rows_psum"))
        eq, ohg, e1, e2, oh1, oh2, gl, free4 = (s4[:, j] for j in range(8))
        gm, gs, gw, v1, v2, dd, aa, den, w1 = (s1[:, j, :] for j in range(9))
        free = s1[:, 9, :]
        with nc.Block() as block:
            @block.sync
            def _(sp):
                sp.dma_start(bias[:, 0:NG], A.b_route_group.broadcast_to([P, NG])).then_inc(bl, 16)
                sp.dma_start(bias[:, NG:], A.b_route_expert.broadcast_to([P, NE])).then_inc(bl, 16)
                sp.wait_ge(io, 3)
                sp.dma_start(m.tok_dram.rearrange("(a p) o -> a (p o)", p=P), spare[:, :]).then_inc(zs, 16)
                sp.wait_ge(sct, 16 * 2 * TILES)
                sp.dma_start(rows[:, :], m.tok_dram.rearrange("(a p) o -> a (p o)", p=P)).then_inc(rl, 16)

            @block.gpsimd
            def _(pool):
                nc.gpsimd.iota(iota[:, :], [[1, LT]], base=0, channel_multiplier=0).then_inc(io, 1)
                nc.gpsimd.iota(tok[:, :, :], [[NT, 2], [P, TILES]], base=0, channel_multiplier=1).then_inc(io, 1)
                nc.gpsimd.iota(spare[:, :], [[1, P]], base=2 * NT, channel_multiplier=P).then_inc(io, 1)
                pool.wait_ge(io, 3)
                pool.wait_ge(zs, 16)
                pool.wait_ge(sr, 1)
                for t in range(TILES):
                    r = rows_of(t)
                    for c in range(2):
                        nc.gpsimd.indirect_dma_start(
                            out=m.tok_dram, out_offset=bass.IndirectOffsetOnAxis(ap=m.slot[0:r, c, t:t + 1], axis=0),
                            in_=tok[0:r, c, t:t + 1], in_offset=None).then_inc(sct, 16)

            @block.scalar
            def _(act):
                act.wait_ge(ex1, 1)
                nc.scalar.activation(e1, gl, ACT.Exp).then_inc(ea, 1)
                act.wait_ge(ex2, 1)
                nc.scalar.activation(aa, dd, ACT.Exp).then_inc(ea, 1)

            @block.tensor
            def _(pe):
                pe.wait_ge(mr, 1)
                mm = s16[:, 2].rearrange("p t g j -> p (t g j)")
                nc.tensor.matmul(m.ps[:, 0, 0:TILES * NE], m.tri[:, :], mm, start=True, stop=True)
                nc.tensor.matmul(m.ps[:, 1, 0:TILES * NE], m.ones[:, :], mm, start=True, stop=True).then_inc(pp, 1)
                pe.wait_ge(rf, 1)
                nc.tensor.transpose(m.ps[:, 2, 0:MAXT * 2], rowsf[:, :], m.ident[0:MAXT * 2, 0:MAXT * 2]).then_inc(rp, 1)

            @block.vector
            def _(dve):
                v = nc.vector
                step = Chain(dve, chain)
                tt, ts = v.tensor_tensor, v.tensor_scalar

                def first_of_highest(values, highest, oh):
                    step(v.tensor_reduce(highest, values, AX.X, ALU.max))
                    step(tt(oh, values, bc(highest, 2, 4), ALU.is_equal))
                    step(ts(free, oh[:, :, 0], -1.0, 1.0, ALU.mult, ALU.add))
                    for j in range(1, 4):
                        step(tt(oh[:, :, j], oh[:, :, j], free, ALU.mult))
                        step(tt(free, free, oh[:, :, j], ALU.subtract))

                lg = m.logits
                dve.wait_ge(bl, 32)
                step(tt(lg[:, :, :], lg[:, :, :], bc(bias[:, :], 1, TILES), ALU.add))
                groups = lg[:, :, 0:NG]
                first_of_highest(groups, gm, ohg)
                tt(gl, groups, bc(gm, 2, 4), ALU.subtract).then_inc(ex1, 1)
                prod = s16[:, 0]
                step(tt(prod, lg[:, :, NG:].rearrange("p t (g j) -> p t g j", g=NG), bc(ohg, 3, EPG), ALU.mult))
                step(v.tensor_reduce(e2, prod.rearrange("p t g j -> p t j g"), AX.X, ALU.add))
                first_of_highest(e2, v1, oh1)
                step(v.scalar_tensor_tensor(e2, oh1, NEG, e2, ALU.mult, ALU.add))
                first_of_highest(e2, v2, oh2)
                tt(dd, v2, v1, ALU.subtract).then_inc(ex2, 1)
                dve.wait_ge(ea, 2)
                step(v.tensor_reduce(gs, e1, AX.X, ALU.add))
                step(ts(den, aa, 1.0, None, ALU.add))
                step(tt(den, den, gs, ALU.mult))
                step(v.reciprocal(m.wt[:, 0, :], den))
                step(tt(m.wt[:, 1, :], m.wt[:, 0, :], aa, ALU.mult))
                for c, oh in enumerate((oh1, oh2)):
                    step(tt(s16[:, c], bc(ohg, 3, EPG), bc(oh, 2, NG), ALU.mult))
                    step(v.memset(s16[DEC:P, c, PT, :, :], 0.0))
                tt(s16[:, 2], s16[:, 0], s16[:, 1], ALU.add).then_inc(mr, 1)
                dve.wait_ge(pp, 1)
                fl = lambda a: a.rearrange("p t g j -> p (t g j)")
                step(v.tensor_copy(tot[:, :, :].rearrange("p t e -> p (t e)"), m.ps[:, 1, 0:TILES * NE]))
                step(v.memset(base[:, 0, :], 0.0))
                for t in range(TILES):
                    step(tt(base[:, t + 1, :], base[:, t, :], tot[:, t, :], ALU.add))
                count, tiles, done, start = (ex[:, j, :] for j in range(4))
                step(ts(tiles, base[:, TILES, :], 0.0, None, ALU.is_gt))
                for j in range(1, -(-NT // SLOTS)):
                    step(v.scalar_tensor_tensor(tiles, base[:, TILES, :], float(j * SLOTS), tiles, ALU.is_gt, ALU.add))
                step(v.tensor_tensor_scan(done, m.ones[:, 0:NE], tiles, 0.0, ALU.mult, ALU.add))
                step(tt(start, done, tiles, ALU.subtract))
                step(ts(start, start, float(SLOTS), None, ALU.mult))
                step(tt(tot[:, :, :], base[:, 0:TILES, :], bc(start, 1, TILES), ALU.add))
                step(tt(tot[:, :, :].rearrange("p t e -> p (t e)"), tot[:, :, :].rearrange("p t e -> p (t e)"),
                        m.ps[:, 0, 0:TILES * NE], ALU.add))
                for c in range(2):
                    step(tt(s16[:, c].rearrange("p t g j -> p t (g j)"), s16[:, c].rearrange("p t g j -> p t (g j)"),
                            tot[:, :, :], ALU.mult))
                    step(v.tensor_reduce(s1[:, 10 + c, :], s16[:, c].rearrange("p t g j -> p t (g j)"), AX.X, ALU.add))
                v.tensor_copy(m.slot[:, :, :], s1[:, 10:12, :]).then_inc(sr, 1)
                dve.wait_ge(io, 3)
                step(v.tensor_copy(ti[:, :], iota[:, :]))
                step(tt(cmp[:, :, :], bc(ti[:, :], 2, NE), bc(done, 1, LT), ALU.is_ge))
                step(v.tensor_reduce(te[:, 0, :], cmp[:, :, :], AX.X, ALU.add))
                step(ts(m.tile_expert[:, :], te[:, 0, :], float(NE - 1), None, ALU.min))
                step(ts(te[:, 1, 0:1], done[:, NE - 1:NE], 0.5, -0.25, ALU.mult, ALU.add))
                step(ts(te[:, 1, 0:1], te[:, 1, 0:1], ROUND, None, ALU.add))
                step(ts(te[:, 1, 0:1], te[:, 1, 0:1], -ROUND, None, ALU.add))
                step(tt(te[:, 1, 1:2], te[:, 1, 0:1], te[:, 1, 0:1], ALU.add))
                step(tt(te[:, 1, 1:2], te[:, 1, 1:2], done[:, NE - 1:NE], ALU.is_lt))
                step(tt(m.pairs[:, :], te[:, 1, 0:1], te[:, 1, 1:2], ALU.add))
                dve.wait_ge(rl, 16)
                v.tensor_copy(rowsf[:, :], rows[:, :]).then_inc(rf, 1)
                dve.wait_ge(rp, 1)
                step(v.tensor_copy(ids[:, 0, :], m.ps[:, 2, 0:MAXT * 2]))
                step(v.tensor_copy(m.slot_row[:, 0:MAXT * 2], ids[:, 0, :]))
                step(ts(ids[:, 1, :], ids[:, 0, :], NT - 0.5, -float(NT), ALU.is_ge, ALU.mult))
                step(tt(ids[:, 1, :], ids[:, 1, :], ids[:, 0, :], ALU.add))
                step(ts(ids[:, 2, :], ids[:, 1, :], NT - 0.5, None, ALU.is_lt))
                step(v.memset(m.slot_token[:, :], 0))
                step(tt(m.slot_token[:, 0:MAXT * 2], ids[:, 1, :], ids[:, 2, :], ALU.mult))


def experts(nc, m, A):
    with ExitStack() as ctx:
        sb = lambda name, shape, dt=F32: ctx.enter_context(nc.sbuf_tensor(name, shape, dt))
        wg = sb("ex_wg", [P, 2, KD, FD])
        wu = sb("ex_wu", [P, 2, KD, FD])
        wd = sb("ex_wd", [P, 2, 2, D])
        idx = sb("ex_idx", [P, 2, 2], I32)
        row = sb("ex_row", [P, 2, 2], I32)
        xg = sb("ex_x", [P, 2, 2, D])
        xT = sb("ex_xT", [P, 2, KD, SLOTS])
        sl = sb("ex_silu", [P, 2, SLOTS])
        hid = sb("ex_hid", [P, 2, 2, SLOTS])
        yo = sb("ex_y", [P, 2, 2, D])
        wl, gl, ys = ([m.sem(f"ex_{n}{i}") for i in range(2)] for n in ("w_loaded", "x_gathered", "y_stored"))
        ic, rc, tp, xed, xea, gp, slr, hr, dn, yea, yed = (m.sem("ex_" + n) for n in (
            "index_copied", "row_copied", "x_transposed", "xT_by_dve", "xT_by_act", "gate_up_psum", "silu_ready", "hid_ready",
            "down_psum", "y_by_act", "y_by_dve"))

        idle = sb("ex_idle", [1, 7])
        begun, idle_set = m.sem("ex_begun"), m.sem("ex_idle_set")

        def wait(engine, sem, value):
            if not (isinstance(value, int) and value <= 0):
                engine.wait_ge(sem, value)

        def wait_alone(place, sem, value):
            nc.gpsimd.wait_ge(sem, value)
            nc.gpsimd.tensor_tensor(idle[:, place:place + 1], idle[:, 0:1], idle[:, 0:1], ALU.add)

        def run(engine, body, before=None, after=None):
            pairs = engine.value_load(m.pairs[0:1, 0:1], min_val=2, max_val=MAXT // 2)
            if before:
                before()
            body(0)
            with engine.Fori(1, pairs) as i:
                body(i)
            if after:
                after(pairs)

        with nc.Block() as block:
            @block.sync
            def _(sp):
                def weights(i, b):
                    e = sp.value_load(m.tile_expert[0:1, bass.ds(2 * i + b, 1)], min_val=0, max_val=NE - 1)
                    for dst, src in ((wg, A.w_gate), (wu, A.w_up), (wd, A.w_down)):
                        sp.dma_start(dst[:, b, :, :], src[bass.ds(e, 1), :, :].rearrange("o (k p) n -> p (o k) n", p=P)) \
                            .then_inc(wl[b], 16)

                def body(i):
                    for b in range(2):
                        sp.wait_ge(dn, 4 * (2 * i + b) + 4)
                        weights(i + 1, b)

                run(sp, body, lambda: (weights(0, 0), weights(0, 1)))

            @block.gpsimd
            def _(pool):
                def gather(i, b):
                    n = 2 * i + b
                    wait(pool, tp, 4 * n - 4)
                    nc.gpsimd.tensor_copy(idx[:, b, :], m.slot_token[:, bass.ds(2 * n, 2)]).then_inc(ic, 1)
                    wait_alone(1 + b, ic, n + 1)
                    for a in range(2):
                        nc.gpsimd.indirect_dma_start(
                            out=xg[:, b, a, :], out_offset=None, in_=m.h2_dram,
                            in_offset=bass.IndirectOffsetOnAxis(ap=idx[:, b, a:a + 1], axis=0)).then_inc(gl[b], 16)

                def scatter(i, b):
                    n = 2 * i + b
                    wait(pool, ys[b], 32 * i)
                    nc.gpsimd.tensor_copy(row[:, b, :], m.slot_row[:, bass.ds(2 * n, 2)]).then_inc(rc, 1)
                    pool.wait_ge(rc, n + 1)
                    for a, ready in enumerate((yea, yed)):
                        wait_alone(3 + 2 * b + a, ready, 2 * n + 2)
                        nc.gpsimd.indirect_dma_start(
                            out=m.y_dram, out_offset=bass.IndirectOffsetOnAxis(ap=row[:, b, a:a + 1], axis=0),
                            in_=yo[:, b, a, :], in_offset=None).then_inc(ys[b], 16)

                def body(i):
                    gather(i, 1)
                    scatter(i, 0)
                    gather(i + 1, 0)
                    scatter(i, 1)

                def after(pairs):
                    for b in range(2):
                        pool.wait_ge(ys[b], 32 * pairs)
                        pool.wait_ge(wl[b], 48 * pairs + 48)

                nc.gpsimd.memset(idle[:, 0:1], 0.0).then_inc(idle_set, 1)
                pool.wait_ge(idle_set, 1)
                run(pool, body, lambda: gather(0, 0), after)

            @block.tensor
            def _(pe):
                def transposes(i, b):
                    n = 2 * i + b
                    pe.wait_ge(gl[b], 32 * i + 32)
                    for q in range(4):
                        wait(pe, (xed, xea)[q % 2], 2 * n + q // 2)
                        for k in range(2):
                            for a in range(2):
                                j = nc.tensor.transpose(m.ps[:, q % 2, SLOTS * k + P * a:SLOTS * k + P * (a + 1)],
                                                        xg[:, b, a, P * (2 * q + k):P * (2 * q + k + 1)], m.ident[:, :])
                        j.then_inc(tp, 1)

                def gate_up(i, b):
                    n = 2 * i + b
                    pe.wait_ge(wl[b], 48 * i + 48)
                    pe.wait_ge(xed, 2 * n + 2)
                    pe.wait_ge(xea, 2 * n + 2)
                    for f in range(2):
                        wait(pe, hr, 2 * n - 1 + f)
                        for x, w in enumerate((wg, wu)):
                            for k in range(KD):
                                j = nc.tensor.matmul(m.ps[:, 2 + f, SLOTS * x:SLOTS * (x + 1)],
                                                     w[:, b, k, P * f:P * (f + 1)], xT[:, b, k, :],
                                                     start=k == 0, stop=k == KD - 1)
                        j.then_inc(gp, 1)

                def down(i, b):
                    n = 2 * i + b
                    pe.wait_ge(hr, 2 * n + 2)
                    for a in range(2):
                        wait(pe, (yea, yed)[a], 2 * n)
                        for c in range(2):
                            for f in range(2):
                                j = nc.tensor.matmul(m.ps[:, 4 + 2 * a + c, :], hid[:, b, f, P * a:P * (a + 1)],
                                                     wd[:, b, f, 512 * c:512 * (c + 1)], start=f == 0, stop=f == 1)
                            j.then_inc(dn, 1)

                def body(i):
                    gate_up(i, 0)
                    transposes(i, 1)
                    down(i, 0)
                    gate_up(i, 1)
                    transposes(i + 1, 0)
                    down(i, 1)

                run(pe, body, lambda: transposes(0, 0))

            @block.scalar
            def _(act):
                def xts(i, b):
                    for q in (1, 3):
                        act.wait_ge(tp, 4 * (2 * i + b) + q + 1)
                        nc.scalar.copy(xT[:, b, 2 * q:2 * q + 2, :].rearrange("p k n -> p (k n)"), m.ps[:, 1, :]).then_inc(xea, 1)

                def half(i, b):
                    n = 2 * i + b
                    for f in range(2):
                        act.wait_ge(gp, 2 * n + f + 1)
                        wait(act, hr, 2 * n - 1 + f)
                        nc.scalar.activation(sl[:, f, :], m.ps[:, 2 + f, 0:SLOTS], ACT.Silu).then_inc(slr, 1)
                    xts(i + b, 1 - b)
                    wait(act, ys[b], 32 * i)
                    for c in range(2):
                        act.wait_ge(dn, 4 * n + c + 1)
                        nc.scalar.copy(yo[:, b, 0, 512 * c:512 * (c + 1)], m.ps[:, 4 + c, :]).then_inc(yea, 1)

                act.wait_ge(begun, 1)
                run(act, lambda i: (half(i, 0), half(i, 1)), lambda: xts(0, 0))

            @block.vector
            def _(dve):
                v = nc.vector

                def xts(i, b):
                    for q in (0, 2):
                        dve.wait_ge(tp, 4 * (2 * i + b) + q + 1)
                        v.tensor_copy(xT[:, b, 2 * q:2 * q + 2, :].rearrange("p k n -> p (k n)"), m.ps[:, 0, :]).then_inc(xed, 1)

                def half(i, b):
                    n = 2 * i + b
                    for f in range(2):
                        dve.wait_ge(slr, 2 * n + f + 1)
                        v.tensor_tensor(hid[:, b, f, :], sl[:, f, :], m.ps[:, 2 + f, SLOTS:2 * SLOTS], ALU.mult).then_inc(hr, 1)
                    xts(i + b, 1 - b)
                    wait(dve, ys[b], 32 * i)
                    for c in range(2):
                        dve.wait_ge(dn, 4 * n + c + 3)
                        v.tensor_copy(yo[:, b, 1, 512 * c:512 * (c + 1)], m.ps[:, 6 + c, :]).then_inc(yed, 1)

                v.memset(sl[:, :, :], 0.0).then_inc(begun, 1)
                dve.wait_ge(begun, 1)
                run(dve, lambda i: (half(i, 0), half(i, 1)), lambda: xts(0, 0))


def combine(nc, m, A, O):
    with ExitStack() as ctx:
        sb = lambda name, shape: ctx.enter_context(nc.sbuf_tensor(name, shape, F32))
        NB = 2
        y = sb("cb_y", [P, NB, 2, D])
        x1 = sb("cb_x1", [P, NB, D])
        o = sb("cb_o", [P, NB, D])
        yl, xl, os_ = ([m.sem(f"cb_{n}{i}") for i in range(NB)] for n in ("y_loaded", "x1_loaded", "stored"))
        chain, orr = m.sem("cb_dve_chain"), m.sem("cb_out_ready")
        with nc.Block() as block:
            @block.vector
            def _(dve):
                step = Chain(dve, chain)
                v = nc.vector
                for t in range(TILES):
                    r, b = rows_of(t), t % NB
                    dve.wait_ge(yl[b], 32 * (t // NB + 1))
                    y1, y2, dst = y[0:r, b, 0, :], y[0:r, b, 1, :], o[0:r, b, :]
                    step(v.tensor_scalar(y1, y1, m.wt[0:r, 0, t:t + 1], None, ALU.mult))
                    step(v.scalar_tensor_tensor(y1, y2, m.wt[0:r, 1, t:t + 1], y1, ALU.mult, ALU.add))
                    step(v.tensor_tensor(y1, y1, m.gate2[0:r, 0, int(t == PT), :], ALU.mult))
                    dve.wait_ge(xl[b], 16 * (t // NB + 1))
                    if t >= NB:
                        dve.wait_ge(os_[b], 16 * (t // NB))
                    v.tensor_tensor(dst, y1, x1[0:r, b, :], ALU.add).then_inc(orr, 1)

            @block.sync
            def _(sp):
                for t in range(TILES + 1):
                    if t < TILES:
                        r, b = rows_of(t), t % NB
                        if t >= NB:
                            sp.wait_ge(orr, t - NB + 1)
                        for c in range(2):
                            sp.dma_start(y[0:r, b, c, :], m.y_dram[c * NT + t * P:c * NT + t * P + r, :]).then_inc(yl[b], 16)
                        sp.dma_start(x1[0:r, b, :], m.x1_dram[t * P:t * P + r, :]).then_inc(xl[b], 16)
                    if t:
                        u = t - 1
                        sp.wait_ge(orr, u + 1)
                        dst = O.y_prompt[0, u * P:(u + 1) * P, :] if u < PT else O.y_sample[0, :, :]
                        sp.dma_start(dst, o[0:rows_of(u), u % NB, :]).then_inc(os_[u % NB], 16)
                for i in range(NB):
                    sp.wait_ge(os_[i], 16 * ((TILES - i + NB - 1) // NB))


def fresh_semaphores(nc, m):
    nc.clear_and_free_semaphores(m.sems)
    nc.all_engine_barrier()
    m.sems = []


def new_semaphore(nc, m, name):
    m.sems.append(nc.alloc_semaphore(name))
    return m.sems[-1]


def program(nc, A, O):
    ctx = ExitStack()
    m = Mem()
    m.sems = []
    m.sem = lambda name: new_semaphore(nc, m, name)
    with ctx:
        def sb(name, shape, dt=F32):
            return ctx.enter_context(nc.sbuf_tensor(name, shape, dt))
        m.ps = ctx.enter_context(nc.psum_tensor("ps", [P, 8, 512], F32))
        m.ident = sb("ident", [P, P])
        m.ones = sb("ones", [P, P])
        m.tri = sb("tri", [P, P])
        m.cT = sb("cT", [P, KD, 2])
        m.mod_dram = nc.dram_tensor("mod", [2, 6 * D], F32, kind="Internal").ap()
        m.sh1 = sb("sh1", [P, KD, 2])
        m.sc1 = sb("sc1", [P, KD, 2])
        m.hT = sb("hT", [P, KD, NT])
        constants(nc, m, A)
        with nc.sbuf_tensor("modrow", [2, 2 * D], F32) as m.modrow:
            adaln(nc, m, A, 0, ADA_FIRST, "a")
            mod_columns(nc, m)
        norm_in(nc, m, A)
        m.q_dram = nc.dram_tensor("q_dram", [P, 4, NT], F32, kind="Internal").ap()
        m.qiT = sb("qiT", [P, 2, NT])
        m.kT = sb("kT", [P, NT])
        m.kiT = sb("kiT", [P, NT])
        m.v = sb("v", [P, PT, HD])
        m.vs = sb("vs", [P, CB + 1, HD])
        m.wi = sb("wi", [P, TILES, IH])
        m.tokqi = sb("tokqi", [P, 2, IH * ID])
        m.zT = sb("zT", [P, 4, NT])
        m.x1_dram = nc.dram_tensor("x1_dram", [NT, D], F32, kind="Internal").ap()
        m.h2_dram = nc.dram_tensor("h2_dram", [NT, D], F32, kind="Internal").ap()
        m.y_dram = nc.dram_tensor("y_dram", [2 * NT + MAXT * SLOTS, D], F32, kind="Internal").ap()
        m.tok_dram = nc.dram_tensor("tok_dram", [MAXT * SLOTS, 1], I32, kind="Internal").ap()
        m.gb_dram = nc.dram_tensor("gate_b_dram", [P, KD, NT], F32, kind="Internal").ap()
        m.left_dram = nc.dram_tensor("merge_left_dram", [P, KD, NT], F32, kind="Internal").ap()
        m.us_dram = nc.dram_tensor("us_dram", [DEC, 512], F32, kind="Internal").ap()
        with nc.sbuf_tensor("u", [P, G, T, J], F32) as m.u, nc.sbuf_tensor("us", [DEC, 512], F32) as m.us:
            with nc.sbuf_tensor("qT", [P, 4, NT], F32) as m.qT:
                project(nc, m, A, O)
            with ExitStack() as ssm:
                ssb = lambda name, shape: ssm.enter_context(nc.sbuf_tensor(name, shape, F32))
                m.M = ssb("M", [P, G, P])
                m.V = ssb("V", [P, 2, PAIR, T + 1, J])
                m.W = ssb("W", [P, 2, PAIR, P])
                m.rot = ssb("rot", [P, 2, PAIR, COLS])
                m.decay = ssb("decay", [P, PAIR, COLS])
                m.r8 = ssb("r8", [P, PAIR])
                m.h0 = ssb("h0", [P, 2, PAIR])
                ssm_parameters(nc, m, A)
                ssm_scan(nc, m, A, O)
        fresh_semaphores(nc, m)
        m.attnT = sb("attnT", [P, 4, NT])
        with ExitStack() as at:
            asb = lambda name, shape, dt=F32: at.enter_context(nc.sbuf_tensor(name, shape, dt))
            m.mask = asb("mask", [P, MK_W], BF16)
            m.kTs = asb("kTs", [P, PAST + DEC])
            with nc.sbuf_tensor("sc", [P, SC_W], F32) as m.sc:
                with nc.sbuf_tensor("kiTs", [P, PAST + DEC], F32) as m.kiTs:
                    cache_keys(nc, m, A)
                    index_scores(nc, m)
                select_keys_and_gates(nc, m, A)
            flat = lambda a: a[:, :, :].rearrange("p k n -> p (k n)")
            m.wout = flat(m.hT)[:, 0:KD * D].rearrange("p (k n) -> p k n", k=KD)
            m.modA = flat(m.zT)[:, 0:4 * D].rearrange("p (a s n) -> p a s n", a=2, s=2)
            attention(nc, m, A)
        fresh_semaphores(nc, m)
        m.logits = sb("logits", [P, TILES, NG + NE])
        m.gate2 = flat(m.attnT)[:, 0:2 * D].rearrange("p (a s n) -> p a s n", a=1, s=2)
        with nc.sbuf_tensor("mergedT", [P, KD, NT], F32) as m.mergedT, nc.sbuf_tensor("shift2", [P, 1, 2, D], F32) as m.shift2:
            merge(nc, m, A)
            output_projection(nc, m, A)
        m.wt = sb("choice_weight", [P, 2, TILES])
        m.slot = sb("slot", [P, 2, TILES], I32)
        m.slot_row = sb("slot_row", [P, MAXT * 2], I32)
        m.slot_token = sb("slot_token", [P, MAXT * 2 + 4], I32)
        m.tile_expert = sb("tile_expert", [P, MAXT + 3], I32)
        m.pairs = sb("pairs", [P, 1], I32)
        routing(nc, m, A)
        experts(nc, m, A)
        combine(nc, m, A, O)


_INS = ['x_prompt', 'x_sample', 'cache_k', 'cache_v', 'cache_kidx', 'state_ssm_re', 'state_ssm_im',
        'c_prompt', 'c_sample', 'w_ada', 'b_ada', 'w_in', 'ssm_a_re', 'ssm_a_im', 'ssm_log_dt',
        'ssm_b_re', 'ssm_b_im', 'ssm_c_re', 'ssm_c_im', 'ssm_d', 'w_glu', 'q_gain', 'k_gain', 'kidx_gain',
        'w_attn_out', 'w_out', 'w_route_group', 'b_route_group', 'w_route_expert', 'b_route_expert',
        'w_gate', 'w_up', 'w_down']
_LAYERED = {n for n in _INS if n.startswith(('w_', 'cache', 'state', 'ssm'))}
_OUTS = [('y_prompt', (1, SEQ, D)), ('y_sample', (1, DEC, D)),
         ('k_prompt', (1, 1, SEQ, HD)), ('v_prompt', (1, 1, SEQ, HD)), ('kidx_prompt', (1, 1, SEQ, ID)),
         ('ssm_re_prompt', (1, 1, G, ST)), ('ssm_im_prompt', (1, 1, G, ST)),
         ('k_sample', (1, 1, DEC, HD)), ('v_sample', (1, 1, DEC, HD)), ('kidx_sample', (1, 1, DEC, ID)),
         ('ssm_re_sample', (1, 1, G, ST)), ('ssm_im_sample', (1, 1, G, ST))]


class Args:
    pass


def kernel(**inputs):
    import numpy as _np
    import concourse.bacc as _bacc
    from concourse.bass_utils import run_bass_kernel_spmd as _run

    nc = _bacc.Bacc("TRN2", target_bir_lowering=False, num_devices=1)
    arrays, ins, outs = {}, Args(), Args()
    for name in _INS:
        a = _np.ascontiguousarray(inputs[name])
        arrays[f"in_{name}"] = a
        ap = nc.dram_tensor(f"in_{name}", a.shape, F32, kind="ExternalInput").ap()
        vars(ins)[name] = ap[0] if name in _LAYERED else ap
    for name, shape in _OUTS:
        vars(outs)[name] = nc.dram_tensor(f"out_{name}", shape, F32, kind="ExternalOutput").ap()
    program(nc, ins, outs)
    r = _run(nc, [arrays], core_ids=[0])
    return tuple(r.results[0][f"out_{name}"] for name, _ in _OUTS)
```

```python
import math
from contextlib import ExitStack

import concourse.bass as bass
from concourse import mybir

F32 = mybir.dt.float32
BF16 = mybir.dt.bfloat16
I32 = mybir.dt.int32
U32 = mybir.dt.uint32
ALU = mybir.AluOpType
ACT = mybir.ActivationFunctionType
AX = mybir.AxisListType

P = 128
D = 1024
KD = D // P
SEQ, DEC = 1024, 64
NT = SEQ + DEC
PT = SEQ // P
TILES = PT + 1
PAST = 2048
CB = PAST // P
NS = PAST + DEC
EPS = 1e-6
NEG = -1e30
H, HD = 8, 64
IH, ID = 8, 32
TOPK = 256
G, ST, J = 32, 64, 16
PAIR = G // 2
T = 8
NCH = SEQ // T
SCH = DEC // T
COLS = NCH + 1 + SCH + 1
S0 = NCH + 1
NG, EPG, NE, FD = 4, 4, 16, 256
SLOTS = 256
MAXT = (2 * NT + NE * (SLOTS - 1)) // SLOTS
MAXT += MAXT % 2
OFF_U, OFF_Q, OFF_R, OFF_GA, OFF_GB = 0, 512, 1024, 1448, 2472
RW = OFF_GA - OFF_R
TW = 512 + RW
K0, V0, QI0, KI0, WI0 = 512, 576, 640, 896, 928


def rows_of(t):
    return P if t < PT else DEC


class Chain:

    def __init__(self, engine, sem):
        self.engine, self.sem, self.n = engine, sem, 0

    def __call__(self, instruction):
        instruction.then_inc(self.sem, 1)
        self.n += 1
        self.engine.wait_ge(self.sem, self.n)


class Mem:
    pass


def constants(nc, m, A):
    made = m.sem("constants_made")
    with nc.Block() as block:
        @block.gpsimd
        def _(pool):
            step = Chain(pool, made)
            step(nc.gpsimd.memset(m.ident[:, :], 0.0))
            step(nc.gpsimd.affine_select(out=m.ident[:, :], in_=m.ident[:, :], compare_op=ALU.not_equal,
                                         fill=1.0, base=0, pattern=[[-1, P]], channel_multiplier=1))
            nc.gpsimd.memset(m.ones[:, :], 1.0)
            step(nc.gpsimd.memset(m.tri[:, :], 1.0))
            step(nc.gpsimd.affine_select(out=m.tri[:, :], in_=m.tri[:, :], compare_op=ALU.is_gt,
                                         fill=0.0, base=0, pattern=[[1, P]], channel_multiplier=-1))


def adaln_and_norm(nc, m, A):
    with ExitStack() as ctx:
        sb = lambda name, shape: ctx.enter_context(nc.sbuf_tensor(name, shape, F32))
        n, NB = 2 * D // 512, 3
        w = [a.rearrange("p (k n) -> p k n", k=KD) for a in (
            m.u[:, :, :, :].rearrange("p g t j -> p (g t j)"), m.qT[:, :, :].rearrange("p k n -> p (k n)")[:, 0:KD * 512],
            m.zT[:, :, :].rearrange("p k n -> p (k n)")[:, 0:KD * 512])]
        b = m.qiT[0:1, :, :].rearrange("p a n -> p (a n)")[:, 0:n * 512]
        c16 = sb("ad_c16", [2 * KD, P])
        x = sb("n1_x", [P, TILES, D])
        junk = sb("n1_sq", [P, 2, D])
        row = junk[0:2, :, :].rearrange("p a n -> p (a n)")
        st = sb("n1_st", [P, 4, TILES])
        sh1 = sb("shift1", [P, KD, 2])
        sc1 = sb("scale1", [P, KD, 2])
        w_in = [m.sem(f"ad_w_loaded{i}") for i in range(NB)]
        x_in = [m.sem(f"n1_x_loaded{t}") for t in range(TILES)]
        c_in, c_t, c_s, ps, rowc, colt, colc = (m.sem("ad_" + k) for k in (
            "c_loaded", "c_transposed", "c_silu", "psum_ready", "rows_copied", "columns_transposed", "columns_copied"))
        sq, dv, sr, xnr, tr, evd, eva = (m.sem("n1_" + k) for k in (
            "sumsq", "dve_chain", "root", "xn_ready", "transposed", "evacuated_by_dve", "evacuated_by_act"))
        wsrc = A.w_ada.rearrange("(k p) n -> p k n", p=P)
        with nc.Block() as block:
            @block.sync
            def _(sp):
                def load_x(t):
                    src = A.x_prompt[0, t * P:(t + 1) * P, :] if t < PT else A.x_sample[0, :, :]
                    sp.dma_start(x[0:rows_of(t), t, :], src).then_inc(x_in[t], 16)

                def load_w(i):
                    sp.dma_start(w[i % NB], wsrc[:, :, i * 512:(i + 1) * 512]).then_inc(w_in[i % NB], 16)

                sp.dma_start(c16[0:KD, :], A.c_prompt.rearrange("o (k p) -> (o k) p", p=P)).then_inc(c_in, 16)
                sp.dma_start(c16[KD:2 * KD, :], A.c_sample.rearrange("o (k p) -> (o k) p", p=P)).then_inc(c_in, 16)
                sp.dma_start(b[:, :], A.b_ada[:, 0:n * 512]).then_inc(c_in, 16)
                for i in range(NB):
                    load_w(i)
                    for t in range(3 * i, 3 * i + 3):
                        load_x(t)
                for i in range(NB, n):
                    sp.wait_ge(ps, i - NB + 1)
                    load_w(i)
                wp = A.w_in.rearrange("(k p) n -> p k n", p=P)
                for lo, hi in ((512, 1024), (1024, OFF_GA), (0, 512)):
                    sp.dma_start(m.pj_w[:, :, lo:hi], wp[:, :, lo:hi]).then_inc(m.pj_loaded, 16)

            @block.tensor
            def _(pe):
                pe.wait_ge(c_in, 48)
                nc.tensor.transpose(m.ps[:, 7, 0:2 * KD], c16[:, :], m.ident[0:2 * KD, 0:2 * KD]).then_inc(c_t, 1)
                pe.wait_ge(c_s, 1)
                for i in range(n):
                    pe.wait_ge(w_in[i % NB], 16 * (i // NB + 1))
                    for k in range(KD):
                        nc.tensor.matmul(m.ps[0:2, i, :], m.cT[:, k, :], w[i % NB][:, k, :], start=k == 0, stop=False)
                    nc.tensor.matmul(m.ps[0:2, i, :], m.ones[0:1, 0:2], b[0:1, i * 512:(i + 1) * 512],
                                     start=False, stop=True).then_inc(ps, 1)
                pe.wait_ge(rowc, 1)
                for j in range(2 * KD):
                    i = nc.tensor.transpose(m.ps[:, 6, 2 * j:2 * j + 2], row[0:2, j * P:(j + 1) * P], m.ident[0:2, 0:2])
                i.then_inc(colt, 1)
                for t in range(TILES):
                    r = rows_of(t)
                    pe.wait_ge(xnr, t + 1)
                    if t == 1:
                        pe.wait_ge(colc, 1)
                    if t >= 2:
                        pe.wait_ge(evd, t - 1)
                        pe.wait_ge(eva, t - 1)
                    for k in range(KD):
                        i = nc.tensor.transpose(m.ps[:, 4 + 2 * (t % 2) + k // 4, (k % 4) * P:(k % 4) * P + r],
                                                x[0:r, t, k * P:(k + 1) * P], m.ident[0:r, 0:r])
                    i.then_inc(tr, 1)

            @block.scalar
            def _(act):
                act.wait_ge(c_t, 1)
                nc.scalar.activation(m.cT[:, :, :].rearrange("p k s -> p s k"),
                                     m.ps[:, 7, 0:2 * KD].rearrange("p (s k) -> p s k", s=2), ACT.Silu).then_inc(c_s, 1)
                act.wait_ge(dv, 1)
                for t in range(TILES):
                    r = rows_of(t)
                    act.wait_ge(x_in[t], 16)
                    if t >= 2:
                        act.wait_ge(sq, t - 1)
                    nc.scalar.activation(junk[0:r, t % 2, :], x[0:r, t, :], ACT.Square,
                                         accum_out=st[0:r, 0, t:t + 1]).then_inc(sq, 1)
                act.wait_ge(dv, 2)
                nc.scalar.activation(st[:, 2, :], st[:, 1, :], ACT.Sqrt).then_inc(sr, 1)
                act.wait_ge(colc, 1)
                for t in range(TILES):
                    r, s = rows_of(t), int(t == PT)
                    act.wait_ge(tr, t + 1)
                    for k in range(KD // 2, KD):
                        i = nc.scalar.activation(m.hT[:, k, t * P:t * P + r], m.ps[:, 5 + 2 * (t % 2), (k % 4) * P:(k % 4) * P + r],
                                                 ACT.Identity, bias=sh1[:, k, s:s + 1], scale=sc1[:, k, s:s + 1])
                    i.then_inc(eva, 1)

            @block.vector
            def _(dve):
                step = Chain(dve, dv)
                v = nc.vector
                step(v.memset(st[:, 0, :], 1.0))
                dve.wait_ge(sq, TILES)
                step(v.tensor_scalar(st[:, 1, :], st[:, 0, :], 1.0 / D, EPS, ALU.mult, ALU.add))
                dve.wait_ge(sr, 1)
                step(v.reciprocal(st[:, 3, :], st[:, 2, :]))
                for t in range(TILES):
                    r = rows_of(t)
                    v.tensor_scalar(x[0:r, t, :], x[0:r, t, :], st[0:r, 3, t:t + 1], None, ALU.mult).then_inc(xnr, 1)
                dve.wait_ge(ps, n)
                v.tensor_copy(row[0:2, :].rearrange("s (c n) -> s c n", n=512), m.ps[0:2, 0:n, :]).then_inc(rowc, 1)
                dve.wait_ge(colt, 1)
                v.tensor_copy(sh1[:, :, :], m.ps[:, 6, 0:2 * KD].rearrange("p (k s) -> p k s", s=2))
                v.tensor_scalar(sc1[:, :, :], m.ps[:, 6, 2 * KD:4 * KD].rearrange("p (k s) -> p k s", s=2),
                                1.0, None, ALU.add).then_inc(colc, 1)
                dve.wait_ge(colc, 1)
                for t in range(TILES):
                    r, s = rows_of(t), int(t == PT)
                    dve.wait_ge(tr, t + 1)
                    for k in range(KD // 2):
                        i = v.tensor_scalar(m.hT[:, k, t * P:t * P + r], m.ps[:, 4 + 2 * (t % 2), k * P:k * P + r],
                                            sc1[:, k, s:s + 1], sh1[:, k, s:s + 1], ALU.mult, ALU.add)
                    i.then_inc(evd, 1)


def bc(ap, axis, n):
    shape = list(ap.shape)
    return ap.unsqueeze(axis).broadcast_to(shape[:axis] + [n] + shape[axis:])


def project(nc, m, A, O):
    with ExitStack() as ctx:
        sb = lambda name, shape: ctx.enter_context(nc.sbuf_tensor(name, shape, F32))
        w, wl = m.pj_w, m.pj_loaded
        tok = sb("pj_tok", [P, 2, TW])
        sq = sb("pj_sq", [P, 608])
        st = sb("pj_st", [P, TILES, 4, 10])
        qn = sb("pj_qn", [P, 2, 512])
        kk = sb("pj_kk", [P, 2, 2, HD])
        ki4 = sb("pj_ki4", [P, 2, 4, ID])
        gk = sb("pj_gk", [P, HD])
        gki = sb("pj_gki", [P, ID])
        gqr = sb("pj_gqr", [2, HD])
        gq = sb("pj_gq", [P, 1])
        gl = m.sem("pj_gains_loaded")
        qr, tokr, sqr, msr, rtr = (m.sem("pj_" + n) for n in ("qr_psum", "tok_copied", "squared", "mean", "root"))
        nr, tr, ev, chain = (m.sem("pj_" + n) for n in ("normalised", "transposed", "evacuated", "dve_chain"))
        up, ue, red = (m.sem("pj_" + n) for n in ("u_psum", "u_copied", "reduced"))
        vst = [m.sem(f"pj_v_stored{i}") for i in range(2)]
        kst = [m.sem(f"pj_k_stored{i}") for i in range(2)]
        gqt, gqe, qst = m.sem("pj_gq_transposed"), m.sem("pj_gq_copied"), m.sem("pj_q_stored")
        with nc.Block() as block:
            @block.sync
            def _(sp):
                sp.dma_start(gk[:, :], A.k_gain.broadcast_to([P, HD])).then_inc(gl, 16)
                sp.dma_start(gki[:, :], A.kidx_gain.broadcast_to([P, ID])).then_inc(gl, 16)
                sp.dma_start(gqr[:, :], A.q_gain.broadcast_to([2, HD])).then_inc(gl, 16)
                for t in range(TILES):
                    r = rows_of(t)
                    sl = slice(t * P, t * P + r)
                    vo = O.v_prompt[0, 0, sl, :] if t < PT else O.v_sample[0, 0, :, :]
                    ko = O.k_prompt[0, 0, sl, :] if t < PT else O.k_sample[0, 0, :, :]
                    kio = O.kidx_prompt[0, 0, sl, :] if t < PT else O.kidx_sample[0, 0, :, :]
                    sp.wait_ge(tokr, t + 1)
                    sp.dma_start(vo, tok[0:r, t % 2, V0:V0 + HD]).then_inc(vst[t % 2], 16)
                    sp.wait_ge(nr, t + 1)
                    sp.dma_start(ko, kk[0:r, t % 2, 0, :]).then_inc(kst[t % 2], 16)
                    sp.dma_start(kio, ki4[0:r, t % 2, 0, :]).then_inc(kst[t % 2], 16)
                sp.wait_ge(ev, TILES)
                sp.dma_start(m.q_dram, m.qT[:, :, :]).then_inc(qst, 16)
                sp.wait_ge(ue, TILES)
                sp.dma_start(m.us_dram, m.us[:, :]).then_inc(qst, 16)
                sp.wait_ge(qst, 32)
                for i in range(2):
                    n = (TILES + 1 - i) // 2
                    sp.wait_ge(vst[i], 16 * n)
                    sp.wait_ge(kst[i], 32 * n)

            @block.tensor
            def _(pe):
                def transposes(t):
                    r = rows_of(t)
                    pe.wait_ge(nr, t + 1)
                    if t:
                        pe.wait_ge(ev, t)
                    for j in range(8):
                        src = (qn[0:r, t % 2, j * P:(j + 1) * P] if j < 4 else
                               m.tokqi[0:r, t % 2, (j - 4) * P:(j - 3) * P] if j < 6 else
                               (kk, ki4)[j - 6][0:r, t % 2, :, :].rearrange("p a d -> p (a d)"))
                        i = nc.tensor.transpose(m.ps[:, 6 + j // 4, (j % 4) * P:(j % 4) * P + r], src, m.ident[0:r, 0:r])
                    i.then_inc(tr, 1)

                pe.wait_ge(gl, 48)
                nc.tensor.transpose(m.ps[0:HD, 7, 0:2], gqr[:, :], m.ident[0:2, 0:2]).then_inc(gqt, 1)
                pe.wait_ge(gqe, 1)
                pe.wait_ge(wl, 48)
                for t in range(TILES):
                    r = rows_of(t)
                    if t >= 2:
                        pe.wait_ge(sqr, t - 1)
                    for k in range(KD):
                        nc.tensor.matmul(m.ps[0:r, 2 * (t % 2), :], m.hT[:, k, t * P:t * P + r], w[:, k, 512:1024],
                                         start=k == 0, stop=k == KD - 1)
                    for k in range(KD):
                        i = nc.tensor.matmul(m.ps[0:r, 2 * (t % 2) + 1, 0:RW], m.hT[:, k, t * P:t * P + r],
                                             w[:, k, 1024:1024 + RW], start=k == 0, stop=k == KD - 1)
                    i.then_inc(qr, 1)
                    if t >= 2:
                        pe.wait_ge(ue, t - 1)
                    for k in range(KD):
                        lhs = m.hT[:, k, t:SEQ:T] if t < T else m.hT[:, k, SEQ:NT]
                        i = nc.tensor.matmul(m.ps[0:r, 4 + t % 2, :], lhs, w[:, k, 0:512], start=k == 0, stop=k == KD - 1)
                    i.then_inc(up, 1)
                    if t:
                        transposes(t - 1)
                transposes(PT)

            @block.scalar
            def _(act):
                act.wait_ge(gqt, 1)
                nc.scalar.copy(gq[0:HD, :], m.ps[0:HD, 7, 0:1])
                nc.scalar.copy(gq[HD:P, :], m.ps[0:HD, 7, 1:2]).then_inc(gqe, 1)
                for t in range(TILES):
                    r = rows_of(t)
                    act.wait_ge(qr, t + 1)
                    if t >= 2:
                        act.wait_ge(nr, t - 1)
                        act.wait_ge(vst[t % 2], 16 * (t // 2))
                        act.wait_ge(tr, t - 1)
                    b = 2 * (t % 2)
                    nc.scalar.copy(tok[0:r, t % 2, 0:512], m.ps[0:r, b, :])
                    nc.scalar.copy(m.tokqi[0:r, t % 2, :], m.ps[0:r, b + 1, 128:384])
                    nc.scalar.copy(tok[0:r, t % 2, 512:TW], m.ps[0:r, b + 1, 0:RW]).then_inc(tokr, 1)
                    if t:
                        act.wait_ge(red, t)
                    nc.scalar.activation(sq[0:r, 0:512], m.ps[0:r, b, :], ACT.Square)
                    nc.scalar.activation(sq[0:r, 512:576], m.ps[0:r, b + 1, 0:64], ACT.Square)
                    nc.scalar.activation(sq[0:r, 576:608], m.ps[0:r, b + 1, 384:416], ACT.Square).then_inc(sqr, 1)
                    act.wait_ge(msr, t + 1)
                    nc.scalar.activation(st[0:r, t, 2, :], st[0:r, t, 1, :], ACT.Sqrt).then_inc(rtr, 1)
                    act.wait_ge(up, t + 1)
                    src = m.ps[0:r, 4 + t % 2, :]
                    if t < T:
                        i = nc.scalar.copy(m.u[:, :, t, :], src.rearrange("c (g j) -> c g j", j=J))
                    else:
                        i = nc.scalar.copy(m.us[:, :], src)
                    i.then_inc(ue, 1)

            @block.vector
            def _(dve):
                step = Chain(dve, chain)

                def evacuate(t):
                    r = rows_of(t)
                    sl = slice(t * P, t * P + r)
                    dve.wait_ge(tr, t + 1)
                    a = m.ps[:, 6, :].rearrange("p (j t) -> p j t", t=P)
                    b = m.ps[:, 7, :].rearrange("p (j t) -> p j t", t=P)
                    nc.vector.tensor_scalar(m.qT[:, :, sl], a[:, :, 0:r], gq[:, 0:1], None, ALU.mult)
                    nc.vector.tensor_copy(m.qiT[:, :, sl], b[:, 0:2, 0:r])
                    nc.vector.tensor_copy(m.kT[:, sl], b[:, 2, 0:r])
                    nc.vector.tensor_copy(m.kiT[:, sl], b[:, 3, 0:r]).then_inc(ev, 1)

                dve.wait_ge(gl, 48)
                dve.wait_ge(gqe, 1)
                for t in range(TILES):
                    r = rows_of(t)
                    dve.wait_ge(sqr, t + 1)
                    ss, ms, rt, rs = (st[0:r, t, j, :] for j in range(4))
                    nc.vector.tensor_reduce(ss[:, 0:9], sq[0:r, 0:576].rearrange("p (h d) -> p h d", d=HD), AX.X, ALU.add)
                    i = nc.vector.tensor_reduce(ss[:, 9:10], sq[0:r, 576:608], AX.X, ALU.add)
                    i.then_inc(red, 1)
                    dve.wait_ge(red, t + 1)
                    nc.vector.tensor_scalar(ms[:, 0:9], ss[:, 0:9], 1.0 / HD, EPS, ALU.mult, ALU.add)
                    nc.vector.tensor_scalar(ms[:, 9:10], ss[:, 9:10], 1.0 / ID, EPS, ALU.mult, ALU.add).then_inc(msr, 1)
                    dve.wait_ge(rtr, t + 1)
                    step(nc.vector.reciprocal(rs, rt))
                    if t >= 2:
                        dve.wait_ge(tr, t - 1)
                        dve.wait_ge(kst[t % 2], 32 * (t // 2))
                    row = tok[0:r, t % 2, :]
                    nc.vector.tensor_tensor(qn[0:r, t % 2, :].rearrange("p (h d) -> p h d", d=HD),
                                            row[:, 0:512].rearrange("p (h d) -> p h d", d=HD),
                                            bc(rs[:, 0:8], 2, HD), ALU.mult)
                    nc.vector.scalar_tensor_tensor(kk[0:r, t % 2, :, :], bc(row[:, K0:K0 + HD], 1, 2), rs[:, 8:9],
                                                   bc(gk[0:r, :], 1, 2), ALU.mult, ALU.mult)
                    nc.vector.scalar_tensor_tensor(ki4[0:r, t % 2, :, :], bc(row[:, KI0:KI0 + ID], 1, 4), rs[:, 9:10],
                                                   bc(gki[0:r, :], 1, 4), ALU.mult, ALU.mult)
                    nc.vector.tensor_scalar(m.wi[0:r, t, :], row[:, WI0:WI0 + IH], (IH * ID) ** -0.5, None, ALU.mult)
                    vd = m.v[:, t, :] if t < PT else m.vs[0:DEC, CB, :]
                    nc.vector.tensor_copy(vd, row[:, V0:V0 + HD]).then_inc(nr, 1)
                    if t:
                        evacuate(t - 1)
                evacuate(PT)


def cache_keys(nc, m, A):
    with ExitStack() as ctx:
        sb = lambda name, shape: ctx.enter_context(nc.sbuf_tensor(name, shape, F32))
        ck = sb("ck_k", [P, CB, HD])
        cki = sb("ck_ki", [P, CB, ID])
        kk = sb("ck_kk", [P, CB, 2, HD])
        ki4 = sb("ck_ki4", [P, CB, 4, ID])
        zs = sb("ck_z", [DEC, 512])
        ld, dup, tr, ev, zl, zp, ze = (m.sem("ck_" + n) for n in (
            "loaded", "repeated", "transposed", "evacuated", "z_loaded", "z_transposed", "z_copied"))
        with nc.Block() as block:
            @block.sync
            def _(sp):
                sp.dma_start(zs[:, :], m.z_dram).then_inc(zl, 16)
                sp.dma_start(ck[:, :, :], A.cache_k[0].rearrange("(b p) d -> p b d", p=P)).then_inc(ld, 16)
                sp.dma_start(cki[:, :, :], A.cache_kidx[0].rearrange("(b p) d -> p b d", p=P)).then_inc(ld, 16)
                sp.dma_start(m.vs[:, 0:CB, :], A.cache_v[0].rearrange("(b p) d -> p b d", p=P)).then_inc(ld, 16)

            @block.vector
            def _(dve):
                dve.wait_ge(ld, 48)
                nc.vector.tensor_copy(m.kTs[:, PAST:], m.kT[:, SEQ:NT])
                nc.vector.tensor_copy(m.kiTs[:, PAST:], m.kiT[:, SEQ:NT])
                nc.vector.tensor_copy(kk[:, :, :, :], bc(ck[:, :, :], 2, 2))
                nc.vector.tensor_copy(ki4[:, :, :, :], bc(cki[:, :, :], 2, 4)).then_inc(dup, 1)
                for g in range(2 * CB // 4):
                    dve.wait_ge(tr, g + 1)
                    dst = (m.kTs, m.kiTs)[g // 4][:, (g % 4) * 512:(g % 4 + 1) * 512]
                    nc.vector.tensor_copy(dst, m.ps[:, g % 4, :]).then_inc(ev, 1)

            @block.scalar
            def _(act):
                act.wait_ge(zp, 1)
                nc.scalar.copy(m.zT[:, :, SEQ:NT], m.ps[:, 4, 0:4 * DEC].rearrange("p (q n) -> p q n", q=4)).then_inc(ze, 1)

            @block.tensor
            def _(pe):
                pe.wait_ge(zl, 16)
                for q in range(4):
                    i = nc.tensor.transpose(m.ps[:, 4, q * DEC:(q + 1) * DEC], zs[:, q * P:(q + 1) * P], m.ident[0:DEC, 0:DEC])
                i.then_inc(zp, 1)
                pe.wait_ge(dup, 1)
                for g in range(2 * CB // 4):
                    if g >= 4:
                        pe.wait_ge(ev, g - 3)
                    for j in range(4):
                        b = (g % 4) * 4 + j
                        src = (kk, ki4)[g // 4][:, b, :, :].rearrange("p a d -> p (a d)")
                        i = nc.tensor.transpose(m.ps[:, g % 4, j * P:(j + 1) * P], src, m.ident[:, :])
                    i.then_inc(tr, 1)


TWO_PI_HI = 6.28125
TWO_PI_MID = 0.0019350051879882812
TWO_PI_LO = 2 * math.pi - TWO_PI_HI - TWO_PI_MID
ROUND = 1.5 * 2.0 ** 23
PI_BELOW = 3.1415925


class ComplexSteps:

    def __init__(self, nc, step):
        self.nc, self.step = nc, step

    def mul(self, out_re, out_im, a_re, a_im, b_re, b_im, tmp, negate_im=False):
        v, step = self.nc.vector, self.step
        step(v.tensor_tensor(tmp, a_re, b_re, ALU.mult))
        step(v.tensor_tensor(out_re, a_im, b_im, ALU.mult))
        step(v.tensor_tensor(out_re, tmp, out_re, ALU.subtract))
        step(v.tensor_tensor(tmp, a_re, b_im, ALU.mult))
        step(v.tensor_tensor(out_im, a_im, b_re, ALU.mult))
        step(v.tensor_tensor(out_im, tmp, out_im, ALU.add))
        if negate_im:
            step(v.tensor_scalar(out_im, out_im, -1.0, None, ALU.mult))


def ssm_parameters(nc, m, A):
    AC = 256
    ada = range(2 * D // AC, 6 * D // AC)
    wada = A.w_ada.rearrange("(k p) n -> p k n", p=P)
    with ExitStack() as ctx:
        sb = lambda name, shape: ctx.enter_context(nc.sbuf_tensor(name, shape, F32))
        rows = sb("sp_rows", [PAIR, 5, P])
        ldt = sb("sp_logdt", [PAIR, 2])
        prm = sb("sp_prm", [P, 5, PAIR])
        cin = sb("sp_c", [P, 2, 2, P])
        cT = sb("sp_cT", [P, 2, PAIR, J])
        b = sb("sp_b", [P, 2, PAIR, J])
        bb = sb("sp_bb", [P, 2, PAIR, J])
        s = sb("sp_small", [P, 24, PAIR])
        pw = sb("sp_powers", [P, 2, PAIR, T + 1])
        idle = m.zT[:, :, :].rearrange("p a n -> p (a n)")
        wt = idle[:, 0:2 * PAIR * P].rearrange("p (c q t j) -> p c q t j", c=2, q=PAIR, t=T)
        tmp = sb("sp_tmp", [P, PAIR * NCH // 2])
        ksb = idle[0:J, 0:G * P].rearrange("j (g n) -> j g n", g=G)
        dd = m.tokqi[0:J, :, :].rearrange("j a n -> j (a n)").rearrange("j (g i) -> j g i", g=G)
        ld, lc = m.sem("sp_loaded"), m.sem("sp_c_loaded")
        ldp, chain, tr, trd = m.sem("sp_dt_rows"), m.sem("sp_dve_chain"), m.sem("sp_transposed"), m.sem("sp_copied")
        a1, a2, a3, th, trig = m.sem("sp_dt"), m.sem("sp_decays"), m.sem("sp_adt"), m.sem("sp_angles"), m.sem("sp_trig")
        aw = sb("sp_ada_w", [P, 2, KD, AC])
        ab = sb("sp_ada_b", [1, 2, AC])
        arow = idle[0:2, G * P:G * P + AC]
        awl = [m.sem(f"sp_ada_w_loaded{i}") for i in range(2)]
        kcp, cte, lc1 = m.sem("sp_k_copied"), m.sem("sp_cT_copied"), m.sem("sp_c_im_loaded")
        ast, aps, aev = m.sem("sp_ada_stored"), m.sem("sp_ada_psum"), m.sem("sp_ada_copied")
        wtr, wps, wev, kps, kev, mz, mst, bbr = (m.sem("sp_" + n) for n in (
            "wt_ready", "w_psum", "w_copied", "k_psum", "k_ready", "m_zeroed", "m_stored", "bb_ready"))
        (dt, adt, ang, ang8, dec, n1, r1, sn, cs, n8, rr8, sn8, cs8, num, den, rden, t1, cr, ci, ab1, ab8) = \
            (s[:, j, :] for j in range(21))
        ar, ai, h0r, h0i, ldtT = (prm[:, j, :] for j in range(5))

        def load_c(engine, j):
            a = (A.ssm_c_re, A.ssm_c_im)[j]
            for q in range(PAIR):
                dst = cin[J * (q % 8):J * (q % 8 + 1), j, q // 8, :].rearrange("j (g p) -> j g p", g=2)
                engine.dma_start(dst, a[2 * q:2 * q + 2].rearrange("g j p -> j g p")).then_inc(lc if j == 0 else lc1, 16)

        def load_mod_weights(engine, i):
            j = ada[i]
            engine.dma_start(aw[:, i % 2, :, :], wada[:, :, j * AC:(j + 1) * AC]).then_inc(awl[i % 2], 16)
            engine.dma_start(ab[:, i % 2, :], A.b_ada[:, j * AC:(j + 1) * AC]).then_inc(awl[i % 2], 16)

        with nc.Block() as block:
            @block.sync
            def _(sp):
                for j, a in enumerate((A.ssm_a_re, A.ssm_a_im)):
                    sp.dma_start(rows[:, j, :], a.rearrange("(q g) p -> q (g p)", g=2)).then_inc(ld, 16)
                for j, a in enumerate((A.state_ssm_re, A.state_ssm_im)):
                    sp.dma_start(rows[:, 2 + j, :], a[0].rearrange("(q g) p -> q (g p)", g=2)).then_inc(ld, 16)
                sp.dma_start(ldt[:, :], A.ssm_log_dt.rearrange("(q g) -> q g", g=2)).then_inc(ld, 16)
                for j, a in enumerate((A.ssm_b_re, A.ssm_b_im)):
                    sp.dma_start(b[:, j, :, :], a.rearrange("(q g) p j -> (g p) q j", g=2)).then_inc(lc, 16)
                load_c(sp, 0)
                sp.dma_start(dd[:, :, :].rearrange("j g i -> j (g i)"),
                             A.ssm_d.rearrange("(o n) -> o n", o=1).broadcast_to([J, 512])).then_inc(lc, 16)
                for i in range(2, len(ada)):
                    sp.wait_ge(aps, i - 1)
                    load_mod_weights(sp, i)
                sp.wait_ge(mz, 1)
                sp.wait_ge(kev, 1)
                for p in range(T):
                    sp.dma_start(m.M[J * p:J * (p + 1), :, J * p:P], ksb[:, :, 0:P - J * p]).then_inc(mst, 16)
                sp.wait_ge(mst, 16 * T)

            @block.gpsimd
            def _(pool):
                load_c(nc.gpsimd, 1)
                nc.gpsimd.memset(m.M[:, :, :], 0.0).then_inc(mz, 1)

            @block.tensor
            def _(pe):
                def mod_chunks(some):
                    for i in some:
                        pe.wait_ge(awl[i % 2], 32 * (i // 2 + 1))
                        if i >= 2:
                            pe.wait_ge(aev, i - 1)
                        for k in range(KD):
                            nc.tensor.matmul(m.ps[0:2, 6 + i % 2, 0:AC], m.cT[:, k, :], aw[:, i % 2, k, :],
                                             start=k == 0, stop=False)
                        nc.tensor.matmul(m.ps[0:2, 6 + i % 2, 0:AC], m.ones[0:1, 0:2], ab[0:1, i % 2, :],
                                         start=False, stop=True).then_inc(aps, 1)

                def input_matrices(some):
                    for x in some:
                        if x == 1:
                            pe.wait_ge(cte, 1)
                        if x >= 6:
                            pe.wait_ge(wev, x - 5)
                        for y in range(4):
                            n = 4 * x + y
                            i = nc.tensor.transpose(m.ps[:, x % 6, P * y:P * (y + 1)],
                                                    wt[:, n // PAIR, n % PAIR, :, :].rearrange("p t j -> p (t j)"), m.ident[:, :])
                        i.then_inc(wps, 1)

                mod_chunks(range(0, 1))
                pe.wait_ge(ldp, 1)
                for j in range(5):
                    i = nc.tensor.transpose(m.ps[:, 0, PAIR * j:PAIR * (j + 1)], rows[:, j, :], m.ident[0:PAIR, 0:PAIR])
                i.then_inc(tr, 1)
                mod_chunks(range(1, 4))
                pe.wait_ge(lc, 16 * (3 + PAIR))
                pe.wait_ge(lc1, 16 * PAIR)
                for j in range(4):
                    i = nc.tensor.transpose(m.ps[:, 1, P * j:P * (j + 1)], cin[:, j // 2, j % 2, :], m.ident[:, :])
                i.then_inc(tr, 1)
                mod_chunks(range(4, 8))
                pe.wait_ge(wtr, 1)
                input_matrices(range(0, 6))
                mod_chunks(range(8, 12))
                pe.wait_ge(bbr, 1)
                input_matrices(range(6, 8))
                pe.wait_ge(wev, 8)
                for x in range(4):
                    if x == 3:
                        pe.wait_ge(kcp, 2)
                    for g in range(8 * x, 8 * x + 8):
                        h = slice(ST * (g % 2), ST * (g % 2 + 1))
                        y = (g % 8) // 2
                        for c in range(2):
                            i = nc.tensor.matmul(m.ps[0:J, (2 * x + g % 2) % 6, P * y:P * (y + 1)], bb[h, c, g // 2, :],
                                                 m.V[h, c, g // 2, 0:T, :].rearrange("p t i -> p (t i)"),
                                                 start=c == 0, stop=c == 1)
                    i.then_inc(kps, 1)
                    if x == 2:
                        mod_chunks(range(12, len(ada)))

            @block.scalar
            def _(act):
                load_mod_weights(nc.scalar, 0)
                load_mod_weights(nc.scalar, 1)
                act.wait_ge(trd, 1)
                nc.scalar.activation(dt, ldtT, ACT.Exp).then_inc(a1, 1)
                act.wait_ge(a3, 1)
                nc.scalar.activation(dec, adt, ACT.Exp)
                nc.scalar.activation(m.r8[:, :], adt, ACT.Exp, scale=float(T)).then_inc(a2, 1)
                act.wait_ge(th, 1)
                nc.scalar.activation(sn, r1, ACT.Sin)
                nc.scalar.activation(cs, ab1, ACT.Sin)
                nc.scalar.activation(sn8, rr8, ACT.Sin)
                nc.scalar.activation(cs8, ab8, ACT.Sin).then_inc(trig, 1)
                for i, j in enumerate(ada):
                    act.wait_ge(aps, i + 1)
                    if i:
                        act.wait_ge(ast, 16 * i)
                    nc.scalar.copy(arow, m.ps[0:2, 6 + i % 2, 0:AC]).then_inc(aev, 1)
                    act.wait_ge(aev, i + 1)
                    nc.scalar.dma_start(m.mod_dram[:, j * AC:(j + 1) * AC], arow).then_inc(ast, 16)
                act.wait_ge(ast, 16 * len(ada))

            @block.vector
            def _(dve):
                step = Chain(dve, chain)
                cx = ComplexSteps(nc, step)
                v = nc.vector
                dve.wait_ge(ld, 80)
                v.tensor_copy(rows[:, 4, :].rearrange("q (g p) -> q g p", g=2), bc(ldt[:, :], 2, ST)).then_inc(ldp, 1)
                dve.wait_ge(tr, 1)
                v.tensor_copy(prm[:, :, :], m.ps[:, 0, 0:5 * PAIR].rearrange("p (a q) -> p a q", a=5)).then_inc(trd, 1)
                dve.wait_ge(trd, 1)
                dve.wait_ge(a1, 1)
                v.tensor_tensor(adt, ar, dt, ALU.mult).then_inc(a3, 1)
                step(v.tensor_tensor(ang, ai, dt, ALU.mult))
                step(v.tensor_scalar(ang8, ang, float(T), None, ALU.mult))
                for angle, turns, red, quarter in ((ang, n1, r1, ab1), (ang8, n8, rr8, ab8)):
                    step(v.tensor_scalar(turns, angle, 1.0 / (2 * math.pi), ROUND, ALU.mult, ALU.add))
                    step(v.tensor_scalar(turns, turns, -ROUND, None, ALU.add))
                    step(v.scalar_tensor_tensor(red, turns, -TWO_PI_HI, angle, ALU.mult, ALU.add))
                    step(v.scalar_tensor_tensor(red, turns, -TWO_PI_MID, red, ALU.mult, ALU.add))
                    step(v.scalar_tensor_tensor(red, turns, -TWO_PI_LO, red, ALU.mult, ALU.add))
                    step(v.tensor_scalar(red, red, PI_BELOW, -PI_BELOW, ALU.min, ALU.max))
                    step(v.scalar_tensor_tensor(quarter, red, -1.0, red, ALU.mult, ALU.max))
                    i = v.tensor_scalar(quarter, quarter, -1.0, math.pi / 2, ALU.mult, ALU.add)
                    if angle is ang:
                        step(i)
                i.then_inc(th, 1)
                dve.wait_ge(trig, 1)
                dve.wait_ge(a2, 1)
                pr, pi = pw[:, 0, :, :], pw[:, 1, :, :]
                v.memset(pr[:, :, 0], 1.0)
                v.memset(pi[:, :, 0], 0.0)
                step(v.tensor_tensor(pr[:, :, 1], dec, cs, ALU.mult))
                step(v.tensor_tensor(pi[:, :, 1], dec, sn, ALU.mult))
                for n in (1, 2, 4):
                    tv = tmp[:, 0:PAIR * n].rearrange("p (q n) -> p q n", n=n)
                    cx.mul(pr[:, :, n + 1:2 * n + 1], pi[:, :, n + 1:2 * n + 1], pr[:, :, 1:n + 1], pi[:, :, 1:n + 1],
                           pr[:, :, n:n + 1].broadcast_to([P, PAIR, n]), pi[:, :, n:n + 1].broadcast_to([P, PAIR, n]), tv)
                lr, li = pr[:, :, 1], pi[:, :, 1]
                step(v.tensor_scalar(num, lr, -1.0, None, ALU.add))
                step(v.tensor_tensor(den, ar, ar, ALU.mult))
                step(v.tensor_tensor(t1, ai, ai, ALU.mult))
                step(v.tensor_tensor(den, den, t1, ALU.add))
                step(v.reciprocal(rden, den))
                step(v.tensor_tensor(cr, num, ar, ALU.mult))
                step(v.tensor_tensor(t1, li, ai, ALU.mult))
                step(v.tensor_tensor(cr, cr, t1, ALU.add))
                step(v.tensor_tensor(cr, cr, rden, ALU.mult))
                step(v.tensor_tensor(ci, li, ar, ALU.mult))
                step(v.tensor_tensor(t1, num, ai, ALU.mult))
                step(v.tensor_tensor(ci, ci, t1, ALU.subtract))
                step(v.tensor_tensor(ci, ci, rden, ALU.mult))
                dve.wait_ge(lc, 16 * (3 + PAIR))
                tv = tmp[:, 0:PAIR * J].rearrange("p (q j) -> p q j", j=J)
                cx.mul(bb[:, 0, :, :], bb[:, 1, :, :], bc(cr, 2, J), bc(ci, 2, J), b[:, 0, :, :], b[:, 1, :, :], tv)
                for q4 in range(4):
                    q = slice(4 * q4, 4 * q4 + 4)
                    tv = tmp[:, 0:4 * T * J].rearrange("p (q t j) -> p q t j", q=4, t=T)
                    rev = pw[:, :, q, T - 1::-1]
                    cx.mul(wt[:, 0, q], wt[:, 1, q], bc(rev[:, 0], 3, J), bc(rev[:, 1], 3, J),
                           bc(bb[:, 0, q, :], 2, T), bc(bb[:, 1, q, :], 2, T), tv)
                v.tensor_copy(s[:, 21, 0:1], wt[:, 0, 0, 0, 0:1]).then_inc(wtr, 1)
                dve.wait_ge(tr, 2)
                v.tensor_copy(cT[:, :, :, :].rearrange("p a q j -> p (a q j)"), m.ps[:, 1, :]).then_inc(cte, 1)
                dve.wait_ge(cte, 1)
                for q4 in range(4):
                    q = slice(4 * q4, 4 * q4 + 4)
                    tv = tmp[:, 0:4 * (T + 1) * J].rearrange("p (q t j) -> p q t j", q=4, t=T + 1)
                    cx.mul(m.V[:, 0, q], m.V[:, 1, q], bc(pr[:, q, :], 3, J), bc(pi[:, q, :], 3, J),
                           bc(cT[:, 0, q, :], 2, T + 1), bc(cT[:, 1, q, :], 2, T + 1), tv, negate_im=True)
                v.tensor_copy(s[:, 22, 0:1], wt[:, 0, 0, 0, 0:1]).then_inc(bbr, 1)
                for x in range(8):
                    dve.wait_ge(wps, x + 1)
                    v.tensor_copy(m.W[:, x // 4, 4 * (x % 4):4 * (x % 4) + 4, :].rearrange("p q n -> p (q n)"),
                                  m.ps[:, x % 6, :]).then_inc(wev, 1)
                tc, ts = m.rot[:, 0, :, :], m.rot[:, 1, :, :]
                v.memset(tc[:, :, 0], 1.0)
                v.memset(ts[:, :, 0], 0.0)
                step(v.tensor_copy(tc[:, :, 1], cs8))
                step(v.tensor_copy(ts[:, :, 1], sn8))
                n = 1
                while n < NCH:
                    tv = tmp[:, 0:PAIR * n].rearrange("p (q n) -> p q n", n=n)
                    cx.mul(tc[:, :, n + 1:2 * n + 1], ts[:, :, n + 1:2 * n + 1], tc[:, :, 1:n + 1], ts[:, :, 1:n + 1],
                           tc[:, :, n:n + 1].broadcast_to([P, PAIR, n]), ts[:, :, n:n + 1].broadcast_to([P, PAIR, n]), tv)
                    n *= 2
                v.tensor_copy(m.rot[:, :, :, S0:COLS], m.rot[:, :, :, 0:COLS - S0])
                step(v.tensor_copy(m.decay[:, :, :], bc(m.r8[:, :], 2, COLS)))
                v.memset(m.decay[:, :, 0], 0.0)
                v.memset(m.decay[:, :, S0], 0.0)
                v.tensor_copy(m.h0[:, :, :], prm[:, 2:4, :])
                i = v.tensor_tensor(dd[:, :, :], dd[:, :, :], bc(m.ident[0:J, 0:J], 1, G), ALU.mult)
                step(i)
                for x in range(8):
                    dve.wait_ge(kps, x // 2 + 1)
                    g0 = 8 * (x // 2) + x % 2
                    v.tensor_copy(ksb[:, g0:min(g0 + 8, G):2, :],
                                  m.ps[0:J, x % 6, :].rearrange("j (g n) -> j g n", n=P)).then_inc(kcp, 1)
                dve.wait_ge(kcp, 8)
                v.tensor_tensor(ksb[:, :, 0:J], ksb[:, :, 0:J], dd[:, :, :], ALU.add).then_inc(kev, 1)


def ssm_scan(nc, m, A, O):
    GQ, PQ = G // 4, PAIR // 4
    with ExitStack() as ctx:
        sb = lambda name, shape: ctx.enter_context(nc.sbuf_tensor(name, shape, F32))
        us = sb("sc_us", [SCH, GQ, T, J])
        uT = sb("sc_uT", [P, 2, GQ, COLS])
        z = sb("sc_z", [P, 4, PQ, COLS])
        hh = sb("sc_h", [P, 2, 2, PQ, COLS])
        yso = sb("sc_ys", [P, 2, GQ * SCH // 2])
        yst = sb("sc_ys_rows", [GQ * SCH, 2, P])
        y = [m.u[:, GQ * q:GQ * (q + 1), :, :].rearrange("c g t i -> c (g t i)").rearrange("c (t n) -> c t n", t=T)
             for q in range(4)]
        h1 = sb("sc_seen", [P, 1])
        last = sb("sc_last", [P, 4, PAIR])
        lastT = m.tokqi[0:PAIR, :, :].rearrange("q a n -> q (a n)").rearrange("q (a n) -> q a n", a=4)
        usl, zst = ([m.sem(f"sc_{n}{i}") for i in range(2)] for n in ("us_loaded", "z_stored"))
        up, ue, zp, chain, hr, yp, ye, ypt, zte, fin, fp, fe, fst, zero = (m.sem("sc_" + n) for n in (
            "u_transposed", "u_copied", "z_psum", "dve_chain", "h_ready", "y_psum", "y_gelu", "y_transposed",
            "zT_copied", "last_ready", "last_transposed", "last_copied", "last_stored", "zeroed"))
        zc = m.sem("sc_z_copied")

        def load_us(engine, half, q):
            if q:
                engine.wait_ge(up, q)
            for g in range(half * GQ // 2, (half + 1) * GQ // 2):
                c = q * P + g * J
                engine.dma_start(us[:, g, :, :], m.us_dram.rearrange("(c s) n -> c s n", s=T)[:, :, c:c + J]).then_inc(usl[half], 16)

        with nc.Block() as block:
            @block.sync
            def _(sp):
                def store_z(q):
                    sp.wait_ge(zte, q + 1)
                    dst = m.z_dram.rearrange("(c t) n -> c t n", t=T)
                    for g in range(GQ):
                        at = (GQ // 2 * (g % 2) + g // 2) * SCH
                        sp.dma_start(dst[:, :, q * P + g * J:q * P + (g + 1) * J],
                                     yst[at:at + SCH, q % 2, :].rearrange("c (t i) -> c t i", i=J)).then_inc(zst[q % 2], 16)

                for q in range(3):
                    load_us(sp, 0, q)
                store_z(0)
                load_us(sp, 0, 3)
                for q in range(1, 4):
                    store_z(q)
                sp.wait_ge(fe, 1)
                for j, o in enumerate((O.ssm_re_prompt, O.ssm_im_prompt, O.ssm_re_sample, O.ssm_im_sample)):
                    sp.dma_start(o[0, 0].rearrange("(q g) p -> q (g p)", g=2), lastT[:, j, :]).then_inc(fst, 16)
                sp.wait_ge(fst, 64)
                for i in range(2):
                    sp.wait_ge(zst[i], 32 * GQ)

            @block.gpsimd
            def _(pool):
                for q in range(4):
                    load_us(nc.gpsimd, 1, q)

            @block.tensor
            def _(pe):
                def inputs(q):
                    if q:
                        pe.wait_ge(zc, q)
                    for g in range(GQ):
                        src = m.u[:, GQ * q + g, :, :].rearrange("c t j -> c (t j)")
                        nc.tensor.transpose(m.ps[:, g // 4, (g % 4) * P:(g % 4 + 1) * P], src, m.ident[:, :])
                    for half in range(2):
                        pe.wait_ge(usl[half], 16 * GQ // 2 * (q + 1))
                    for g in range(GQ):
                        i = nc.tensor.transpose(m.ps[:, 2, g * SCH:(g + 1) * SCH], us[:, g, :, :].rearrange("c t j -> c (t j)"),
                                                m.ident[0:SCH, 0:SCH])
                    i.then_inc(up, 1)
                    pe.wait_ge(ue, q + 1)
                    for c in range(2):
                        for n in range(PQ):
                            x = PQ * c + n
                            for g in range(2):
                                i = nc.tensor.matmul(
                                    m.ps[ST * g:ST * (g + 1), x // 3, (x % 3) * COLS:(x % 3 + 1) * COLS],
                                    m.W[:, c, PQ * q + n, ST * g:ST * (g + 1)], uT[:, q % 2, 2 * n + g, :], start=True, stop=True)
                    i.then_inc(zp, 1)

                def outputs(q):
                    pe.wait_ge(hr, q + 1)
                    if q:
                        pe.wait_ge(zte, q)
                    for g in range(GQ):
                        h = slice(ST * (g % 2), ST * (g % 2 + 1))
                        out = m.ps[:, 3 + g % 2, (g // 2) * P:(g // 2 + 1) * P]
                        nc.tensor.matmul(out, uT[:, q % 2, g, 1:1 + NCH], m.M[:, GQ * q + g, :], start=True, stop=False)
                        for c in range(2):
                            nc.tensor.matmul(out, hh[h, q % 2, c, g // 2, 0:NCH],
                                             m.V[h, c, PQ * q + g // 2, 1:T + 1, :].rearrange("p t i -> p (t i)"),
                                             start=False, stop=c == 1)
                    for g in range(GQ):
                        h = slice(ST * (g % 2), ST * (g % 2 + 1))
                        out = m.ps[:, 5 + g % 2, (g // 2) * SCH:(g // 2 + 1) * SCH]
                        nc.tensor.matmul(out, m.M[:, GQ * q + g, :], uT[:, q % 2, g, S0 + 1:COLS], start=True, stop=False)
                        for c in range(2):
                            i = nc.tensor.matmul(out, m.V[h, c, PQ * q + g // 2, 1:T + 1, :].rearrange("p t i -> p (t i)"),
                                                 hh[h, q % 2, c, g // 2, S0:S0 + SCH], start=False, stop=c == 1)
                    i.then_inc(yp, 1)
                    pe.wait_ge(ye, q + 1)
                    for t in range(T):
                        nc.tensor.transpose(m.ps[:, 3 + t // 4, (t % 4) * P:(t % 4 + 1) * P], y[q][:, t, :], m.ident[:, :])
                    i = nc.tensor.transpose(m.ps[0:GQ * SCH, 5, 0:P], yso[:, :, :].rearrange("p x n -> p (x n)"), m.ident[:, :])
                    i.then_inc(ypt, 1)

                pe.wait_ge(zero, 1)
                inputs(0)
                inputs(1)
                for q in range(4):
                    outputs(q)
                    if q + 2 < 4:
                        inputs(q + 2)
                pe.wait_ge(fin, 1)
                for j in range(4):
                    i = nc.tensor.transpose(m.ps[0:PAIR, 7, j * P:(j + 1) * P], last[:, j, :], m.ident[:, :])
                i.then_inc(fp, 1)

            @block.scalar
            def _(act):
                def inputs(q):
                    act.wait_ge(up, q + 1)
                    for x in range(2):
                        nc.scalar.copy(uT[:, q % 2, 4 * x:4 * x + 4, 1:NCH + 1], m.ps[:, x, :].rearrange("p (g c) -> p g c", g=4))
                    nc.scalar.copy(uT[:, q % 2, :, S0 + 1:COLS],
                                   m.ps[:, 2, 0:GQ * SCH].rearrange("p (g c) -> p g c", g=GQ)).then_inc(ue, 1)

                act.wait_ge(zero, 1)
                inputs(0)
                inputs(1)
                for q in range(4):
                    act.wait_ge(yp, q + 1)
                    for x in range(2):
                        nc.scalar.activation(y[q].rearrange("c t (g i) -> c t g i", i=J)[:, :, x:GQ:2, :],
                                             m.ps[:, 3 + x, :].rearrange("c (g t i) -> c t g i", g=4, t=T), ACT.Gelu_apprx_tanh)
                    nc.scalar.activation(yso[:, :, :], m.ps[:, 5:7, 0:GQ * SCH // 2], ACT.Gelu_apprx_tanh).then_inc(ye, 1)
                    act.wait_ge(ypt, q + 1)
                    for x in range(2):
                        nc.scalar.copy(m.zT[:, q, 0:SEQ].rearrange("p (c t) -> p t c", t=T)[:, 4 * x:4 * x + 4, :],
                                       m.ps[:, 3 + x, :].rearrange("p (t c) -> p t c", t=4))
                    if q >= 2:
                        act.wait_ge(zst[q % 2], 16 * GQ)
                    nc.scalar.copy(yst[:, q % 2, :], m.ps[0:GQ * SCH, 5, 0:P]).then_inc(zte, 1)
                    if q + 2 < 4:
                        inputs(q + 2)

            @block.vector
            def _(dve):
                step = Chain(dve, chain)
                v = nc.vector
                for b in range(2):
                    v.memset(uT[:, b, :, 0], 0.0)
                    i = v.memset(uT[:, b, :, S0], 0.0)
                i.then_inc(zero, 1)
                for q in range(4):
                    dve.wait_ge(zp, q + 1)
                    zr, zi, tr, ti = (z[:, j, :, :] for j in range(4))
                    zf = z[:, 0:2, :, :].rearrange("p a q c -> p (a q c)")
                    step(v.tensor_copy(zf[:, 0:6 * COLS].rearrange("p (b c) -> p b c", b=2), m.ps[:, 0:2, 0:3 * COLS]))
                    step(v.tensor_copy(zf[:, 6 * COLS:8 * COLS], m.ps[:, 2, 0:2 * COLS]))
                    v.tensor_copy(h1[:, 0:1], zf[:, 8 * COLS - 1:8 * COLS]).then_inc(zc, 1)
                    qs = slice(PQ * q, PQ * (q + 1))
                    step(v.tensor_copy(z[:, 0:2, :, S0], m.h0[:, :, qs]))
                    rc, rs = m.rot[:, 0, qs, :], m.rot[:, 1, qs, :]
                    step(v.tensor_tensor(tr, zr, rc, ALU.mult))
                    step(v.tensor_tensor(ti, zi, rs, ALU.mult))
                    step(v.tensor_tensor(tr, tr, ti, ALU.add))
                    step(v.tensor_tensor(ti, zi, rc, ALU.mult))
                    step(v.tensor_tensor(zr, zr, rs, ALU.mult))
                    step(v.tensor_tensor(ti, ti, zr, ALU.subtract))
                    flat = lambda a: a.rearrange("p q c -> p (q c)")
                    dec = flat(m.decay[:, qs, :])
                    step(v.tensor_tensor_scan(flat(zr), dec, flat(tr), 0.0, ALU.mult, ALU.add))
                    step(v.tensor_tensor_scan(flat(zi), dec, flat(ti), 0.0, ALU.mult, ALU.add))
                    if q >= 2:
                        dve.wait_ge(yp, q - 1)
                    hre, him = hh[:, q % 2, 0, :, :], hh[:, q % 2, 1, :, :]
                    step(v.tensor_tensor(hre, zr, rc, ALU.mult))
                    step(v.tensor_tensor(ti, zi, rs, ALU.mult))
                    step(v.tensor_tensor(hre, hre, ti, ALU.subtract))
                    step(v.tensor_tensor(him, zi, rc, ALU.mult))
                    step(v.tensor_tensor(ti, zr, rs, ALU.mult))
                    step(v.tensor_tensor(him, him, ti, ALU.add))
                    v.tensor_copy(last[:, 0:2, qs], hh[:, q % 2, :, :, NCH])
                    v.tensor_copy(last[:, 2:4, qs], hh[:, q % 2, :, :, COLS - 1]).then_inc(hr, 1)
                dve.wait_ge(hr, 4)
                v.tensor_copy(last[:, :, 0:1], last[:, :, 0:1]).then_inc(fin, 1)
                dve.wait_ge(fp, 1)
                v.tensor_copy(lastT[:, :, :].rearrange("q a n -> q (a n)"), m.ps[0:PAIR, 7, :]).then_inc(fe, 1)


SEL = range(2, PT)
SC_COL = {t: P * sum(j + 1 for j in range(2, t)) for t in SEL}
SC_SAMPLE = P * sum(j + 1 for j in SEL)
SC_W = SC_SAMPLE + PAST + DEC
MK_COL = {t: P * sum(j + 1 for j in range(t)) for t in range(PT)}
MK_SAMPLE = P * sum(j + 1 for j in range(PT))
MK_W = MK_SAMPLE + PAST + DEC


def keys_of(t):
    return (P * (t + 1), MK_COL[t]) if t < PT else (PAST + DEC, MK_SAMPLE)


def pieces(n, size=1024):
    return [(k, min(size, n - k)) for k in range(0, n, size)]


def index_scores(nc, m):
    tiles = [PT] + list(SEL)
    units = [(i, t, k, w) for i, t in enumerate(tiles) for k, w in pieces(PAST + DEC if t == PT else P * (t + 1))]
    steps = [(i, t, k, w, h) for i, t, k, w in units for h in range(IH // 2 if t == PT else IH)]
    with ExitStack() as ctx:
        sb = lambda name, shape: ctx.enter_context(nc.sbuf_tensor(name, shape, F32))
        relu = sb("ix_relu", [P, 4, 1024])
        qz = sb("ix_q", [P, 2, IH, P])
        qs = sb("ix_q_sample", [P, IH // 2, P])
        ws = sb("ix_w_sample", [P, IH // 2])
        other = sb("ix_other_half", [DEC, PAST + DEC])
        ps, rl, acc, qr, zero, wsl, ol = (m.sem("ix_" + n) for n in (
            "psum", "relu", "added", "queries_ready", "zeroed", "w_sample_loaded", "other_loaded"))
        before = [next(n for n, s in enumerate(steps) if s[0] == i) for i in range(len(tiles))]
        with nc.Block() as block:
            @block.sync
            def _(sp):
                for x in range(2):
                    sp.dma_start(ws[DEC * x:DEC * (x + 1), :], m.wi[0:DEC, PT, IH // 2 * x:IH // 2 * (x + 1)]).then_inc(wsl, 16)
                sp.wait_ge(acc, before[1])
                sp.dma_start(other[:, :], m.sc[DEC:P, SC_SAMPLE:SC_SAMPLE + PAST + DEC]).then_inc(ol, 16)

            @block.gpsimd
            def _(pool):
                nc.gpsimd.memset(qs[:, :, :], 0.0)
                nc.gpsimd.memset(qz[:, :, :, :], 0.0).then_inc(zero, 1)
                pool.wait_ge(zero, 1)
                for i, t in enumerate(tiles):
                    if i >= 3:
                        pool.wait_ge(ps, before[i - 1])
                    for x in range(4):
                        rows = slice(ID * x, ID * (x + 1))
                        if t == PT:
                            j = nc.gpsimd.tensor_copy(qs[rows, x, :].rearrange("p (a n) -> p a n", a=2), m.qiT[rows, :, SEQ:NT])
                        else:
                            j = nc.gpsimd.tensor_copy(qz[rows, i % 2, x:IH:4, :], m.qiT[rows, :, t * P:(t + 1) * P])
                    j.then_inc(qr, 1)

            @block.tensor
            def _(pe):
                for n, (i, t, k0, w, h) in enumerate(steps):
                    if n in before:
                        pe.wait_ge(qr, i + 1)
                    if n >= 4:
                        pe.wait_ge(rl, n - 3)
                    src, q = (m.kiTs, qs[:, h, :]) if t == PT else (m.kiT, qz[:, i % 2, h, :])
                    for c, (k, x) in enumerate(pieces(w, 512)):
                        j = nc.tensor.matmul(m.ps[:, 2 * (n % 4) + c, 0:x], q, src[:, k0 + k:k0 + k + x], start=True, stop=True)
                    j.then_inc(ps, 1)

            @block.scalar
            def _(act):
                for n, (_, _, _, w, _) in enumerate(steps):
                    act.wait_ge(ps, n + 1)
                    if n >= 4:
                        act.wait_ge(acc, n - 3)
                    src = m.ps[:, 2 * (n % 4):2 * (n % 4) + 2, :].rearrange("p b n -> p (b n)")
                    nc.scalar.activation(relu[:, n % 4, 0:w], src[:, 0:w], ACT.Relu).then_inc(rl, 1)

            @block.vector
            def _(dve):
                dve.wait_ge(wsl, 32)
                for n, (_, t, k0, w, h) in enumerate(steps):
                    c = (SC_COL[t] if t < PT else SC_SAMPLE) + k0
                    sc = m.sc[:, c:c + w]
                    wt = m.wi[:, t, h:h + 1] if t < PT else ws[:, h:h + 1]
                    dve.wait_ge(rl, n + 1)
                    if h == 0:
                        i = nc.vector.tensor_scalar(sc, relu[:, n % 4, 0:w], wt, None, ALU.mult)
                    else:
                        i = nc.vector.scalar_tensor_tensor(sc, relu[:, n % 4, 0:w], wt, sc, ALU.mult, ALU.add)
                    i.then_inc(acc, 1)
                    dve.wait_ge(acc, n + 1)
                    if t < PT and h == IH - 1:
                        nc.vector.memset(m.sc[0:DEC, c + w - DEC:c + w], NEG)
                dve.wait_ge(ol, 16)
                total = m.sc[0:DEC, SC_SAMPLE:SC_SAMPLE + PAST + DEC]
                nc.vector.tensor_tensor(total, total, other[:, :], ALU.add)


SPANS = ((0, 512), (512, 512), (1024, DEC))


def select_keys_and_gates(nc, m, A):
    GB, GA, GG, GV = range(4)
    NB = 2
    units = [(c, lo, n) for c in range(KD) for lo, n in SPANS]
    kp = lambda a: a.rearrange("(k p) n -> p k n", p=P)
    parts = ((GB, 0, KD, kp(A.w_in), OFF_GB, m.hT), (GA, 8, KD, kp(A.w_in), OFF_GA, m.hT),
             (GG, 16, 4, kp(A.w_glu), D, m.zT), (GV, 20, 4, kp(A.w_glu), 0, m.zT))
    NL = len(SEL) + 1
    lists = [(P, SC_COL[t], P * (t + 1), MK_COL[t]) for t in SEL] + [(DEC, SC_SAMPLE, PAST + DEC, MK_SAMPLE)]
    with ExitStack() as ctx:
        sb = lambda name, shape, dt=F32: ctx.enter_context(nc.sbuf_tensor(name, shape, dt))
        thr = sb("tk_thr", [P, NL], I32)
        cand = sb("tk_cand", [P, NL], I32)
        neg = sb("tk_neg", [P, NL])
        negi = sb("tk_negi", [P, NL], I32)
        take = sb("tk_take", [P, NL], I32)
        cnt = sb("tk_cnt", [P, NL])
        bit = sb("tk_bit", [P, 1], I32)
        hits = sb("tk_hits", [P, PAST + DEC], BF16)
        eq = sb("tk_eq", [P, PAST + DEC])
        pre = sb("tk_pre", [P, PAST + DEC])
        w = sb("gt_w", [P, NB, 24, P])
        sga = sb("gt_sig_a", [P, 2, 512])
        sgg = sb("gt_sig_g", [P, 2, 512])
        gv = sb("gt_value", [P, 2, 512])
        gb = sb("gt_sig_b", [P, 2, NT])
        left = m.qiT
        chain, loop, done, dup = m.sem("tk_chain"), m.sem("tk_loop"), m.sem("tk_mask_ready"), m.sem("tk_mask_copied")
        wl, st = ([m.sem(f"gt_{n}{i}") for i in range(2)] for n in ("w_loaded", "stored"))
        ql = m.sem("gt_q_loaded")
        ps, ev, pc = m.sem("gt_psum"), m.sem("gt_from_psum"), m.sem("gt_pool_chain")
        with nc.Block() as block:
            @block.sync
            def _(sp):
                def load(c):
                    for _, at, n, src, off, _ in parts:
                        sp.dma_start(w[:, c % NB, at:at + n, :], src[:, :, off + c * P:off + (c + 1) * P]).then_inc(wl[c % NB], 16)

                load(0)
                load(1)
                sp.dma_start(m.attnT[:, :, :], m.q_dram).then_inc(ql, 16)
                for c in range(KD):
                    if c + NB < KD:
                        sp.wait_ge(ps, 12 * (c + 1))
                        load(c + NB)
                    sp.wait_ge(ev, 12 * (c + 1))
                    sp.wait_ge(pc, 6 * (c + 1))
                    sp.dma_start(m.gb_dram[:, c, :], gb[:, c % 2, :]).then_inc(st[c % 2], 16)
                    sp.dma_start(m.left_dram[:, c, :], left[:, c % 2, :]).then_inc(st[c % 2], 16)
                sp.wait_ge(done, 1)
                sp.dma_start(m.mask[DEC:P, MK_SAMPLE:MK_W], m.mask[0:DEC, MK_SAMPLE:MK_W]).then_inc(dup, 16)
                sp.wait_ge(dup, 16)
                sp.wait_ge(ql, 16)
                for i in range(2):
                    sp.wait_ge(st[i], 32 * KD // 2)

            @block.tensor
            def _(pe):
                for u, (c, lo, n) in enumerate(units):
                    if u % 3 == 0:
                        pe.wait_ge(wl[c % NB], 64 * (c // NB + 1))
                    for j, at, nk, _, _, rhs in parts:
                        seq = 4 * u + j
                        if seq >= 8:
                            pe.wait_ge(ev, seq - 7)
                        for k in range(nk):
                            i = nc.tensor.matmul(m.ps[:, seq % 8, 0:n], w[:, c % NB, at + k, :], rhs[:, k, lo:lo + n],
                                                 start=k == 0, stop=k == nk - 1)
                        i.then_inc(ps, 1)

            @block.scalar
            def _(act):
                for u, (c, lo, n) in enumerate(units):
                    if u % 3 == 0 and c >= 2:
                        act.wait_ge(st[c % 2], 32 * (c // 2))
                    if u >= 2:
                        act.wait_ge(pc, 2 * (u - 1))
                    for j, dst in ((GB, gb[:, c % 2, lo:lo + n]), (GA, sga[:, u % 2, 0:n]), (GG, sgg[:, u % 2, 0:n])):
                        act.wait_ge(ps, 4 * u + j + 1)
                        nc.scalar.activation(dst, m.ps[:, (4 * u + j) % 8, 0:n], ACT.Sigmoid).then_inc(ev, 1)
                    act.wait_ge(ps, 4 * u + GV + 1)
                    nc.scalar.copy(gv[:, u % 2, 0:n], m.ps[:, (4 * u + GV) % 8, 0:n]).then_inc(ev, 1)

            @block.gpsimd
            def _(pool):
                step = Chain(pool, pc)
                for u, (c, lo, n) in enumerate(units):
                    pool.wait_ge(ev, 4 * u + 4)
                    if u % 3 == 0 and c >= 2:
                        pool.wait_ge(st[c % 2], 32 * (c // 2))
                    step(nc.gpsimd.tensor_tensor(gv[:, u % 2, 0:n], gv[:, u % 2, 0:n], sgg[:, u % 2, 0:n], ALU.mult))
                    step(nc.gpsimd.tensor_tensor(left[:, c % 2, lo:lo + n], gv[:, u % 2, 0:n], sga[:, u % 2, 0:n], ALU.mult))

            @block.vector
            def _(dve):
                step = Chain(dve, chain)
                v = nc.vector

                def count(j, scalar):
                    r, c, w, _ = lists[j]
                    return v.tensor_scalar(hits[0:r, 0:w], m.sc[0:r, c:c + w], scalar, 0.0, ALU.is_ge, ALU.add,
                                           accum_out=cnt[0:r, j:j + 1])

                step(v.memset(cnt[:, :], 0.0))
                for j in range(NL):
                    step(count(j, 0.0))
                step(v.tensor_scalar(neg[:, :], cnt[:, :], TOPK - 0.5, None, ALU.is_lt))
                step(v.tensor_copy(negi[:, :], neg[:, :]))
                step(v.tensor_scalar(thr[:, :], negi[:, :], 31, None, ALU.logical_shift_left))
                step(v.memset(bit[:, :], 1 << 30))
                STEPS = NL + 4
                with dve.Fori(0, 31) as i:
                    at = STEPS * i
                    v.tensor_tensor(cand[:, :], thr[:, :], bit[:, :].broadcast_to([P, NL]), ALU.bitwise_or).then_inc(loop, 1)
                    dve.wait_ge(loop, at + 1)
                    for j in range(NL):
                        r = lists[j][0]
                        count(j, cand[0:r, j:j + 1].bitcast(F32)).then_inc(loop, 1)
                        dve.wait_ge(loop, at + 2 + j)
                    v.scalar_tensor_tensor(take[:, :], cnt[:, :], TOPK - 0.5, neg[:, :], ALU.is_ge, ALU.not_equal).then_inc(loop, 1)
                    dve.wait_ge(loop, at + STEPS - 2)
                    v.tensor_scalar(bit[:, :], bit[:, :], 1, None, ALU.logical_shift_right).then_inc(loop, 1)
                    v.copy_predicated(thr[:, :], take[:, :], cand[:, :]).then_inc(loop, 1)
                    dve.wait_ge(loop, at + STEPS)
                step(v.tensor_tensor(thr[:, :], thr[:, :], negi[:, :], ALU.add))
                for j, (r, c, w, mc) in enumerate(lists):
                    sc, mk, tf = m.sc[0:r, c:c + w], m.mask[0:r, mc:mc + w], thr[0:r, j:j + 1].bitcast(F32)
                    e, p, need = eq[0:r, 0:w], pre[0:r, 0:w], cnt[0:r, j:j + 1]
                    step(v.tensor_scalar(mk, sc, tf, 0.0, ALU.is_gt, ALU.add, accum_out=need))
                    step(v.tensor_scalar(need, need, -1.0, float(TOPK), ALU.mult, ALU.add))
                    step(v.tensor_scalar(e, sc, tf, None, ALU.is_equal))
                    step(v.tensor_tensor_scan(p, m.ones[0:r, 0:1].broadcast_to([r, w]), e, 0.0, ALU.mult, ALU.add))
                    step(v.scalar_tensor_tensor(e, p, need, e, ALU.is_le, ALU.mult))
                    step(v.scalar_tensor_tensor(mk, e, -1.0, mk, ALU.add, ALU.add))
                    step(v.tensor_scalar(mk, mk, -NEG, None, ALU.mult))
                step(v.memset(m.mask[:, 0:3 * P], 0.0))
                for t in range(2):
                    c = MK_COL[t] + P * (t + 1)
                    i = v.memset(m.mask[0:DEC, c - DEC:c], NEG)
                    if t:
                        i.then_inc(done, 1)
                    else:
                        step(i)


def attention(nc, m, A):
    order = range(PT, -1, -1)
    units = [(p, t, h) for p, t in enumerate(order) for h in range(H // 2 if t == PT else H)]
    first = [units.index((p, t, 0)) for p, t in enumerate(order)]
    NU = len(units)
    chunks = [pieces(keys_of(t)[0]) for _, t, _ in units]
    blocks = [pieces(keys_of(t)[0], P) for _, t, _ in units]
    groups = [[b[i:i + 4] for i in range(0, len(b), 4)] for b in blocks]
    c_at = [sum(map(len, chunks[:u])) for u in range(NU + 1)]
    g_at = [sum(map(len, groups[:u])) for u in range(NU + 1)]
    SCALE = HD ** -0.5
    with ExitStack() as ctx:
        sb = lambda name, shape, dt=F32: ctx.enter_context(nc.sbuf_tensor(name, shape, dt))
        qb = sb("at_qb", [P, 4, P])
        s = sb("at_s", [P, 3, PAST + DEC])
        pT = sb("at_pT", [P, 2, CB + 1, P])
        mx = sb("at_mx", [P, 4, 4])
        nb = sb("at_nb", [P, NU])
        sm = sb("at_sum", [P, NU])
        rs = sb("at_rsum", [P, NU])
        o = sb("at_o", [P, 2, 512])
        os_ = sb("at_os", [P, 4, HD])
        wol = m.sem("at_w_out_loaded")
        qz, sp_, sd, mxr, nbr, er, tp, te, pv, oc, rr, otp, ote, osr, osm = (m.sem("at_" + n) for n in (
            "qb_ready", "s_psum", "s_masked", "max_ready", "bias_ready", "exp_ready", "p_transposed", "p_copied",
            "pv_psum", "o_copied", "recip_ready", "o_transposed", "oT_copied", "os_ready", "os_moved"))
        with nc.Block() as block:
            @block.tensor
            def _(pe):
                def scores(u):
                    _, t, h = units[u]
                    for c, (k0, w) in enumerate(chunks[u]):
                        n = c_at[u] + c
                        if n >= 2:
                            pe.wait_ge(sd, n - 1)
                        for b, (k, x) in enumerate(pieces(w, 512)):
                            out = m.ps[:, 2 * (n % 2) + b, 0:x]
                            if t < PT:
                                half = slice(HD * (h % 2), HD * (h % 2 + 1))
                                i = nc.tensor.matmul(out, m.attnT[half, h // 2, t * P:(t + 1) * P],
                                                     m.kT[half, k0 + k:k0 + k + x], start=True, stop=True)
                            else:
                                i = nc.tensor.matmul(out, qb[:, h, :], m.kTs[:, k0 + k:k0 + k + x], start=True, stop=True)
                        i.then_inc(sp_, 1)

                def transposes(u):
                    pe.wait_ge(er, u + 1)
                    for g, bs in enumerate(groups[u]):
                        n = g_at[u] + g
                        if n >= 2:
                            pe.wait_ge(te, n - 1)
                        for j, (k, x) in enumerate(bs):
                            i = nc.tensor.transpose(m.ps[0:x, 4 + n % 2, j * P:(j + 1) * P], s[:, u % 3, k:k + x], m.ident[:, :])
                        i.then_inc(tp, 1)

                def values(u):
                    p, t, h = units[u]
                    pe.wait_ge(te, g_at[u + 1])
                    if h == 0 and p:
                        pe.wait_ge(oc, p)
                    src = m.v if t < PT else m.vs
                    for b, (k, x) in enumerate(blocks[u]):
                        i = nc.tensor.matmul(m.ps[:, 6, h * HD:(h + 1) * HD], pT[0:x, u % 2, b, :], src[0:x, b, :],
                                             start=b == 0, stop=b == len(blocks[u]) - 1)
                    i.then_inc(pv, 1)

                def output(p):
                    pe.wait_ge(oc, p + 1)
                    r = rows_of(order[p])
                    if order[p] == PT:
                        pe.wait_ge(osm, 32)
                    if p:
                        pe.wait_ge(ote, p)
                    for j in range(4):
                        i = nc.tensor.transpose(m.ps[:, 7, j * P:j * P + r], o[0:r, p % 2, j * P:(j + 1) * P], m.ident[0:r, 0:r])
                    i.then_inc(otp, 1)

                pe.wait_ge(qz, 4)
                scores(0)
                scores(1)
                for u in range(NU + 1):
                    if u + 2 < NU:
                        scores(u + 2)
                    if u < NU:
                        transposes(u)
                    if u:
                        values(u - 1)
                        p, _, h = units[u - 1]
                        if h == 3 and p:
                            output(p - 1)
                output(PT)

            @block.vector
            def _(dve):
                v = nc.vector

                def normalise(p):
                    a, n = first[p], H // 2 if order[p] == PT else H
                    dve.wait_ge(pv, a + n)
                    v.reciprocal(rs[:, a:a + n], sm[:, a:a + n]).then_inc(rr, 1)
                    dve.wait_ge(rr, p + 1)
                    if p >= 2:
                        dve.wait_ge(otp, p - 1)
                    dst = os_[:, :, :] if order[p] == PT else o[:, p % 2, :].rearrange("p (h d) -> p h d", d=HD)
                    v.tensor_tensor(dst, m.ps[:, 6, 0:n * HD].rearrange("p (h d) -> p h d", d=HD),
                                    bc(rs[:, a:a + n], 2, HD), ALU.mult).then_inc(oc, 1)

                def place(p):
                    dve.wait_ge(otp, p + 1)
                    t, r = order[p], rows_of(order[p])
                    v.tensor_copy(m.attnT[:, :, t * P:t * P + r],
                                  m.ps[:, 7, :].rearrange("p (j t) -> p j t", t=P)[:, :, 0:r]).then_inc(ote, 1)

                v.memset(qb[:, :, :], 0.0).then_inc(qz, 1)
                dve.wait_ge(qz, 1)
                for x in range(2):
                    half = slice(HD * x, HD * (x + 1))
                    v.tensor_copy(qb[half, :, DEC * x:DEC * (x + 1)], m.attnT[half, :, SEQ:NT]).then_inc(qz, 1)
                v.memset(sm[:, :], 0.0).then_inc(qz, 1)
                for u, (p, t, h) in enumerate(units):
                    mc = keys_of(t)[1]
                    if u >= 3:
                        dve.wait_ge(tp, g_at[u - 2])
                    for c, (k0, w) in enumerate(chunks[u]):
                        n = c_at[u] + c
                        dve.wait_ge(sp_, n + 1)
                        src = m.ps[:, 2 * (n % 2):2 * (n % 2) + 2, :].rearrange("p b n -> p (b n)")[:, 0:w]
                        v.tensor_tensor_reduce(out=s[:, u % 3, k0:k0 + w], in0=src, in1=m.mask[:, mc + k0:mc + k0 + w],
                                               scale=1.0, scalar=-3.0e38, op0=ALU.add, op1=ALU.max,
                                               accum_out=mx[:, u % 4, c:c + 1]).then_inc(sd, 1)
                    dve.wait_ge(sd, c_at[u + 1])
                    v.tensor_reduce(mx[:, u % 4, 3:4], mx[:, u % 4, 0:len(chunks[u])], AX.X, ALU.max).then_inc(mxr, 1)
                    dve.wait_ge(mxr, u + 1)
                    v.tensor_scalar(nb[:, u:u + 1], mx[:, u % 4, 3:4], -SCALE, None, ALU.mult).then_inc(nbr, 1)
                    if h == 2 and p:
                        normalise(p - 1)
                    if h == 5 and p:
                        place(p - 1)
                normalise(PT)
                place(PT)

            @block.scalar
            def _(act):
                def copies(u):
                    for g, bs in enumerate(groups[u]):
                        n = g_at[u] + g
                        act.wait_ge(tp, n + 1)
                        if u >= 2 and g == 0:
                            act.wait_ge(pv, u - 1)
                        x = bs[-1][1]
                        if x == P:
                            i = nc.scalar.copy(pT[:, u % 2, 4 * g:4 * g + len(bs), :].rearrange("p b n -> p (b n)"),
                                               m.ps[:, 4 + n % 2, 0:len(bs) * P])
                        else:
                            i = nc.scalar.copy(pT[0:x, u % 2, 4 * g, :], m.ps[0:x, 4 + n % 2, 0:P])
                        i.then_inc(te, 1)

                for u, (_, t, _) in enumerate(units):
                    n = keys_of(t)[0]
                    act.wait_ge(nbr, u + 1)
                    nc.scalar.activation(s[:, u % 3, 0:n], s[:, u % 3, 0:n], ACT.Exp, bias=nb[:, u:u + 1], scale=SCALE,
                                         accum_out=sm[:, u:u + 1]).then_inc(er, 1)
                    if u:
                        copies(u - 1)
                copies(NU - 1)

            @block.sync
            def _(sp):
                def load_next():
                    wo = A.w_out.rearrange("(k p) n -> p k n", p=P)
                    for k in range(KD):
                        sp.dma_start(m.wout[:, k, :], wo[:, k, :]).then_inc(wol, 16)
                    load_mod_rows(m, sp, m.modA, (2, 4), wol)

                sp.wait_ge(oc, 1)
                dst = o[0:DEC, 0, :].rearrange("p (j x d) -> p j x d", j=4, x=2)
                for x in range(2):
                    sp.dma_start(dst[:, :, x, :], os_[DEC * x:DEC * (x + 1), :, :]).then_inc(osm, 16)
                load_next()
                sp.wait_ge(osm, 32)
                sp.wait_ge(wol, 16 * KD + 64)


def merge(nc, m, A):
    NB = 3
    units = [(c, lo, n) for c in range(KD) for lo, n in SPANS]
    with ExitStack() as ctx:
        sb = lambda name, shape: ctx.enter_context(nc.sbuf_tensor(name, shape, F32))
        w = sb("mg_w", [P, 4, D])
        gb = sb("mg_gb", [P, NB, NT])
        tt = sb("mg_t", [P, 2, 512])
        wl, gl = m.sem("mg_w_loaded"), [m.sem(f"mg_gate_loaded{i}") for i in range(NB)]
        ps, dv, mbl = m.sem("mg_psum"), m.sem("mg_dve_chain"), m.sem("mg_mod_loaded")
        with nc.Block() as block:
            @block.sync
            def _(sp):
                sp.dma_start(w[:, :, :], A.w_attn_out.rearrange("(k p) n -> p k n", p=P)).then_inc(wl, 16)
                for c in range(KD):
                    if c >= NB:
                        sp.wait_ge(dv, 6 * (c - NB + 1))
                    sp.dma_start(gb[:, c % NB, :], m.gb_dram[:, c, :]).then_inc(gl[c % NB], 16)
                    sp.dma_start(m.mergedT[:, c, :], m.left_dram[:, c, :]).then_inc(gl[c % NB], 16)
                load_mod_rows(m, sp, m.shift2, (3,), mbl)
                sp.wait_ge(mbl, 32)

            @block.tensor
            def _(pe):
                pe.wait_ge(wl, 16)
                for u, (c, lo, n) in enumerate(units):
                    if u >= 8:
                        pe.wait_ge(dv, 2 * (u - 8) + 1)
                    for k in range(4):
                        i = nc.tensor.matmul(m.ps[:, u % 8, 0:n], w[:, k, c * P:(c + 1) * P], m.attnT[:, k, lo:lo + n],
                                             start=k == 0, stop=k == 3)
                    i.then_inc(ps, 1)

            @block.vector
            def _(dve):
                step = Chain(dve, dv)
                v = nc.vector
                for u, (c, lo, n) in enumerate(units):
                    t, out = tt[:, u % 2, 0:n], m.mergedT[:, c, lo:lo + n]
                    if u % 3 == 0:
                        dve.wait_ge(gl[c % NB], 32 * (c // NB + 1))
                    dve.wait_ge(ps, u + 1)
                    step(v.tensor_tensor(t, m.ps[:, u % 8, 0:n], gb[:, c % NB, lo:lo + n], ALU.mult))
                    step(v.tensor_tensor(out, t, out, ALU.add))


def load_mod_rows(m, engine, dst, first, sem):
    for i, j in enumerate(first):
        for s in range(2):
            engine.dma_start(dst[:, i, s, :], m.mod_dram[s:s + 1, j * D:(j + 1) * D].broadcast_to([P, D])).then_inc(sem, 16)


def output_projection(nc, m, A):
    with ExitStack() as ctx:
        sb = lambda name, shape: ctx.enter_context(nc.sbuf_tensor(name, shape, F32))
        x = sb("op_x", [P, 2, D])
        xa = sb("op_xa", [P, 2, D])
        h2 = sb("op_h2", [P, 2, D])
        sq = sb("op_sq", [P, D])
        h2T = sb("op_h2T", [P, 2, KD, P])
        wr = sb("op_wr", [P, KD, NG + NE])
        st = sb("op_st", [P, TILES, 4])
        wl, xl = m.sem("op_w_loaded"), [m.sem(f"op_x_loaded{i}") for i in range(2)]
        x1s, h2s = ([m.sem(f"op_{n}_stored{i}") for i in range(2)] for n in ("x1", "h2"))
        pm, dm, pa, sqr, msr, rtr, rcp, hm, hr, tp, te, rp, re, one = (m.sem("op_" + n) for n in (
            "psum", "gated", "x1_ready", "squared", "mean", "root", "recip", "h2_scaled", "h2_ready",
            "transposed", "h2T_ready", "router_psum", "logits", "scale_ready"))
        g2l = m.sem("op_gate2_loaded")
        g1 = m.modA[:, 0, :, :]
        sc2 = m.modA[:, 1, :, :]
        sh2 = m.shift2[:, 0, :, :]
        with nc.Block() as block:
            @block.sync
            def _(sp):
                sp.dma_start(wr[:, :, 0:NG], A.w_route_group.rearrange("(k p) n -> p k n", p=P)).then_inc(wl, 16)
                sp.dma_start(wr[:, :, NG:], A.w_route_expert.rearrange("(k p) n -> p k n", p=P)).then_inc(wl, 16)
                for t in range(TILES + 1):
                    if t < TILES:
                        r = rows_of(t)
                        if t >= 2:
                            sp.wait_ge(pa, t - 1)
                        src = A.x_prompt[0, t * P:(t + 1) * P, :] if t < PT else A.x_sample[0, :, :]
                        sp.dma_start(x[0:r, t % 2, :], src).then_inc(xl[t % 2], 16)
                    if t:
                        u = t - 1
                        r = rows_of(u)
                        sp.wait_ge(pa, u + 1)
                        sp.dma_start(m.x1_dram[u * P:u * P + r, :], xa[0:r, u % 2, :]).then_inc(x1s[u % 2], 16)
                        sp.wait_ge(hr, u + 1)
                        sp.dma_start(m.h2_dram[u * P:u * P + r, :], h2[0:r, u % 2, :]).then_inc(h2s[u % 2], 16)
                load_mod_rows(m, sp, m.gate2, (5,), g2l)
                sp.wait_ge(g2l, 32)
                for i in range(2):
                    sp.wait_ge(x1s[i], 16 * ((TILES + 1 - i) // 2))
                    sp.wait_ge(h2s[i], 16 * ((TILES + 1 - i) // 2))

            @block.tensor
            def _(pe):
                def main(t):
                    r = rows_of(t)
                    if t >= 2:
                        pe.wait_ge(dm, t - 1)
                    for n in range(2):
                        for k in range(KD):
                            i = nc.tensor.matmul(m.ps[0:r, 2 * (t % 2) + n, :], m.mergedT[:, k, t * P:t * P + r],
                                                 m.wout[:, k, n * 512:(n + 1) * 512], start=k == 0, stop=k == KD - 1)
                    i.then_inc(pm, 1)

                def transposes(t):
                    r = rows_of(t)
                    pe.wait_ge(hr, t + 1)
                    if t:
                        pe.wait_ge(te, t)
                    for k in range(KD):
                        i = nc.tensor.transpose(m.ps[:, 4 + k // 4, (k % 4) * P:(k % 4) * P + r],
                                                h2[0:r, t % 2, k * P:(k + 1) * P], m.ident[0:r, 0:r])
                    i.then_inc(tp, 1)

                def route(t):
                    r = rows_of(t)
                    pe.wait_ge(te, t + 1)
                    if t >= 2:
                        pe.wait_ge(re, t - 1)
                    for k in range(KD):
                        i = nc.tensor.matmul(m.ps[0:r, 6 + t % 2, 0:NG + NE], h2T[:, t % 2, k, 0:r], wr[:, k, :],
                                             start=k == 0, stop=k == KD - 1)
                    i.then_inc(rp, 1)

                pe.wait_ge(wl, 32)
                for t in range(TILES + 2):
                    if t < TILES:
                        main(t)
                    if 1 <= t <= TILES:
                        transposes(t - 1)
                    if t >= 2:
                        route(t - 2)

            @block.gpsimd
            def _(pool):
                for t in range(TILES):
                    r = rows_of(t)
                    pool.wait_ge(dm, t + 1)
                    pool.wait_ge(xl[t % 2], 16 * (t // 2 + 1))
                    nc.gpsimd.tensor_tensor(xa[0:r, t % 2, :], xa[0:r, t % 2, :], x[0:r, t % 2, :], ALU.add).then_inc(pa, 1)
                    pool.wait_ge(hm, t + 1)
                    nc.gpsimd.tensor_tensor(h2[0:r, t % 2, :], h2[0:r, t % 2, :], sh2[0:r, int(t == PT), :],
                                            ALU.add).then_inc(hr, 1)

            @block.scalar
            def _(act):
                for t in range(TILES):
                    r = rows_of(t)
                    act.wait_ge(pa, t + 1)
                    if t:
                        act.wait_ge(sqr, t)
                    nc.scalar.activation(sq[0:r, :], xa[0:r, t % 2, :], ACT.Square, accum_out=st[0:r, t, 0:1]).then_inc(sqr, 1)
                    act.wait_ge(msr, t + 1)
                    nc.scalar.activation(st[0:r, t, 2:3], st[0:r, t, 1:2], ACT.Sqrt).then_inc(rtr, 1)
                    act.wait_ge(tp, t + 1)
                    if t >= 2:
                        act.wait_ge(rp, t - 1)
                    nc.scalar.copy(h2T[:, t % 2, :, 0:r].rearrange("p (b k) r -> p b k r", b=2),
                                   m.ps[:, 4:6, :].rearrange("p b (k r) -> p b k r", r=P)[:, :, :, 0:r]).then_inc(te, 1)

            @block.vector
            def _(dve):
                v = nc.vector

                def gated(t):
                    r = rows_of(t)
                    dve.wait_ge(pm, t + 1)
                    if t >= 2:
                        dve.wait_ge(x1s[t % 2], 16 * (t // 2))
                        dve.wait_ge(hm, t - 1)
                    v.tensor_tensor(xa[0:r, t % 2, :].rearrange("p (b n) -> p b n", b=2),
                                    m.ps[0:r, 2 * (t % 2):2 * (t % 2) + 2, :],
                                    g1[0:r, int(t == PT), :].rearrange("p (b n) -> p b n", b=2), ALU.mult).then_inc(dm, 1)

                def logits(t):
                    dve.wait_ge(rp, t + 1)
                    r = rows_of(t)
                    v.tensor_copy(m.logits[0:r, t, :], m.ps[0:r, 6 + t % 2, 0:NG + NE]).then_inc(re, 1)

                v.tensor_scalar(sc2, sc2, 1.0, None, ALU.add).then_inc(one, 1)
                v.memset(m.logits[:, :, :], 0.0).then_inc(one, 1)
                dve.wait_ge(one, 2)
                for t in range(TILES):
                    r = rows_of(t)
                    gated(t)
                    dve.wait_ge(sqr, t + 1)
                    v.tensor_scalar(st[0:r, t, 1:2], st[0:r, t, 0:1], 1.0 / D, EPS, ALU.mult, ALU.add).then_inc(msr, 1)
                    dve.wait_ge(rtr, t + 1)
                    v.reciprocal(st[0:r, t, 3:4], st[0:r, t, 2:3]).then_inc(rcp, 1)
                    dve.wait_ge(rcp, t + 1)
                    if t >= 2:
                        dve.wait_ge(tp, t - 1)
                        dve.wait_ge(h2s[t % 2], 16 * (t // 2))
                    v.scalar_tensor_tensor(h2[0:r, t % 2, :], xa[0:r, t % 2, :], st[0:r, t, 3:4], sc2[0:r, int(t == PT), :],
                                           ALU.mult, ALU.mult).then_inc(hm, 1)
                    if t:
                        logits(t - 1)
                logits(PT)


def routing(nc, m, A):
    LT = MAXT + 3
    with ExitStack() as ctx:
        sb = lambda name, shape, dt=F32: ctx.enter_context(nc.sbuf_tensor(name, shape, dt))
        bias = sb("rt_bias", [P, NG + NE])
        s4 = sb("rt_s4", [P, 8, TILES, 4])
        s16 = sb("rt_s16", [P, 4, TILES, NG, EPG])
        s1 = sb("rt_s1", [P, 12, TILES])
        base = sb("rt_base", [P, TILES + 1, NE])
        tot = sb("rt_tot", [P, TILES, NE])
        ex = sb("rt_experts", [P, 4, NE])
        ti = sb("rt_tiles", [P, LT])
        te = sb("rt_te", [P, 2, LT])
        cmp = sb("rt_cmp", [P, LT, NE])
        iota = sb("rt_iota", [P, LT], I32)
        spare = sb("rt_spare", [MAXT * 2, P], I32)
        rows = sb("rt_rows", [MAXT * 2, P], I32)
        rowsf = sb("rt_rowsf", [MAXT * 2, P])
        tok = sb("rt_tok", [P, 2, TILES], I32)
        ids = sb("rt_ids", [P, 3, MAXT * 2])
        bl, io, chain, ex1, ex2, ea, mr, pp, zs, sr, sct, rl, rf, rp = (m.sem("rt_" + n) for n in (
            "bias_loaded", "iotas", "dve_chain", "exp_group", "exp_expert", "exps", "choices_ready", "psum",
            "table_zeroed", "slots_ready", "scattered", "rows_loaded", "rows_float", "rows_psum"))
        eq, ohg, e1, e2, oh1, oh2, gl, free4 = (s4[:, j] for j in range(8))
        gm, gs, gw, v1, v2, dd, aa, den, w1 = (s1[:, j, :] for j in range(9))
        free = s1[:, 9, :]
        with nc.Block() as block:
            @block.sync
            def _(sp):
                sp.dma_start(bias[:, 0:NG], A.b_route_group.broadcast_to([P, NG])).then_inc(bl, 16)
                sp.dma_start(bias[:, NG:], A.b_route_expert.broadcast_to([P, NE])).then_inc(bl, 16)
                sp.wait_ge(io, 3)
                sp.dma_start(m.tok_dram.rearrange("(a p) o -> a (p o)", p=P), spare[:, :]).then_inc(zs, 16)
                sp.wait_ge(sct, 16 * 2 * TILES)
                sp.dma_start(rows[:, :], m.tok_dram.rearrange("(a p) o -> a (p o)", p=P)).then_inc(rl, 16)

            @block.gpsimd
            def _(pool):
                nc.gpsimd.iota(iota[:, :], [[1, LT]], base=0, channel_multiplier=0).then_inc(io, 1)
                nc.gpsimd.iota(tok[:, :, :], [[NT, 2], [P, TILES]], base=0, channel_multiplier=1).then_inc(io, 1)
                nc.gpsimd.iota(spare[:, :], [[1, P]], base=2 * NT, channel_multiplier=P).then_inc(io, 1)
                pool.wait_ge(io, 3)
                pool.wait_ge(zs, 16)
                pool.wait_ge(sr, 1)
                for t in range(TILES):
                    r = rows_of(t)
                    for c in range(2):
                        nc.gpsimd.indirect_dma_start(
                            out=m.tok_dram, out_offset=bass.IndirectOffsetOnAxis(ap=m.slot[0:r, c, t:t + 1], axis=0),
                            in_=tok[0:r, c, t:t + 1], in_offset=None).then_inc(sct, 16)

            @block.scalar
            def _(act):
                act.wait_ge(ex1, 1)
                nc.scalar.activation(e1, gl, ACT.Exp).then_inc(ea, 1)
                act.wait_ge(ex2, 1)
                nc.scalar.activation(aa, dd, ACT.Exp).then_inc(ea, 1)

            @block.tensor
            def _(pe):
                pe.wait_ge(mr, 1)
                mm = s16[:, 2].rearrange("p t g j -> p (t g j)")
                nc.tensor.matmul(m.ps[:, 0, 0:TILES * NE], m.tri[:, :], mm, start=True, stop=True)
                nc.tensor.matmul(m.ps[:, 1, 0:TILES * NE], m.ones[:, :], mm, start=True, stop=True).then_inc(pp, 1)
                pe.wait_ge(rf, 1)
                nc.tensor.transpose(m.ps[:, 2, 0:MAXT * 2], rowsf[:, :], m.ident[0:MAXT * 2, 0:MAXT * 2]).then_inc(rp, 1)

            @block.vector
            def _(dve):
                v = nc.vector
                step = Chain(dve, chain)
                tt, ts = v.tensor_tensor, v.tensor_scalar

                def first_of_highest(values, highest, oh):
                    step(v.tensor_reduce(highest, values, AX.X, ALU.max))
                    step(tt(oh, values, bc(highest, 2, 4), ALU.is_equal))
                    step(ts(free, oh[:, :, 0], -1.0, 1.0, ALU.mult, ALU.add))
                    for j in range(1, 4):
                        step(tt(oh[:, :, j], oh[:, :, j], free, ALU.mult))
                        step(tt(free, free, oh[:, :, j], ALU.subtract))

                lg = m.logits
                dve.wait_ge(bl, 32)
                step(tt(lg[:, :, :], lg[:, :, :], bc(bias[:, :], 1, TILES), ALU.add))
                groups = lg[:, :, 0:NG]
                first_of_highest(groups, gm, ohg)
                tt(gl, groups, bc(gm, 2, 4), ALU.subtract).then_inc(ex1, 1)
                prod = s16[:, 0]
                step(tt(prod, lg[:, :, NG:].rearrange("p t (g j) -> p t g j", g=NG), bc(ohg, 3, EPG), ALU.mult))
                step(v.tensor_reduce(e2, prod.rearrange("p t g j -> p t j g"), AX.X, ALU.add))
                first_of_highest(e2, v1, oh1)
                step(v.scalar_tensor_tensor(e2, oh1, NEG, e2, ALU.mult, ALU.add))
                first_of_highest(e2, v2, oh2)
                tt(dd, v2, v1, ALU.subtract).then_inc(ex2, 1)
                dve.wait_ge(ea, 2)
                step(v.tensor_reduce(gs, e1, AX.X, ALU.add))
                step(ts(den, aa, 1.0, None, ALU.add))
                step(tt(den, den, gs, ALU.mult))
                step(v.reciprocal(m.wt[:, 0, :], den))
                step(tt(m.wt[:, 1, :], m.wt[:, 0, :], aa, ALU.mult))
                for c, oh in enumerate((oh1, oh2)):
                    step(tt(s16[:, c], bc(ohg, 3, EPG), bc(oh, 2, NG), ALU.mult))
                    step(v.memset(s16[DEC:P, c, PT, :, :], 0.0))
                tt(s16[:, 2], s16[:, 0], s16[:, 1], ALU.add).then_inc(mr, 1)
                dve.wait_ge(pp, 1)
                fl = lambda a: a.rearrange("p t g j -> p (t g j)")
                step(v.tensor_copy(tot[:, :, :].rearrange("p t e -> p (t e)"), m.ps[:, 1, 0:TILES * NE]))
                step(v.memset(base[:, 0, :], 0.0))
                for t in range(TILES):
                    step(tt(base[:, t + 1, :], base[:, t, :], tot[:, t, :], ALU.add))
                count, tiles, done, start = (ex[:, j, :] for j in range(4))
                step(ts(tiles, base[:, TILES, :], 0.0, None, ALU.is_gt))
                for j in range(1, -(-NT // SLOTS)):
                    step(v.scalar_tensor_tensor(tiles, base[:, TILES, :], float(j * SLOTS), tiles, ALU.is_gt, ALU.add))
                step(v.tensor_tensor_scan(done, m.ones[:, 0:NE], tiles, 0.0, ALU.mult, ALU.add))
                step(tt(start, done, tiles, ALU.subtract))
                step(ts(start, start, float(SLOTS), None, ALU.mult))
                step(tt(tot[:, :, :], base[:, 0:TILES, :], bc(start, 1, TILES), ALU.add))
                step(tt(tot[:, :, :].rearrange("p t e -> p (t e)"), tot[:, :, :].rearrange("p t e -> p (t e)"),
                        m.ps[:, 0, 0:TILES * NE], ALU.add))
                for c in range(2):
                    step(tt(s16[:, c].rearrange("p t g j -> p t (g j)"), s16[:, c].rearrange("p t g j -> p t (g j)"),
                            tot[:, :, :], ALU.mult))
                    step(v.tensor_reduce(s1[:, 10 + c, :], s16[:, c].rearrange("p t g j -> p t (g j)"), AX.X, ALU.add))
                v.tensor_copy(m.slot[:, :, :], s1[:, 10:12, :]).then_inc(sr, 1)
                dve.wait_ge(io, 3)
                step(v.tensor_copy(ti[:, :], iota[:, :]))
                step(tt(cmp[:, :, :], bc(ti[:, :], 2, NE), bc(done, 1, LT), ALU.is_ge))
                step(v.tensor_reduce(te[:, 0, :], cmp[:, :, :], AX.X, ALU.add))
                step(ts(m.tile_expert[:, :], te[:, 0, :], float(NE - 1), None, ALU.min))
                step(ts(te[:, 1, 0:1], done[:, NE - 1:NE], 0.5, -0.25, ALU.mult, ALU.add))
                step(ts(te[:, 1, 0:1], te[:, 1, 0:1], ROUND, None, ALU.add))
                step(ts(te[:, 1, 0:1], te[:, 1, 0:1], -ROUND, None, ALU.add))
                step(tt(te[:, 1, 1:2], te[:, 1, 0:1], te[:, 1, 0:1], ALU.add))
                step(tt(te[:, 1, 1:2], te[:, 1, 1:2], done[:, NE - 1:NE], ALU.is_lt))
                step(tt(te[:, 1, 0:1], te[:, 1, 0:1], te[:, 1, 1:2], ALU.add))
                step(v.tensor_copy(m.pairs[:, 0:1], te[:, 1, 0:1]))
                step(ts(m.pairs[:, 1:2], te[:, 1, 0:1], -1.0, None, ALU.add))
                dve.wait_ge(rl, 16)
                v.tensor_copy(rowsf[:, :], rows[:, :]).then_inc(rf, 1)
                dve.wait_ge(rp, 1)
                step(v.tensor_copy(ids[:, 0, :], m.ps[:, 2, 0:MAXT * 2]))
                step(v.tensor_copy(m.slot_row[:, 0:MAXT * 2], ids[:, 0, :]))
                step(ts(ids[:, 1, :], ids[:, 0, :], NT - 0.5, -float(NT), ALU.is_ge, ALU.mult))
                step(tt(ids[:, 1, :], ids[:, 1, :], ids[:, 0, :], ALU.add))
                step(ts(ids[:, 2, :], ids[:, 1, :], NT - 0.5, None, ALU.is_lt))
                step(v.memset(m.slot_token[:, :], 0))
                step(tt(m.slot_token[:, 0:MAXT * 2], ids[:, 1, :], ids[:, 2, :], ALU.mult))


def experts(nc, m, A):
    PAIRS = (-(-2 * NT // SLOTS) + 1) // 2, MAXT // 2
    with ExitStack() as ctx:
        sb = lambda name, shape, dt=F32: ctx.enter_context(nc.sbuf_tensor(name, shape, dt))
        wg = sb("ex_wg", [P, 2, KD, FD])
        wu = sb("ex_wu", [P, 2, KD, FD])
        wd = sb("ex_wd", [P, 2, 2, D])
        idx = sb("ex_idx", [P, 2, 2], I32)
        row = sb("ex_row", [P, 2, 2], I32)
        xg = sb("ex_x", [P, 2, 2, D])
        xT = sb("ex_xT", [P, 2, KD, SLOTS])
        sl = sb("ex_silu", [P, 2, SLOTS])
        hid = sb("ex_hid", [P, 2, 2, SLOTS])
        yo = sb("ex_y", [P, 2, 2, D])
        gul, wdl, gl, ys = ([m.sem(f"ex_{n}{i}") for i in range(2)] for n in (
            "gate_up_loaded", "down_loaded", "x_gathered", "y_stored"))
        ic, rc, tp, xed, xea, gp, slr, hr, dn, yea, yed = (m.sem("ex_" + n) for n in (
            "index_copied", "row_copied", "x_transposed", "xT_by_dve", "xT_by_act", "gate_up_psum", "silu_ready", "hid_ready",
            "down_psum", "y_by_act", "y_by_dve"))

        idle = sb("ex_idle", [1, 7])
        begun, idle_set = m.sem("ex_begun"), m.sem("ex_idle_set")

        def wait(engine, sem, value):
            if not (isinstance(value, int) and value <= 0):
                engine.wait_ge(sem, value)

        def wait_alone(place, sem, value):
            nc.gpsimd.wait_ge(sem, value)
            nc.gpsimd.tensor_tensor(idle[:, place:place + 1], idle[:, 0:1], idle[:, 0:1], ALU.add)

        def run(engine, body, before=None, after=None):
            pairs = engine.value_load(m.pairs[0:1, 0:1], min_val=PAIRS[0], max_val=PAIRS[1])
            if before:
                before()
            body(0)
            body(1)
            with engine.Fori(2, pairs) as i:
                body(i)
            if after:
                after(engine.value_load(m.pairs[0:1, 1:2], min_val=PAIRS[0] - 1, max_val=PAIRS[1] - 1))

        def last_tile(step, i, b):
            if b:
                step(i, 0)
            elif not (isinstance(i, int) and i == 0):
                step(i - 1, 1)

        with nc.Block() as block:
            @block.sync
            def _(sp):
                def load(parts, sem, i, b, used=None, count=0):
                    e = sp.value_load(m.tile_expert[0:1, bass.ds(2 * i + b, 1)], min_val=0, max_val=NE - 1)
                    wait(sp, used, count)
                    for dst, src in parts:
                        sp.dma_start(dst[:, b, :, :], src[bass.ds(e, 1), :, :].rearrange("o (k p) n -> p (o k) n", p=P)) \
                            .then_inc(sem[b], 16)

                gate_up, down = ((wg, A.w_gate), (wu, A.w_up)), ((wd, A.w_down),)

                def body(i):
                    for b in range(2):
                        n = 2 * i + b
                        load(gate_up, gul, i + 1, b, gp, 2 * n + 2)
                        load(down, wdl, i + b, 1 - b, dn, 4 * n)

                run(sp, body, lambda: (load(gate_up, gul, 0, 0), load(gate_up, gul, 0, 1), load(down, wdl, 0, 0)))

            @block.gpsimd
            def _(pool):
                def gather(i, b):
                    n = 2 * i + b
                    wait(pool, tp, 4 * n - 4)
                    nc.gpsimd.tensor_copy(idx[:, b, :], m.slot_token[:, bass.ds(2 * n, 2)]).then_inc(ic, 1)
                    wait_alone(1 + b, ic, n + 1)
                    for a in range(2):
                        nc.gpsimd.indirect_dma_start(
                            out=xg[:, b, a, :], out_offset=None, in_=m.h2_dram,
                            in_offset=bass.IndirectOffsetOnAxis(ap=idx[:, b, a:a + 1], axis=0)).then_inc(gl[b], 16)

                def scatter(i, b):
                    n = 2 * i + b
                    wait(pool, ys[b], 32 * i)
                    nc.gpsimd.tensor_copy(row[:, b, :], m.slot_row[:, bass.ds(2 * n, 2)]).then_inc(rc, 1)
                    pool.wait_ge(rc, n + 1)
                    for a, ready in enumerate((yea, yed)):
                        wait_alone(3 + 2 * b + a, ready, 2 * n + 2)
                        nc.gpsimd.indirect_dma_start(
                            out=m.y_dram, out_offset=bass.IndirectOffsetOnAxis(ap=row[:, b, a:a + 1], axis=0),
                            in_=yo[:, b, a, :], in_offset=None).then_inc(ys[b], 16)

                def body(i):
                    for b in range(2):
                        gather(i + 1, b)
                        last_tile(scatter, i, b)

                def after(last):
                    scatter(last, 1)
                    for b in range(2):
                        pool.wait_ge(ys[b], 32 * last + 32)
                        pool.wait_ge(gl[b], 32 * last + 64)
                        pool.wait_ge(gul[b], 32 * last + 64)
                    pool.wait_ge(wdl[0], 16 * last + 32)

                nc.gpsimd.memset(idle[:, 0:1], 0.0).then_inc(idle_set, 1)
                pool.wait_ge(idle_set, 1)
                run(pool, body, lambda: (gather(0, 0), gather(0, 1)), after)

            @block.tensor
            def _(pe):
                def transposes(i, b, f):
                    n = 2 * i + b
                    if f == 0:
                        pe.wait_ge(gl[b], 32 * i + 32)
                    for q in (2 * f, 2 * f + 1):
                        wait(pe, (xed, xea)[q % 2], 2 * n + q // 2)
                        for k in range(2):
                            for a in range(2):
                                j = nc.tensor.transpose(m.ps[:, q % 2, SLOTS * k + P * a:SLOTS * k + P * (a + 1)],
                                                        xg[:, b, a, P * (2 * q + k):P * (2 * q + k + 1)], m.ident[:, :])
                        j.then_inc(tp, 1)

                def gate_up(i, b, f):
                    n = 2 * i + b
                    if f == 0:
                        pe.wait_ge(gul[b], 32 * i + 32)
                        pe.wait_ge(xed, 2 * n + 2)
                        pe.wait_ge(xea, 2 * n + 2)
                    wait(pe, hr, 2 * n - 1 + f)
                    for x, w in enumerate((wg, wu)):
                        for k in range(KD):
                            j = nc.tensor.matmul(m.ps[:, 2 + f, SLOTS * x:SLOTS * (x + 1)],
                                                 w[:, b, k, P * f:P * (f + 1)], xT[:, b, k, :],
                                                 start=k == 0, stop=k == KD - 1)
                    j.then_inc(gp, 1)

                def down(i, b):
                    n = 2 * i + b
                    pe.wait_ge(wdl[b], 16 * i + 16)
                    pe.wait_ge(hr, 2 * n + 2)
                    for a in range(2):
                        wait(pe, (yea, yed)[a], 2 * n)
                        for c in range(2):
                            for f in range(2):
                                j = nc.tensor.matmul(m.ps[:, 4 + 2 * a + c, :], hid[:, b, f, P * a:P * (a + 1)],
                                                     wd[:, b, f, 512 * c:512 * (c + 1)], start=f == 0, stop=f == 1)
                            j.then_inc(dn, 1)

                def body(i):
                    for b in range(2):
                        gate_up(i, b, 0)
                        transposes(i + b, 1 - b, 0)
                        last_tile(down, i, b)
                        gate_up(i, b, 1)
                        transposes(i + b, 1 - b, 1)

                run(pe, body, lambda: (transposes(0, 0, 0), transposes(0, 0, 1)), lambda last: down(last, 1))

            @block.scalar
            def _(act):
                def xts(i, b, f):
                    act.wait_ge(tp, 4 * (2 * i + b) + 2 * f + 2)
                    nc.scalar.copy(xT[:, b, 4 * f + 2:4 * f + 4, :].rearrange("p k n -> p (k n)"), m.ps[:, 1, :]).then_inc(xea, 1)

                def silu(i, b, f):
                    n = 2 * i + b
                    act.wait_ge(gp, 2 * n + f + 1)
                    wait(act, hr, 2 * n - 1 + f)
                    nc.scalar.activation(sl[:, f, :], m.ps[:, 2 + f, 0:SLOTS], ACT.Silu).then_inc(slr, 1)

                def rows(i, b):
                    n = 2 * i + b
                    wait(act, ys[b], 32 * i)
                    for c in range(2):
                        act.wait_ge(dn, 4 * n + c + 1)
                        nc.scalar.copy(yo[:, b, 0, 512 * c:512 * (c + 1)], m.ps[:, 4 + c, :]).then_inc(yea, 1)

                def body(i):
                    for b in range(2):
                        silu(i, b, 0)
                        xts(i + b, 1 - b, 0)
                        last_tile(rows, i, b)
                        silu(i, b, 1)
                        xts(i + b, 1 - b, 1)

                act.wait_ge(begun, 1)
                run(act, body, lambda: (xts(0, 0, 0), xts(0, 0, 1)), lambda last: rows(last, 1))

            @block.vector
            def _(dve):
                v = nc.vector

                def xts(i, b, f):
                    dve.wait_ge(tp, 4 * (2 * i + b) + 2 * f + 1)
                    v.tensor_copy(xT[:, b, 4 * f:4 * f + 2, :].rearrange("p k n -> p (k n)"), m.ps[:, 0, :]).then_inc(xed, 1)

                def hidden(i, b, f):
                    dve.wait_ge(slr, 2 * (2 * i + b) + f + 1)
                    v.tensor_tensor(hid[:, b, f, :], sl[:, f, :], m.ps[:, 2 + f, SLOTS:2 * SLOTS], ALU.mult).then_inc(hr, 1)

                def rows(i, b):
                    n = 2 * i + b
                    wait(dve, ys[b], 32 * i)
                    for c in range(2):
                        dve.wait_ge(dn, 4 * n + c + 3)
                        v.tensor_copy(yo[:, b, 1, 512 * c:512 * (c + 1)], m.ps[:, 6 + c, :]).then_inc(yed, 1)

                def body(i):
                    for b in range(2):
                        xts(i + b, 1 - b, 0)
                        hidden(i, b, 0)
                        last_tile(rows, i, b)
                        xts(i + b, 1 - b, 1)
                        hidden(i, b, 1)

                v.memset(sl[:, :, :], 0.0).then_inc(begun, 1)
                dve.wait_ge(begun, 1)
                run(dve, body, lambda: (xts(0, 0, 0), xts(0, 0, 1)), lambda last: rows(last, 1))


def combine(nc, m, A, O):
    with ExitStack() as ctx:
        sb = lambda name, shape: ctx.enter_context(nc.sbuf_tensor(name, shape, F32))
        NB = 2
        y = sb("cb_y", [P, NB, 2, D])
        x1 = sb("cb_x1", [P, NB, D])
        o = sb("cb_o", [P, NB, D])
        yl, xl, os_ = ([m.sem(f"cb_{n}{i}") for i in range(NB)] for n in ("y_loaded", "x1_loaded", "stored"))
        chain, orr = m.sem("cb_dve_chain"), m.sem("cb_out_ready")
        with nc.Block() as block:
            @block.vector
            def _(dve):
                step = Chain(dve, chain)
                v = nc.vector
                for t in range(TILES):
                    r, b = rows_of(t), t % NB
                    dve.wait_ge(yl[b], 32 * (t // NB + 1))
                    y1, y2, dst = y[0:r, b, 0, :], y[0:r, b, 1, :], o[0:r, b, :]
                    step(v.tensor_scalar(y1, y1, m.wt[0:r, 0, t:t + 1], None, ALU.mult))
                    step(v.scalar_tensor_tensor(y1, y2, m.wt[0:r, 1, t:t + 1], y1, ALU.mult, ALU.add))
                    step(v.tensor_tensor(y1, y1, m.gate2[0:r, 0, int(t == PT), :], ALU.mult))
                    dve.wait_ge(xl[b], 16 * (t // NB + 1))
                    if t >= NB:
                        dve.wait_ge(os_[b], 16 * (t // NB))
                    v.tensor_tensor(dst, y1, x1[0:r, b, :], ALU.add).then_inc(orr, 1)

            @block.sync
            def _(sp):
                for t in range(TILES + 1):
                    if t < TILES:
                        r, b = rows_of(t), t % NB
                        if t >= NB:
                            sp.wait_ge(orr, t - NB + 1)
                        for c in range(2):
                            sp.dma_start(y[0:r, b, c, :], m.y_dram[c * NT + t * P:c * NT + t * P + r, :]).then_inc(yl[b], 16)
                        sp.dma_start(x1[0:r, b, :], m.x1_dram[t * P:t * P + r, :]).then_inc(xl[b], 16)
                    if t:
                        u = t - 1
                        sp.wait_ge(orr, u + 1)
                        dst = O.y_prompt[0, u * P:(u + 1) * P, :] if u < PT else O.y_sample[0, :, :]
                        sp.dma_start(dst, o[0:rows_of(u), u % NB, :]).then_inc(os_[u % NB], 16)
                for i in range(NB):
                    sp.wait_ge(os_[i], 16 * ((TILES - i + NB - 1) // NB))


def fresh_semaphores(nc, m):
    nc.clear_and_free_semaphores(m.sems)
    nc.all_engine_barrier()
    m.sems = []


def new_semaphore(nc, m, name):
    m.sems.append(nc.alloc_semaphore(name))
    return m.sems[-1]


def program(nc, A, O):
    ctx = ExitStack()
    m = Mem()
    m.sems = []
    m.sem = lambda name: new_semaphore(nc, m, name)
    with ctx:
        def sb(name, shape, dt=F32):
            return ctx.enter_context(nc.sbuf_tensor(name, shape, dt))
        m.ps = ctx.enter_context(nc.psum_tensor("ps", [P, 8, 512], F32))
        m.ident = sb("ident", [P, P])
        m.ones = sb("ones", [P, P])
        m.tri = sb("tri", [P, P])
        m.cT = sb("cT", [P, KD, 2])
        m.mod_dram = nc.dram_tensor("mod", [2, 6 * D], F32, kind="Internal").ap()
        m.hT = sb("hT", [P, KD, NT])
        constants(nc, m, A)
        m.pj_loaded = m.sem("pj_weights_loaded")
        m.q_dram = nc.dram_tensor("q_dram", [P, 4, NT], F32, kind="Internal").ap()
        m.qiT = sb("qiT", [P, 2, NT])
        m.kT = sb("kT", [P, NT])
        m.kiT = sb("kiT", [P, NT])
        m.v = sb("v", [P, PT, HD])
        m.vs = sb("vs", [P, CB + 1, HD])
        m.wi = sb("wi", [P, TILES, IH])
        m.tokqi = sb("tokqi", [P, 2, IH * ID])
        m.zT = sb("zT", [P, 4, NT])
        m.x1_dram = nc.dram_tensor("x1_dram", [NT, D], F32, kind="Internal").ap()
        m.h2_dram = nc.dram_tensor("h2_dram", [NT, D], F32, kind="Internal").ap()
        m.y_dram = nc.dram_tensor("y_dram", [2 * NT + MAXT * SLOTS, D], F32, kind="Internal").ap()
        m.tok_dram = nc.dram_tensor("tok_dram", [MAXT * SLOTS, 1], I32, kind="Internal").ap()
        m.gb_dram = nc.dram_tensor("gate_b_dram", [P, KD, NT], F32, kind="Internal").ap()
        m.left_dram = nc.dram_tensor("merge_left_dram", [P, KD, NT], F32, kind="Internal").ap()
        m.z_dram = nc.dram_tensor("z_dram", [DEC, 512], F32, kind="Internal").ap()
        m.us_dram = nc.dram_tensor("us_dram", [DEC, 512], F32, kind="Internal").ap()
        with nc.sbuf_tensor("u", [P, G, T, J], F32) as m.u, nc.sbuf_tensor("us", [DEC, 512], F32) as m.us:
            with nc.sbuf_tensor("qT", [P, 4, NT], F32) as m.qT, nc.sbuf_tensor("pj_w", [P, KD, 1024 + RW], F32) as m.pj_w:
                adaln_and_norm(nc, m, A)
                project(nc, m, A, O)
            with ExitStack() as ssm:
                ssb = lambda name, shape: ssm.enter_context(nc.sbuf_tensor(name, shape, F32))
                m.M = ssb("M", [P, G, P])
                m.V = ssb("V", [P, 2, PAIR, T + 1, J])
                m.W = ssb("W", [P, 2, PAIR, P])
                m.rot = ssb("rot", [P, 2, PAIR, COLS])
                m.decay = ssb("decay", [P, PAIR, COLS])
                m.r8 = ssb("r8", [P, PAIR])
                m.h0 = ssb("h0", [P, 2, PAIR])
                ssm_parameters(nc, m, A)
                ssm_scan(nc, m, A, O)
        fresh_semaphores(nc, m)
        m.attnT = sb("attnT", [P, 4, NT])
        with ExitStack() as at:
            asb = lambda name, shape, dt=F32: at.enter_context(nc.sbuf_tensor(name, shape, dt))
            m.mask = asb("mask", [P, MK_W], BF16)
            m.kTs = asb("kTs", [P, PAST + DEC])
            with nc.sbuf_tensor("sc", [P, SC_W], F32) as m.sc:
                with nc.sbuf_tensor("kiTs", [P, PAST + DEC], F32) as m.kiTs:
                    cache_keys(nc, m, A)
                    index_scores(nc, m)
                select_keys_and_gates(nc, m, A)
            flat = lambda a: a[:, :, :].rearrange("p k n -> p (k n)")
            m.wout = flat(m.hT)[:, 0:KD * D].rearrange("p (k n) -> p k n", k=KD)
            m.modA = flat(m.zT)[:, 0:4 * D].rearrange("p (a s n) -> p a s n", a=2, s=2)
            attention(nc, m, A)
        fresh_semaphores(nc, m)
        m.logits = sb("logits", [P, TILES, NG + NE])
        m.gate2 = flat(m.attnT)[:, 0:2 * D].rearrange("p (a s n) -> p a s n", a=1, s=2)
        with nc.sbuf_tensor("mergedT", [P, KD, NT], F32) as m.mergedT, nc.sbuf_tensor("shift2", [P, 1, 2, D], F32) as m.shift2:
            merge(nc, m, A)
            output_projection(nc, m, A)
        m.wt = sb("choice_weight", [P, 2, TILES])
        m.slot = sb("slot", [P, 2, TILES], I32)
        m.slot_row = sb("slot_row", [P, MAXT * 2], I32)
        m.slot_token = sb("slot_token", [P, MAXT * 2 + 4], I32)
        m.tile_expert = sb("tile_expert", [P, MAXT + 3], I32)
        m.pairs = sb("pairs", [P, 2], I32)
        routing(nc, m, A)
        experts(nc, m, A)
        combine(nc, m, A, O)


_INS = ['x_prompt', 'x_sample', 'cache_k', 'cache_v', 'cache_kidx', 'state_ssm_re', 'state_ssm_im',
        'c_prompt', 'c_sample', 'w_ada', 'b_ada', 'w_in', 'ssm_a_re', 'ssm_a_im', 'ssm_log_dt',
        'ssm_b_re', 'ssm_b_im', 'ssm_c_re', 'ssm_c_im', 'ssm_d', 'w_glu', 'q_gain', 'k_gain', 'kidx_gain',
        'w_attn_out', 'w_out', 'w_route_group', 'b_route_group', 'w_route_expert', 'b_route_expert',
        'w_gate', 'w_up', 'w_down']
_LAYERED = {n for n in _INS if n.startswith(('w_', 'cache', 'state', 'ssm'))}
_OUTS = [('y_prompt', (1, SEQ, D)), ('y_sample', (1, DEC, D)),
         ('k_prompt', (1, 1, SEQ, HD)), ('v_prompt', (1, 1, SEQ, HD)), ('kidx_prompt', (1, 1, SEQ, ID)),
         ('ssm_re_prompt', (1, 1, G, ST)), ('ssm_im_prompt', (1, 1, G, ST)),
         ('k_sample', (1, 1, DEC, HD)), ('v_sample', (1, 1, DEC, HD)), ('kidx_sample', (1, 1, DEC, ID)),
         ('ssm_re_sample', (1, 1, G, ST)), ('ssm_im_sample', (1, 1, G, ST))]


class Args:
    pass


def kernel(**inputs):
    import numpy as _np
    import concourse.bacc as _bacc
    from concourse.bass_utils import run_bass_kernel_spmd as _run

    nc = _bacc.Bacc("TRN2", target_bir_lowering=False, num_devices=1)
    arrays, ins, outs = {}, Args(), Args()
    for name in _INS:
        a = _np.ascontiguousarray(inputs[name])
        arrays[f"in_{name}"] = a
        ap = nc.dram_tensor(f"in_{name}", a.shape, F32, kind="ExternalInput").ap()
        vars(ins)[name] = ap[0] if name in _LAYERED else ap
    for name, shape in _OUTS:
        vars(outs)[name] = nc.dram_tensor(f"out_{name}", shape, F32, kind="ExternalOutput").ap()
    program(nc, ins, outs)
    r = _run(nc, [arrays], core_ids=[0])
    return tuple(r.results[0][f"out_{name}"] for name, _ in _OUTS)
```
